# Optimizing a Trainium2 kernel written in Bass

```python
import jax, jax.numpy as jnp
from jax import lax

D_MODEL = 1024
BATCH = 1
SEQ = 1024
DEPTH = 1

CHUNK = 64
SB_HEADS = 8
SB_HEAD_DIM = 64
SB_WIDTH = SB_HEADS * SB_HEAD_DIM
HG_HEADS = 4
HG_HEAD_DIM = 128
HG_WIDTH = HG_HEADS * HG_HEAD_DIM
MIX_WIDTH = SB_WIDTH + HG_WIDTH
IN_PROJ_WIDTH = 3 * SB_WIDTH + 4 * HG_WIDTH
Q_BLOCK = 128
RECUR_BLOCK = CHUNK // 2
N_EXPERTS = 32
TOP_K = 4
D_EXPERT = D_MODEL
SWIGLU_LIMIT = 7.0
SWIGLU_ALPHA = 1.702
EXPERT_BLOCK = 128
EPS = 1e-6

kernel_name = "hybrid_stickbreak_hgrn2_moe"

def rms_norm(x, g):
    xf = x.astype(jnp.float32)
    y = xf * lax.rsqrt(jnp.mean(xf * xf, axis=-1, keepdims=True) + EPS)
    return (y * g.astype(jnp.float32)).astype(x.dtype)

def stick_breaking_attention(q, k, v):
    seq = q.shape[2]
    scale = SB_HEAD_DIM ** -0.5
    outs = []
    for blk in range(seq // Q_BLOCK):
        lo, hi = blk * Q_BLOCK, (blk + 1) * Q_BLOCK
        z = jnp.einsum("bhqd,bhkd->bhqk", q[:, :, lo:hi], k[:, :, :hi]).astype(jnp.float32) * scale
        t_idx = lo + jnp.arange(Q_BLOCK)[:, None]
        s_idx = jnp.arange(hi)[None, :]
        strict = s_idx < t_idx
        log_1mb = jnp.where(strict, jax.nn.log_sigmoid(-z), 0.0)
        after = lax.cumsum(log_1mb, axis=3, reverse=True) - log_1mb
        w = jnp.where(strict, jnp.exp(jax.nn.log_sigmoid(z) + after), 0.0)
        outs.append(jnp.einsum("bhqk,bhkd->bhqd", w.astype(v.dtype), v[:, :, :hi]))
    return jnp.concatenate(outs, axis=2)

def hgrn2_recurrence(q, f_pre, i, lb):
    bsz, seq, nh, dk = q.shape
    nb = seq // RECUR_BLOCK
    qf = q.astype(jnp.float32)
    ff = f_pre.astype(jnp.float32)
    vf = i.astype(jnp.float32)
    lbf = lb.astype(jnp.float32)
    log_f = jnp.log(lbf + (1.0 - lbf) * jax.nn.sigmoid(ff))
    kf = (1.0 - lbf) * jax.nn.sigmoid(-ff)

    def to_blocks(a):
        return a.reshape(bsz, nb, RECUR_BLOCK, nh, a.shape[-1]).transpose(1, 0, 3, 2, 4)

    causal = jnp.tril(jnp.ones((RECUR_BLOCK, RECUR_BLOCK), jnp.float32))

    def step(state, inp):
        qc, kc, vc, gc = inp
        b = jnp.cumsum(gc, axis=2)
        q_e = qc * jnp.exp(b)
        k_e = kc * jnp.exp(-b)
        attn = jnp.einsum("bhtd,bhsd->bhts", q_e, k_e) * causal
        o = jnp.einsum("bhts,bhse->bhte", attn, vc) + jnp.einsum("bhtd,bhde->bhte", q_e, state)
        b_last = b[:, :, -1:, :]
        state = jnp.exp(b_last[:, :, 0, :])[..., None] * state + jnp.einsum(
            "bhsd,bhse->bhde", kc * jnp.exp(b_last - b), vc)
        return state, o

    s0 = jnp.zeros((bsz, nh, dk, vf.shape[-1]), jnp.float32)
    _, o = lax.scan(step, s0, (to_blocks(qf), to_blocks(kf), to_blocks(vf), to_blocks(log_f)))
    o = o.transpose(1, 0, 3, 2, 4).reshape(bsz, seq, nh, vf.shape[-1])
    return o.astype(q.dtype)

def moe_ffn(h, w_router, b_router, w_gate_up, b_gate_up, w_down, b_down):
    n_tok, d = h.shape
    logits = (h @ w_router + b_router).astype(jnp.float32)
    top_val, top_idx = lax.top_k(logits, TOP_K)
    gate = jax.nn.softmax(top_val, axis=-1)
    n_assign = n_tok * TOP_K
    flat_e = top_idx.reshape(-1).astype(jnp.int32)
    flat_tok = jnp.arange(n_assign, dtype=jnp.int32) // TOP_K
    flat_g = gate.reshape(-1)
    order = jnp.argsort(flat_e)
    e_sorted = flat_e[order]
    counts = jnp.zeros((N_EXPERTS,), jnp.int32).at[flat_e].add(1)
    starts = jnp.cumsum(counts) - counts
    padded = (counts + EXPERT_BLOCK - 1) // EXPERT_BLOCK * EXPERT_BLOCK
    pad_ends = jnp.cumsum(padded)
    pad_starts = pad_ends - padded
    dest = pad_starts[e_sorted] + (jnp.arange(n_assign, dtype=jnp.int32) - starts[e_sorted])
    n_blocks = (n_assign + EXPERT_BLOCK - 1) // EXPERT_BLOCK + N_EXPERTS
    n_rows = n_blocks * EXPERT_BLOCK
    row_tok = jnp.full((n_rows,), n_tok, jnp.int32).at[dest].set(flat_tok[order])
    row_g = jnp.zeros((n_rows,), jnp.float32).at[dest].set(flat_g[order])
    block_start = jnp.arange(n_blocks, dtype=jnp.int32) * EXPERT_BLOCK
    block_e = jnp.minimum(jnp.searchsorted(pad_ends, block_start, side="right"), N_EXPERTS - 1)
    h_pad = jnp.concatenate([h, jnp.zeros((1, d), h.dtype)], axis=0)
    xb = h_pad[row_tok].reshape(n_blocks, EXPERT_BLOCK, d)

    def expert_block(args):
        xblk, e = args
        gu = xblk @ w_gate_up[e] + b_gate_up[e]
        g_lin = jnp.minimum(gu[:, :D_EXPERT], SWIGLU_LIMIT)
        u_lin = jnp.clip(gu[:, D_EXPERT:], -SWIGLU_LIMIT, SWIGLU_LIMIT)
        act = g_lin * jax.nn.sigmoid(SWIGLU_ALPHA * g_lin) * (u_lin + 1.0)
        return act @ w_down[e] + b_down[e]

    yb = lax.map(expert_block, (xb, block_e)).reshape(n_rows, d)
    y = jnp.zeros((n_tok + 1, d), h.dtype).at[row_tok].add(yb * row_g[:, None].astype(h.dtype))
    return y[:n_tok]

def setup_inputs(seed: int = 0) -> dict:
    key = jax.random.key(seed)
    ks = jax.random.split(key, 16)
    nrm = jax.random.normal
    f32 = jnp.float32
    return {
        "x": nrm(ks[0], (BATCH, SEQ, D_MODEL), f32),
        "norm1_g": 1.0 + 0.02 * nrm(ks[1], (DEPTH, D_MODEL), f32),
        "w_in": nrm(ks[2], (DEPTH, D_MODEL, IN_PROJ_WIDTH), f32) * D_MODEL ** -0.5,
        "sb_q_norm_g": 1.0 + 0.02 * nrm(ks[3], (DEPTH, SB_HEAD_DIM), f32),
        "sb_k_norm_g": 1.0 + 0.02 * nrm(ks[4], (DEPTH, SB_HEAD_DIM), f32),
        "sb_out_norm_g": 1.0 + 0.02 * nrm(ks[5], (DEPTH, SB_WIDTH), f32),
        "hg_lb_logits": 0.1 * nrm(ks[6], (DEPTH + 1, HG_WIDTH), f32),
        "hg_out_norm_g": 1.0 + 0.02 * nrm(ks[7], (DEPTH, HG_WIDTH), f32),
        "w_out": nrm(ks[8], (DEPTH, MIX_WIDTH, D_MODEL), f32) * MIX_WIDTH ** -0.5,
        "norm2_g": 1.0 + 0.02 * nrm(ks[9], (DEPTH, D_MODEL), f32),
        "w_router": nrm(ks[10], (DEPTH, D_MODEL, N_EXPERTS), f32) * D_MODEL ** -0.5,
        "b_router": 0.01 * nrm(ks[11], (DEPTH, N_EXPERTS), f32),
        "w_gate_up": nrm(ks[12], (DEPTH, N_EXPERTS, D_MODEL, 2 * D_EXPERT), f32) * D_MODEL ** -0.5,
        "b_gate_up": 0.02 * nrm(ks[13], (DEPTH, N_EXPERTS, 2 * D_EXPERT), f32),
        "w_down": nrm(ks[14], (DEPTH, N_EXPERTS, D_EXPERT, D_MODEL), f32) * D_EXPERT ** -0.5,
        "b_down": 0.02 * nrm(ks[15], (DEPTH, N_EXPERTS, D_MODEL), f32),
    }

def reference(x, norm1_g, w_in, sb_q_norm_g, sb_k_norm_g, sb_out_norm_g, hg_lb_logits,
              hg_out_norm_g, w_out, norm2_g, w_router, b_router, w_gate_up, b_gate_up,
              w_down, b_down):
    bsz, seq, d = x.shape
    lb_all = jnp.cumsum(jax.nn.softmax(hg_lb_logits.astype(jnp.float32), axis=0), axis=0)
    for l in range(DEPTH):
        h = rms_norm(x, norm1_g[l])
        p = h @ w_in[l]
        sb_q, sb_k, sb_v, hg_q, hg_f, hg_i, hg_g = jnp.split(
            p, [SB_WIDTH, 2 * SB_WIDTH, 3 * SB_WIDTH, 3 * SB_WIDTH + HG_WIDTH,
                3 * SB_WIDTH + 2 * HG_WIDTH, 3 * SB_WIDTH + 3 * HG_WIDTH], axis=-1)
        heads = lambda a: a.reshape(bsz, seq, SB_HEADS, SB_HEAD_DIM).transpose(0, 2, 1, 3)
        q = rms_norm(heads(sb_q), sb_q_norm_g[l])
        k = rms_norm(heads(sb_k), sb_k_norm_g[l])
        a = stick_breaking_attention(q, k, heads(sb_v)).transpose(0, 2, 1, 3)
        a = rms_norm(a, sb_out_norm_g[l].reshape(SB_HEADS, SB_HEAD_DIM)).reshape(bsz, seq, SB_WIDTH)
        hh = lambda t: t.reshape(bsz, seq, HG_HEADS, HG_HEAD_DIM)
        lb = lb_all[l].reshape(HG_HEADS, HG_HEAD_DIM)
        r = hgrn2_recurrence(hh(hg_q), hh(hg_f), hh(hg_i), lb)
        r = rms_norm(r, hg_out_norm_g[l].reshape(HG_HEADS, HG_HEAD_DIM)).reshape(bsz, seq, HG_WIDTH)
        r = r * jax.nn.silu(hg_g)
        x = x + jnp.concatenate([a, r], axis=-1) @ w_out[l]
        h2 = rms_norm(x, norm2_g[l]).reshape(bsz * seq, d)
        x = x + moe_ffn(h2, w_router[l], b_router[l], w_gate_up[l], b_gate_up[l],
                        w_down[l], b_down[l]).reshape(bsz, seq, d)
    return x


_drawn_inputs = setup_inputs


def setup_inputs(seed=0):
    import zlib

    import numpy as np

    out = dict(_drawn_inputs(seed))
    spreads = {}
    factors = {'sb_q_norm_g': 2.892,
     'sb_k_norm_g': 3.119,
     'hg_out_norm_g': 3.172,
     'b_gate_up': 6.252,
     'b_down': 7.245}
    for name, (base, spread) in spreads.items():
        noise = np.random.default_rng([zlib.crc32(name.encode()), seed]).standard_normal(out[name].shape)
        drawn = base * np.exp(spread * noise) if base else spread * noise
        out[name] = __import__('jax').numpy.asarray(drawn.astype(out[name].dtype))
    for name, factor in factors.items():
        out[name] = (out[name] * factor).astype(out[name].dtype)
    return out
```

```python
from contextlib import ExitStack

import concourse.bass as bass
from concourse import mybir

F32 = mybir.dt.float32
BF16 = mybir.dt.bfloat16
FP16 = mybir.dt.float16
I32 = mybir.dt.int32
ALU = mybir.AluOpType
ACT = mybir.ActivationFunctionType
AX_X = mybir.AxisListType.X
ds = bass.ds

P = 128


def build_trunk(nc, x, norm1_g, w_in, sb_q_norm_g, sb_k_norm_g, sb_out_norm_g, hg_lb_logits,
                hg_out_norm_g, w_out, norm2_g, w_router, b_router, w_gate_up, b_gate_up,
                w_down, b_down, out, dbg=None):
    T, D = x.shape[1], x.shape[2]
    KT = D // P
    NT = T // P
    SBW = sb_out_norm_g.shape[1]
    HGW = hg_out_norm_g.shape[1]
    DH = sb_q_norm_g.shape[1]
    HT = SBW // P
    NH = HGW // P
    RB = 32
    NB = P // RB
    EPS = 1e-6
    WC = 256
    with ExitStack() as ctx:
        def sb(name, shape, dt):
            return ctx.enter_context(nc.sbuf_tensor(name, shape, dt))

        def ps(name, shape, dt):
            return ctx.enter_context(nc.psum_tensor(name, shape, dt))

        def sem(name):
            return ctx.enter_context(nc.semaphore(name))

        region_a = sb("region_a", [P, 2 * KT * T // 2], F32)
        region_b = sb("region_b", [P, 16 * T], F32)
        region_c = sb("region_c", [P, NT * 3 * SBW], F32)
        region_d = sb("region_d", [P, 8192 + 2048], F32)

        hT_hi = region_a[:, 0:KT * T // 2].bitcast(FP16).rearrange("p (k t) -> p k t", k=KT)
        hT_lo = region_a[:, KT * T // 2:KT * T].bitcast(FP16).rearrange("p (k t) -> p k t", k=KT)
        x_all = region_b[:, 0:NT * D].rearrange("p (n d) -> p n d", n=NT)
        cm = region_b[:, :].rearrange("p (c t) -> p c t", c=16)
        tm = region_c[:, :].rearrange("p (n c) -> p n c", n=NT)

        ident = sb("ident", [P, P], F32)
        neg_tri = sb("neg_tri", [P, P], F32)
        neg_ones = sb("neg_ones", [P, P], F32)
        ones = sb("ones", [P, P], F32)
        head_ones = sb("head_ones", [P, P], F32)
        block_tri = sb("block_tri", [P, P], F32)
        keep = sb("keep", [P, P], F32)
        never = sb("never", [P, P], F32)
        eps = sb("eps", [P, 1], F32)
        g_q = sb("g_q", [P, 1], F32)
        g_k = sb("g_k", [P, 1], F32)
        g_mix = sb("g_mix", [P, 2 * HT], F32)
        sumsq = sb("sumsq", [P, 2 * NT], F32)
        rstd = sb("rstd", [P, 2 * NT], F32)

        bank = [ps(f"bank{i}", [P, 512], F32) for i in range(8)]

        g1_rows = region_d[:, 0:D]
        xn = [region_d[:, D:2 * D], region_d[:, 2 * D:3 * D]]
        sq_junk = region_d[:, 3 * D:4 * D]
        s_x, s_g1, s_small = sem("x_loaded"), sem("g1_loaded"), sem("gains_loaded")
        s_const, s_ss, s_rstd, s_xn = sem("const_ready"), sem("sumsq_ready"), sem("rstd_ready"), sem("xn_ready")
        s_xT, s_hhi, s_hlo = sem("xT_ready"), sem("h_hi_ready"), sem("h_lo_ready")
        with nc.Block() as block:
            @block.sync
            def _(sp):
                for n in range(4):
                    sp.dma_start(x_all[:, 2 * n:2 * n + 2, :],
                                 x[0, 2 * n * P:(2 * n + 2) * P, :].rearrange("(n p) d -> p n d", p=P)).then_inc(s_x, 16)
                sp.dma_start(g1_rows, norm1_g[0:1, :].partition_broadcast(P)).then_inc(s_g1, 16)
                for half in range(2):
                    sp.dma_start(g_q[64 * half:64 * half + 64, :], sb_q_norm_g[0, :].rearrange("(p a) -> p a", a=1)).then_inc(s_small, 16)
                    sp.dma_start(g_k[64 * half:64 * half + 64, :], sb_k_norm_g[0, :].rearrange("(p a) -> p a", a=1)).then_inc(s_small, 16)
                with nc.allow_non_contiguous_dma("gains, a few hundred words"):
                    sp.dma_start(g_mix[:, 0:HT], sb_out_norm_g[0, :].rearrange("(c p) -> p c", p=P)).then_inc(s_small, 16)
                    sp.dma_start(g_mix[:, HT:2 * HT], hg_out_norm_g[0, :].rearrange("(c p) -> p c", p=P)).then_inc(s_small, 16)
                sp.wait_ge(s_small, 96)

            @block.gpsimd
            def _(pool):
                pool.memset(ident[:, :], 0.0).then_inc(s_const, 1)
                pool.memset(neg_tri[:, :], -1.0).then_inc(s_const, 1)
                pool.memset(block_tri[:, :], 1.0).then_inc(s_const, 1)
                pool.memset(head_ones[:, :], 1.0).then_inc(s_const, 1)
                pool.memset(ones[:, :], 1.0).then_inc(s_const, 1)
                pool.memset(neg_ones[:, :], -1.0).then_inc(s_const, 1)
                pool.memset(eps[:, :], EPS).then_inc(s_const, 1)
                pool.memset(keep[:, :], 1.0).then_inc(s_const, 1)
                pool.memset(never[:, :], 0.0).then_inc(s_const, 1)
                pool.wait_ge(s_const, 9)
                pool.affine_select(out=never[:, :], in_=never[:, :], compare_op=ALU.is_gt, fill=-1.0e30, base=0,
                                   pattern=[[1, P]], channel_multiplier=-1).then_inc(s_const, 1)
                pool.affine_select(out=keep[:, :], in_=keep[:, :], compare_op=ALU.is_gt, fill=0.0, base=0,
                                   pattern=[[1, P]], channel_multiplier=-1).then_inc(s_const, 1)
                pool.affine_select(out=ident[:, :], in_=ident[:, :], compare_op=ALU.not_equal, fill=1.0, base=0,
                                   pattern=[[-1, P]], channel_multiplier=1).then_inc(s_const, 1)
                pool.affine_select(out=neg_tri[:, :], in_=neg_tri[:, :], compare_op=ALU.is_ge, fill=0.0, base=0,
                                   pattern=[[-1, P]], channel_multiplier=1).then_inc(s_const, 1)
                bt = block_tri[:, :].rearrange("p (c t) -> p c t", t=RB)
                ho = head_ones[:, :].rearrange("p (c t) -> p c t", t=DH)
                pool.affine_select(out=bt, in_=bt, compare_op=ALU.is_ge, fill=0.0, base=0,
                                   pattern=[[RB, NB], [1, RB]], channel_multiplier=-1).then_inc(s_const, 1)
                pool.affine_select(out=ho, in_=ho, compare_op=ALU.is_ge, fill=0.0, base=0,
                                   pattern=[[-DH, 2], [0, DH]], channel_multiplier=1).then_inc(s_const, 1)
                pool.wait_ge(s_const, 15)
                pool.affine_select(out=bt, in_=bt, compare_op=ALU.is_ge, fill=0.0, base=0,
                                   pattern=[[-RB, NB], [0, RB]], channel_multiplier=1).then_inc(s_const, 1)
                pool.affine_select(out=ho, in_=ho, compare_op=ALU.is_ge, fill=0.0, base=DH - 1,
                                   pattern=[[DH, 2], [0, DH]], channel_multiplier=-1).then_inc(s_const, 1)

            @block.scalar
            def _(act):
                act.wait_ge(s_const, 9)
                act.wait_ge(s_x, 64)
                for n in range(NT):
                    if n >= 1:
                        act.wait_ge(s_ss, n)
                    act.activation(sq_junk, x_all[:, n, :], ACT.Square,
                                   accum_out=sumsq[:, n:n + 1]).then_inc(s_ss, 1)
                act.wait_ge(s_ss, NT)
                act.activation(rstd[:, 0:NT], sumsq[:, 0:NT], ACT.Ln, bias=eps[:, :], scale=1.0 / D).then_inc(s_rstd, 1)
                act.wait_ge(s_rstd, 1)
                act.activation(rstd[:, 0:NT], rstd[:, 0:NT], ACT.Exp, scale=-0.5).then_inc(s_rstd, 1)
                with act.Fori(0, NT) as n:
                    for half in range(2):
                        act.wait_ge(s_xT, 2 * n + half + 1)
                        act.activation(hT_hi[:, 4 * half:4 * half + 4, ds(n * P, P)],
                                       bank[half][:, :].rearrange("p (k t) -> p k t", k=4), ACT.Copy).then_inc(s_hhi, 1)

            @block.vector
            def _(dve):
                dve.wait_ge(s_rstd, 2)
                dve.wait_ge(s_g1, 16)

                def scaled_row(n, at):
                    dve.scalar_tensor_tensor(out=xn[at], in0=x_all[:, n, :] if isinstance(n, int) else x_all[:, ds(n, 1), :].rearrange("p a d -> p (a d)"),
                                             scalar=rstd[:, n:n + 1] if isinstance(n, int) else rstd[:, ds(n, 1)],
                                             in1=g1_rows, op0=ALU.mult, op1=ALU.mult).then_inc(s_xn, 1)

                with dve.Fori(0, NT // 2) as m:
                    for par in range(2):
                        n = m * 2 + par
                        dve.wait_ge(s_xT, 4 * m + 2 * par)
                        scaled_row(n, par)
                        for half in range(2):
                            dve.wait_ge(s_hhi, 4 * m + 2 * par + half + 1)
                            dve.tensor_tensor(hT_lo[:, 4 * half:4 * half + 4, ds(n * P, P)],
                                              bank[half][:, :].rearrange("p (k t) -> p k t", k=4),
                                              hT_hi[:, 4 * half:4 * half + 4, ds(n * P, P)], ALU.subtract).then_inc(s_hlo, 1)

            @block.tensor
            def _(pe):
                pe.wait_ge(s_const, 17)
                with pe.Fori(0, NT // 2) as m:
                    for par in range(2):
                        pe.wait_ge(s_xn, 2 * m + par + 1)
                        for half in range(2):
                            pe.wait_ge(s_hlo, 4 * m + 2 * par)
                            for k in range(4):
                                at = (4 * half + k) * P
                                mm = pe.transpose(bank[half][:, k * P:(k + 1) * P], xn[par][:, at:at + P], ident[:, :])
                            mm.then_inc(s_xT, 1)

        w_raw = [region_d[:, n * KT * WC:(n + 1) * KT * WC].rearrange("p (k c) -> p k c", k=KT) for n in range(2)]
        w_par = [region_d[:, 2 * KT * WC + n * KT * WC:2 * KT * WC + (n + 1) * KT * WC].bitcast(FP16)
                 .rearrange("p (s k c) -> p s k c", s=2, k=KT) for n in range(2)]
        s_w = [sem("w_in_loaded0"), sem("w_in_loaded1")]
        s_whi, s_wlo, s_piece, s_evac = sem("w_hi_ready"), sem("w_lo_ready"), sem("piece_ready"), sem("piece_copied")
        w_in_k = w_in[0].rearrange("(k p) c -> p k c", p=P)
        RUNS = [(0, 4, True, 0), (1024, 2, False, 0), (1536, 2, True, 8), (2048, 4, False, 512), (3072, 2, True, 12)]
        PC = 4

        def chunk_runs(eng):
            first = 0
            for c0, n, major, dst in RUNS:
                with eng.Fori(0, n // 2) as m:
                    for par in range(2):
                        yield m * 2 + (first + par), m + first // 2, m * 2 + par, par, c0, major, dst
                first += n

        with nc.Block() as block:
            @block.sync
            def _(sp):
                for at, uses, n, par, c0, major, dst in chunk_runs(sp):
                    sp.wait_ge(s_wlo, at)
                    sp.dma_start(w_raw[par], w_in_k[:, :, ds(n * WC + c0, WC)]).then_inc(s_w[par], 16)

            @block.scalar
            def _(act):
                for at, uses, n, par, c0, major, dst in chunk_runs(act):
                    act.wait_ge(s_w[par], uses * 16 + 16)
                    act.wait_ge(s_piece, at * PC)
                    act.activation(w_par[par][:, 0], w_raw[par], ACT.Copy).then_inc(s_whi, 1)

            @block.gpsimd
            def _(pool):
                pool.nop().then_inc(s_wlo, 1)
                for at, uses, n, par, c0, major, dst in chunk_runs(pool):
                    pool.wait_ge(s_whi, at + 1)
                    pool.tensor_tensor(w_par[par][:, 1], w_raw[par], w_par[par][:, 0], ALU.subtract).then_inc(s_wlo, 1)

            @block.tensor
            def _(pe):
                pe.nop().then_inc(s_piece, PC)
                for at, uses, n, par, c0, major, dst in chunk_runs(pe):
                    pe.wait_ge(s_wlo, at + 2)
                    for q in range(PC):
                        pe.wait_ge(s_evac, at * PC + q)
                        if major:
                            ct, half = q // 2, q % 2
                            for k in range(KT):
                                w = [w_par[par][:, s, k, ct * P:(ct + 1) * P] for s in range(2)]
                                h = [t[:, k, half * 512:(half + 1) * 512] for t in (hT_hi, hT_lo)]
                                for j, (a, b) in enumerate(((w[0], h[0]), (w[0], h[1]), (w[1], h[0]))):
                                    mm = pe.matmul(bank[q][:, :], a, b, start=(k == 0 and j == 0),
                                                   stop=(k == KT - 1 and j == 2))
                        else:
                            for tt in range(2):
                                for k in range(KT):
                                    t0 = (2 * q + tt) * P
                                    w = [w_par[par][:, s, k, :] for s in range(2)]
                                    h = [t[:, k, t0:t0 + P] for t in (hT_hi, hT_lo)]
                                    for j, (a, b) in enumerate(((h[0], w[0]), (h[0], w[1]), (h[1], w[0]))):
                                        mm = pe.matmul(bank[q][:, tt * WC:(tt + 1) * WC], a, b,
                                                       start=(k == 0 and j == 0), stop=(k == KT - 1 and j == 2))
                        mm.then_inc(s_piece, 1)

            @block.vector
            def _(dve):
                dve.nop().then_inc(s_evac, PC - 1)
                for at, uses, n, par, c0, major, dst in chunk_runs(dve):
                    for q in range(PC):
                        dve.wait_ge(s_piece, at * PC + (PC + q + 1))
                        if major:
                            ct, half = q // 2, q % 2
                            dst_ap = cm[:, ds(n * 2 + (dst + ct), 1), half * 512:(half + 1) * 512].rearrange("p a t -> p (a t)")
                            dve.tensor_copy(dst_ap, bank[q][:, :]).then_inc(s_evac, 1)
                        else:
                            dve.tensor_copy(tm[:, 2 * q:2 * q + 2, ds(n * WC + dst, WC)],
                                            bank[q][:, :].rearrange("p (a c) -> p a c", a=2)).then_inc(s_evac, 1)
        if dbg is not None and dbg[0] == 2:
            s_dbg = sem("dbg")
            with nc.Block() as block:
                @block.sync
                def _(sp):
                    sp.dma_start(dbg[1][:, 0:16 * T], region_b[:, :]).then_inc(s_dbg, 16)
                    sp.dma_start(dbg[1][:, 16 * T:16 * T + NT * 3 * SBW], region_c[:, :]).then_inc(s_dbg, 16)
                    sp.dma_start(out[0], x[0]).then_inc(s_dbg, 16)
                    sp.wait_ge(s_dbg, 48)
            return

        def norm_buffers(base):
            sq = [region_d[:, base + n * 512:base + (n + 1) * 512] for n in range(2)]
            rs = [region_d[:, base + 1024 + n * 512:base + 1024 + (n + 1) * 512] for n in range(2)]
            return sq, rs

        gains = sb("gains", [P, 2 * HT], F32)
        s_gain = sem("gains_ready")
        s_sq, s_sumsq, s_ln, s_rs, s_nrm = sem("qk_sq"), sem("qk_sumsq"), sem("qk_ln"), sem("qk_rs"), sem("qk_normed")
        sq, rs = norm_buffers(0)
        with nc.Block() as block:
            @block.scalar
            def _(act):
                with act.Fori(0, 2 * HT) as c:
                    for half in range(2):
                        part = cm[:, ds(c, 1), half * 512:half * 512 + 512].rearrange("p a t -> p (a t)")
                        act.wait_ge(s_sumsq, c * 2)
                        act.activation(sq[half], part, ACT.Square).then_inc(s_sq, 1)
                    for half in range(2):
                        act.wait_ge(s_sumsq, c * 2 + (half + 1))
                        act.wait_ge(s_nrm, c * 2)
                        act.activation(rs[half], bank[half][:, :], ACT.Ln, bias=eps[:, :], scale=1.0 / DH).then_inc(s_ln, 1)
                        act.wait_ge(s_ln, c * 2 + (half + 1))
                        act.activation(rs[half], rs[half], ACT.Exp, scale=-0.5).then_inc(s_rs, 1)

            @block.tensor
            def _(pe):
                with pe.Fori(0, 2 * HT) as c:
                    for half in range(2):
                        pe.wait_ge(s_sq, c * 2 + (half + 1))
                        pe.wait_ge(s_ln, c * 2)
                        pe.matmul(bank[half][:, :], head_ones[:, :], sq[half], start=True, stop=True).then_inc(s_sumsq, 1)

            @block.vector
            def _(dve):
                dve.tensor_scalar(gains[:, 0:HT], ones[:, 0:HT], g_q[:, 0:1], DH ** -0.5, ALU.mult, ALU.mult).then_inc(s_gain, 1)
                dve.tensor_scalar(gains[:, HT:2 * HT], ones[:, 0:HT], g_k[:, 0:1], None, ALU.mult).then_inc(s_gain, 1)
                dve.wait_ge(s_gain, 2)
                with dve.Fori(0, 2 * HT) as c:
                    for half in range(2):
                        part = cm[:, ds(c, 1), half * 512:half * 512 + 512].rearrange("p a t -> p (a t)")
                        dve.wait_ge(s_rs, c * 2 + (half + 1))
                        dve.scalar_tensor_tensor(out=part, in0=part, scalar=gains[:, ds(c, 1)], in1=rs[half],
                                                 op0=ALU.mult, op1=ALU.mult).then_inc(s_nrm, 1)

        q_cur, k_cur = region_d[:, 0:T], region_d[:, T:2 * T]
        zc = [region_d[:, 2048 + n * 512:2560 + n * 512] for n in range(2)]
        lg = [region_d[:, 3072 + n * 512:3584 + n * 512] for n in range(2)]
        spl = [region_d[:, 4096 + n * 512:4608 + n * 512] for n in range(3)]
        wt = [region_d[:, 5632 + n * 512:6144 + n * 512] for n in range(2)]
        carry = [[region_d[:, 6656 + (2 * h + n) * 512:7168 + (2 * h + n) * 512] for n in range(2)] for h in range(2)]
        a_tm = [region_d[:, 8704 + n * 512:9216 + n * 512] for n in range(2)]
        SP_MAX = 40.0
        GB = 4
        steps = [(g, s, h) for g in range(NT // GB) for s in range(GB * (g + 1) - 1, -1, -1) for h in range(2)]
        NS = len(steps)
        diag = [s >= GB * g for g, s, h in steps]
        col = [max(0, s - GB * g) * P for g, s, h in steps]
        n_diag = [sum(diag[:n + 1]) for n in range(NS)]
        adds = [s > 0 for g, s, h in steps]
        n_adds = [sum(adds[:n + 1]) for n in range(NS)]
        ND, NA = n_diag[-1], n_adds[-1]
        turn = []
        seen = {}
        for g, s, h in steps:
            turn.append(seen.get((g, h), 0) % 2)
            seen[(g, h)] = seen.get((g, h), 0) + 1
        LAG_T, LAG_V = 2, 3
        zb, ab_bank, tb = bank[0:4], bank[4:6], bank[6]
        s_pair, s_z, s_cap, s_e, s_l = sem("pair_copied"), sem("z_ready"), sem("capped_ready"), sem("e_ready"), sem("log_ready")
        s_sp, s_spm, s_add, s_tri = sem("sp_ready"), sem("sp_masked"), sem("carry_ready"), sem("exponent_ready")
        s_wx, _, s_pv, s_asb, s_aT, s_acp = sem("w_ready"), None, sem("pv_done"), sem("a_rows_ready"), sem("aT_ready"), sem("aT_copied")
        with nc.Block() as block:
            @block.gpsimd
            def _(pool):
                with pool.Fori(0, HT) as c:
                    pool.wait_ge(s_z, c * NS)
                    pool.tensor_copy(q_cur, cm[:, ds(c, 1), :].rearrange("p a t -> p (a t)")).then_inc(s_pair, 1)
                    pool.tensor_copy(k_cur, cm[:, ds(c + HT, 1), :].rearrange("p a t -> p (a t)")).then_inc(s_pair, 1)

                    for n, (g, s, h) in enumerate(steps):
                        c0, size = col[n], GB * P - col[n]
                        pool.wait_ge(s_sp, c * NS + (n + 1))
                        if diag[n]:
                            pool.tensor_tensor(spl[n % 3][:, 0:P], spl[n % 3][:, 0:P], keep[:, :], ALU.mult).then_inc(s_spm, 1)
                            pool.wait_ge(s_spm, c * ND + n_diag[n])
                        if adds[n]:
                            if n >= 4:
                                pool.wait_ge(s_tri, c * NS + (n - 3))
                            new, old = carry[h][turn[n]], carry[h][1 - turn[n]]
                            if n >= 2 and adds[n - 2]:
                                pool.wait_ge(s_add, c * NA + n_adds[n - 2])
                            first = s == GB * (g + 1) - 1
                            edge = c0 + P if diag[n] else c0
                            if diag[n]:
                                cp = pool.tensor_tensor(new[:, c0:edge], spl[n % 3][:, 0:P], keep[:, :], ALU.mult)
                            if not first:
                                cp = pool.tensor_tensor(new[:, edge:512], old[:, edge:512], spl[n % 3][:, edge - c0:size], ALU.add)
                            cp.then_inc(s_add, 1)

            @block.vector
            def _(dve):
                with dve.Fori(0, HT) as c:
                    def capped(n):
                        size = GB * P - col[n]
                        dve.wait_ge(s_z, c * NS + (n + 1))
                        if n >= 2:
                            dve.wait_ge(s_e, c * NS + (n - 1))
                        dve.tensor_scalar(zc[n % 2][:, 0:size], zb[n % 4][:, 0:size], SP_MAX, None, ALU.min).then_inc(s_cap, 1)

                    capped(0)
                    for n, (g, s, h) in enumerate(steps):
                        size = GB * P - col[n]
                        if n + 1 < NS:
                            capped(n + 1)
                        dve.wait_ge(s_l, c * NS + (n + 1))
                        if n >= 3:
                            dve.wait_ge(s_tri, c * NS + (n - 2))
                            if n_adds[n - 3]:
                                dve.wait_ge(s_add, c * NA + n_adds[n - 3])
                        dve.tensor_tensor(spl[n % 3][:, 0:size], zb[n % 4][:, 0:size], lg[n % 2][:, 0:size],
                                          ALU.max).then_inc(s_sp, 1)
                    for g in range(2):
                        dve.wait_ge(s_aT, c * 2 + (g + 1))
                        dve.tensor_copy(cm[:, ds(c, 1), g * 512:g * 512 + 512].rearrange("p a t -> p (a t)"),
                                        tb[:, :]).then_inc(s_acp, 1)

            @block.scalar
            def _(act):
                with act.Fori(0, HT) as c:
                    def weight(n):
                        size = GB * P - col[n]
                        act.wait_ge(s_tri, c * NS + (n + 1))
                        if n >= 2:
                            act.wait_ge(s_pv, c * NS + (n - 1))
                        act.activation(wt[n % 2][:, 0:size], zb[n % 4][:, 0:size], ACT.Exp).then_inc(s_wx, 1)

                    for n, (g, s, h) in enumerate(steps):
                        size = GB * P - col[n]
                        act.wait_ge(s_cap, c * NS + (n + 1))
                        if n >= 2:
                            act.wait_ge(s_sp, c * NS + (n - 1))
                        act.activation(lg[n % 2][:, 0:size], zc[n % 2][:, 0:size], ACT.Exp).then_inc(s_e, 1)
                        act.wait_ge(s_e, c * NS + (n + 1))
                        act.activation(lg[n % 2][:, 0:size], lg[n % 2][:, 0:size], ACT.Ln, bias=ones[:, 0:1]).then_inc(s_l, 1)
                        if n >= 2:
                            weight(n - 2)
                    weight(NS - 2)
                    weight(NS - 1)
                    for g in range(2):
                        last = max(n for n in range(NS) if steps[n][0] == g)
                        act.wait_ge(s_pv, c * NS + (last + 1))
                        act.wait_ge(s_aT, c * 2)
                        act.activation(a_tm[g], ab_bank[g][:, :], ACT.Copy).then_inc(s_asb, 1)

            @block.tensor
            def _(pe):
                with pe.Fori(0, HT) as c:
                    pe.wait_ge(s_pair, c * 2 + 2)
                    for n in range(NS + LAG_V):
                        if n < NS:
                            g, s, h = steps[n]
                            size, t0 = GB * P - col[n], g * GB * P + col[n]
                            if n >= 4:
                                pe.wait_ge(s_wx, c * NS + (n - 3))
                            elif n == 0:
                                pe.wait_ge(s_wx, c * NS)
                            pe.matmul(zb[n % 4][:, 0:size], k_cur[64 * h:64 * h + 64, s * P:(s + 1) * P],
                                      q_cur[64 * h:64 * h + 64, t0:t0 + size], start=True, stop=True,
                                      skip_group_check=True).then_inc(s_z, 1)
                        m = n - LAG_T
                        if 0 <= m < NS:
                            g, s, h = steps[m]
                            size, c0 = GB * P - col[m], col[m]
                            if diag[m]:
                                pe.wait_ge(s_spm, c * ND + n_diag[m])
                            pe.wait_ge(s_sp, c * NS + (m + 1))
                            first = s == GB * (g + 1) - 1
                            mm = pe.matmul(zb[m % 4][:, 0:size], neg_tri[:, :], spl[m % 3][:, 0:size], start=False, stop=True,
                                           skip_group_check=True)
                            if not first:
                                pe.wait_ge(s_add, c * NA + n_adds[m - 2])
                                edge = c0 + P if diag[m] else c0
                                mm = pe.matmul(zb[m % 4][:, edge - c0:size], neg_ones[:, :], carry[h][turn[m - 2]][:, edge:512],
                                               start=False, stop=True, skip_group_check=True)
                            if diag[m]:
                                mm = pe.matmul(zb[m % 4][:, 0:P], ident[:, :], never[:, :], start=False, stop=True,
                                               skip_group_check=True)
                            mm.then_inc(s_tri, 1)
                        m = n - LAG_V
                        if 0 <= m < NS:
                            g, s, h = steps[m]
                            c0 = col[m]
                            pe.wait_ge(s_wx, c * NS + (m + 1))
                            if m == 0:
                                pe.wait_ge(s_asb, c * 2)
                            for b in range(c0 // P, GB):
                                mm = pe.matmul(ab_bank[g][:, b * P + 64 * h:b * P + 64 * h + 64],
                                               wt[m % 2][:, b * P - c0:b * P - c0 + P],
                                               tm[:, s, ds(c * P + 64 * h, 64)],
                                               start=(s == GB * (g + 1) - 1 and h == 0), stop=(s == 0), skip_group_check=True)
                            mm.then_inc(s_pv, 1)
                    for g in range(2):
                        pe.wait_ge(s_asb, c * 2 + (g + 1))
                        pe.wait_ge(s_acp, c * 2 + g)
                        for b in range(GB):
                            mm = pe.transpose(tb[:, b * P:(b + 1) * P], a_tm[g][:, b * P:(b + 1) * P], ident[:, :])
                        mm.then_inc(s_aT, 1)
        if dbg is not None and dbg[0] == 4:
            s_dbg = sem("dbg")
            with nc.Block() as block:
                @block.sync
                def _(sp):
                    sp.dma_start(dbg[1][:, 0:16 * T], region_b[:, :]).then_inc(s_dbg, 16)
                    sp.dma_start(out[0], x[0]).then_inc(s_dbg, 16)
                    sp.wait_ge(s_dbg, 32)
            return
        W4 = NH * P

        def tmp(n, count=1):
            return region_d[:, n * 512:(n + count) * 512]

        lb_rows, oml_rows = tmp(0), tmp(1)
        fc, e_f, r_f, k_tm, log_f = tmp(2), tmp(3), tmp(4), tmp(5), tmp(6)
        i_cur, eb, enb, qe, ke, kd, kd_tm, att = (tmp(n) for n in range(7, 15))
        state = [tmp(15 + n) for n in range(4)]
        b_bank, kt_bank, att_bank, o_bank = bank[0:4]
        u_bank = bank[4:8]
        F_MIN = -80.0
        heads = lambda ap: ap.rearrange("p (h t) -> p h t", h=NH)
        blocks = lambda ap: ap.rearrange("p (g t) -> p g t", t=RB)
        s_lbl, s_lb = sem("lb_logits_loaded"), sem("lb_steps")
        s_fc, s_ef, s_fd, s_lf1, s_lf = sem("f_capped"), sem("f_exp"), sem("f_steps"), sem("log_f_input"), sem("log_f_ready")
        s_icur, s_b, s_kT, s_ebr, s_qk, s_kd = sem("i_copied"), sem("b_ready"), sem("kT_ready"), sem("exp_b_ready"), sem("qe_ke_ready"), sem("kd_ready")
        s_kdT, s_kdtm, s_att, s_attm, s_u = sem("kdT_ready"), sem("kd_rows_ready"), sem("att_ready"), sem("att_masked"), sem("u_ready")
        s_st, s_o, s_or = sem("state_ready"), sem("o_ready"), sem("o_copied")
        with nc.Block() as block:
            @block.sync
            def _(sp):
                sp.dma_start(tmp(2), hg_lb_logits[0:1, :].partition_broadcast(P)).then_inc(s_lbl, 16)
                sp.dma_start(tmp(3), hg_lb_logits[1:2, :].partition_broadcast(P)).then_inc(s_lbl, 16)

            @block.gpsimd
            def _(pool):
                with pool.Fori(0, NT) as n:
                    pool.wait_ge(s_o, n)
                    pool.tensor_copy(i_cur, tm[:, ds(n, 1), 2 * SBW:3 * SBW].rearrange("p a c -> p (a c)")).then_inc(s_icur, 1)
                    pool.wait_ge(s_fd, n * 4 + 2)
                    pool.wait_ge(s_b, n)
                    pool.tensor_tensor(log_f, r_f, oml_rows, ALU.mult).then_inc(s_lf1, 1)
                    pool.wait_ge(s_lf1, n * 2 + 1)
                    pool.tensor_tensor(log_f, log_f, lb_rows, ALU.add).then_inc(s_lf1, 1)

            @block.scalar
            def _(act):
                act.wait_ge(s_lb, 3)
                act.activation(tmp(2), tmp(2), ACT.Exp).then_inc(s_lb, 1)
                act.activation(tmp(3), tmp(3), ACT.Exp).then_inc(s_lb, 1)
                with act.Fori(0, NT) as n:
                    act.wait_ge(s_fc, n + 1)
                    act.activation(e_f, fc, ACT.Exp, scale=-1.0).then_inc(s_ef, 1)
                    act.wait_ge(s_lf1, n * 2 + 2)
                    act.activation(log_f, log_f, ACT.Ln).then_inc(s_lf, 1)
                    act.wait_ge(s_b, n + 1)
                    act.activation(eb, b_bank[:, :], ACT.Exp).then_inc(s_ebr, 1)
                    act.activation(enb, b_bank[:, :], ACT.Exp, scale=-1.0).then_inc(s_ebr, 1)
                    act.wait_ge(s_kdT, n + 1)
                    act.activation(kd_tm, kt_bank[:, :], ACT.Copy).then_inc(s_kdtm, 1)
                    act.wait_ge(s_o, n + 1)
                    act.activation(cm[:, 2 * HT:2 * HT + NH, ds(n * P, P)], heads(o_bank[:, :]), ACT.Copy).then_inc(s_or, 1)

            @block.vector
            def _(dve):
                dve.wait_ge(s_lbl, 32)
                dve.tensor_tensor(tmp(4), tmp(2), tmp(3), ALU.max).then_inc(s_lb, 1)
                dve.wait_ge(s_lb, 1)
                dve.tensor_tensor(tmp(2), tmp(2), tmp(4), ALU.subtract).then_inc(s_lb, 1)
                dve.tensor_tensor(tmp(3), tmp(3), tmp(4), ALU.subtract).then_inc(s_lb, 1)
                dve.wait_ge(s_lb, 5)
                dve.tensor_tensor(tmp(4), tmp(2), tmp(3), ALU.add).then_inc(s_lb, 1)
                dve.wait_ge(s_lb, 6)
                dve.reciprocal(tmp(4), tmp(4)).then_inc(s_lb, 1)
                dve.wait_ge(s_lb, 7)
                dve.tensor_tensor(lb_rows, tmp(2), tmp(4), ALU.mult).then_inc(s_lb, 1)
                dve.wait_ge(s_lb, 8)
                dve.tensor_scalar(oml_rows, lb_rows, -1.0, 1.0, ALU.mult, ALU.add).then_inc(s_lb, 1)
                dve.memset(state[0], 0.0).then_inc(s_lb, 1)
                dve.wait_ge(s_lb, 10)
                with dve.Fori(0, NT) as n:
                    dve.wait_ge(s_ef, n)
                    dve.tensor_scalar(fc, tm[:, ds(n, 1), SBW:2 * SBW].rearrange("p a c -> p (a c)"), F_MIN, None, ALU.max).then_inc(s_fc, 1)
                    dve.wait_ge(s_ef, n + 1)
                    dve.wait_ge(s_lf1, n * 2)
                    dve.tensor_scalar(r_f, e_f, 1.0, None, ALU.add).then_inc(s_fd, 1)
                    dve.wait_ge(s_fd, n * 4 + 1)
                    dve.reciprocal(r_f, r_f).then_inc(s_fd, 1)
                    dve.wait_ge(s_fd, n * 4 + 2)
                    dve.tensor_tensor(k_tm, e_f, r_f, ALU.mult).then_inc(s_fd, 1)
                    dve.wait_ge(s_fd, n * 4 + 3)
                    dve.tensor_tensor(k_tm, k_tm, oml_rows, ALU.mult).then_inc(s_fd, 1)
                    dve.wait_ge(s_ebr, n * 2 + 2)
                    dve.tensor_tensor(heads(qe), cm[:, 2 * HT:2 * HT + NH, ds(n * P, P)], heads(eb), ALU.mult).then_inc(s_qk, 1)
                    dve.wait_ge(s_kT, n + 1)
                    dve.tensor_tensor(ke, kt_bank[:, :], enb, ALU.mult).then_inc(s_qk, 1)
                    dve.wait_ge(s_qk, n * 2 + 2)
                    dve.tensor_tensor(blocks(kd), blocks(ke), blocks(eb)[:, :, RB - 1:RB].to_broadcast([P, NH * NB, RB]),
                                      ALU.mult).then_inc(s_kd, 1)
                    dve.wait_ge(s_att, n + 1)
                    dve.tensor_tensor(heads(att), heads(att_bank[:, :]), block_tri[:, :].unsqueeze(1).to_broadcast([P, NH, P]),
                                      ALU.mult).then_inc(s_attm, 1)
                    dve.wait_ge(s_u, n + 1)
                    for c in range(NB):
                        if c:
                            dve.wait_ge(s_st, n * (NB * NH) + c * NH)
                        if c == NB - 1:
                            dve.wait_ge(s_o, n + 1)
                        for h in range(NH):
                            last = h * P + c * RB + RB - 1
                            dve.scalar_tensor_tensor(out=state[(c + 1) % NB][:, h * P:(h + 1) * P], in0=state[c][:, h * P:(h + 1) * P],
                                                     scalar=eb[:, last:last + 1], in1=u_bank[c][:, h * P:(h + 1) * P],
                                                     op0=ALU.mult, op1=ALU.add).then_inc(s_st, 1)

            @block.tensor
            def _(pe):
                with pe.Fori(0, NT) as n:
                    pe.wait_ge(s_lf, n + 1)
                    for h in range(NH):
                        mm = pe.matmul(b_bank[:, h * P:(h + 1) * P], log_f[:, h * P:(h + 1) * P], block_tri[:, :], start=True, stop=True)
                    mm.then_inc(s_b, 1)
                    pe.wait_ge(s_fd, n * 4 + 4)
                    for h in range(NH):
                        mm = pe.transpose(kt_bank[:, h * P:(h + 1) * P], k_tm[:, h * P:(h + 1) * P], ident[:, :])
                    mm.then_inc(s_kT, 1)
                    pe.wait_ge(s_kd, n + 1)
                    for h in range(NH):
                        mm = pe.transpose(kt_bank[:, h * P:(h + 1) * P], kd[:, h * P:(h + 1) * P], ident[:, :])
                    mm.then_inc(s_kdT, 1)
                    for h in range(NH):
                        mm = pe.matmul(att_bank[:, h * P:(h + 1) * P], ke[:, h * P:(h + 1) * P], qe[:, h * P:(h + 1) * P], start=True, stop=True)
                    mm.then_inc(s_att, 1)
                    pe.wait_ge(s_kdtm, n + 1)
                    pe.wait_ge(s_icur, n + 1)
                    pe.wait_ge(s_st, n * (NB * NH))
                    for c in range(NB):
                        rows = slice(c * RB, (c + 1) * RB)
                        for h in range(NH):
                            mm = pe.matmul(u_bank[c][:, h * P:(h + 1) * P], kd_tm[rows, h * P:(h + 1) * P], i_cur[rows, h * P:(h + 1) * P],
                                           start=True, stop=True)
                    mm.then_inc(s_u, 1)
                    pe.wait_ge(s_attm, n + 1)
                    pe.wait_ge(s_or, n)
                    for h in range(NH):
                        pe.matmul(o_bank[:, h * P:(h + 1) * P], i_cur[:, h * P:(h + 1) * P], att[:, h * P:(h + 1) * P],
                                  start=(h == 0), stop=False, skip_group_check=True)
                    for c in range(NB):
                        if c:
                            pe.wait_ge(s_st, n * (NB * NH) + c * NH)
                        for h in range(NH):
                            at = h * P + c * RB
                            mm = pe.matmul(o_bank[:, at:at + RB], state[c][:, h * P:(h + 1) * P], qe[:, at:at + RB],
                                           start=False, stop=True, skip_group_check=True)
                    mm.then_inc(s_o, 1)

        mix_hi, mix_lo = hT_hi, hT_lo
        sq, rs = norm_buffers(0)
        gate_t = [tmp(4), tmp(5)]
        mixed = [tmp(6), tmp(7)]
        wo_raw = region_c[:, 0:KT * D].rearrange("p (k c) -> p k c", k=KT)
        s_wo, s_mq, s_ms, s_mln, s_mrs = sem("w_out_loaded"), sem("mix_sq"), sem("mix_sumsq"), sem("mix_ln"), sem("mix_rs")
        s_gs_r = sem("gate_times_rs")
        s_gc, s_ge, s_gs, s_mx, s_mhi, s_mlo = sem("gate_capped"), sem("gate_exp"), sem("gate_steps"), sem("mix_ready"), sem("mix_hi_ready"), sem("mix_lo_ready")
        with nc.Block() as block:
            @block.sync
            def _(sp):
                sp.dma_start(wo_raw, w_out[0].rearrange("(k p) c -> p k c", p=P)).then_inc(s_wo, 16)

            def tiles(eng):
                for first, src in ((0, 0), (HT, 2 * HT)):
                    with eng.Fori(0, HT) as c:
                        yield c, c + first, src, first > 0

            @block.scalar
            def _(act):
                for c, k, src, rec in tiles(act):
                    for half in range(2):
                        part = cm[:, ds(c + src, 1), half * 512:half * 512 + 512].rearrange("p a t -> p (a t)")
                        act.wait_ge(s_ms, k * 2)
                        act.activation(sq[half], part, ACT.Square).then_inc(s_mq, 1)
                    if rec:
                        for half in range(2):
                            act.wait_ge(s_gc, c * 2 + (half + 1))
                            act.activation(gate_t[half], gate_t[half], ACT.Exp, scale=-1.0).then_inc(s_ge, 1)
                    for half in range(2):
                        act.wait_ge(s_ms, k * 2 + (half + 1))
                        act.wait_ge(s_mx, k * 2)
                        act.activation(rs[half], bank[half][:, :], ACT.Ln, bias=eps[:, :], scale=1.0 / (P if rec else DH)).then_inc(s_mln, 1)
                        act.wait_ge(s_mln, k * 2 + (half + 1))
                        act.activation(rs[half], rs[half], ACT.Exp, scale=-0.5).then_inc(s_mrs, 1)
                    for half in range(2):
                        act.wait_ge(s_mx, k * 2 + (half + 1))
                        act.activation(mix_hi[:, ds(k, 1), half * 512:half * 512 + 512].rearrange("p a t -> p (a t)"), mixed[half],
                                       ACT.Copy).then_inc(s_mhi, 1)

            @block.tensor
            def _(pe):
                for c, k, src, rec in tiles(pe):
                    for half in range(2):
                        pe.wait_ge(s_mq, k * 2 + (half + 1))
                        pe.wait_ge(s_mln, k * 2)
                        pe.matmul(bank[half][:, :], (ones if rec else head_ones)[:, :], sq[half], start=True, stop=True).then_inc(s_ms, 1)

            @block.vector
            def _(dve):
                for c, k, src, rec in tiles(dve):
                    if rec:
                        for half in range(2):
                            part = cm[:, ds(c + 3 * HT, 1), half * 512:half * 512 + 512].rearrange("p a t -> p (a t)")
                            dve.wait_ge(s_mx, k * 2)
                            dve.tensor_scalar(gate_t[half], part, F_MIN, None, ALU.max).then_inc(s_gc, 1)
                        for half in range(2):
                            part = cm[:, ds(c + 3 * HT, 1), half * 512:half * 512 + 512].rearrange("p a t -> p (a t)")
                            dve.wait_ge(s_ge, c * 2 + (half + 1))
                            dve.tensor_scalar(gate_t[half], gate_t[half], 1.0, None, ALU.add).then_inc(s_gs, 1)
                            dve.wait_ge(s_gs, c * 6 + (3 * half + 1))
                            dve.reciprocal(gate_t[half], gate_t[half]).then_inc(s_gs, 1)
                            dve.wait_ge(s_gs, c * 6 + (3 * half + 2))
                            dve.tensor_tensor(gate_t[half], gate_t[half], part, ALU.mult).then_inc(s_gs, 1)
                    for half in range(2):
                        part = cm[:, ds(c + src, 1), half * 512:half * 512 + 512].rearrange("p a t -> p (a t)")
                        dve.wait_ge(s_mrs, k * 2 + (half + 1))
                        dve.wait_ge(s_mlo, k * 2)
                        if rec:
                            dve.wait_ge(s_gs, c * 6 + (3 * half + 3))
                            dve.tensor_tensor(rs[half], rs[half], gate_t[half], ALU.mult).then_inc(s_gs_r, 1)
                            dve.wait_ge(s_gs_r, c * 2 + (half + 1))
                        dve.scalar_tensor_tensor(out=mixed[half], in0=part, scalar=g_mix[:, ds(k, 1)], in1=rs[half],
                                                 op0=ALU.mult, op1=ALU.mult).then_inc(s_mx, 1)
                    for half in range(2):
                        dve.wait_ge(s_mhi, k * 2 + (half + 1))
                        hi, lo = (t[:, ds(k, 1), half * 512:half * 512 + 512].rearrange("p a t -> p (a t)") for t in (mix_hi, mix_lo))
                        dve.tensor_tensor(lo, mixed[half], hi, ALU.subtract).then_inc(s_mlo, 1)
        if dbg is not None and dbg[0] == 6:
            s_dbg = sem("dbg")
            with nc.Block() as block:
                @block.sync
                def _(sp):
                    sp.dma_start(dbg[1][:, 0:16 * T], region_b[:, :]).then_inc(s_dbg, 16)
                    sp.dma_start(dbg[1][:, 16 * T:16 * T + KT * T], region_a[:, :]).then_inc(s_dbg, 16)
                    sp.dma_start(out[0], x[0]).then_inc(s_dbg, 16)
                    sp.wait_ge(s_dbg, 48)
            return
        NE = w_router.shape[2]
        TOPK = 4
        x2_all = region_b[:, 0:NT * D].rearrange("p (n d) -> p n d", n=NT)

        def unit(n):
            return region_b[:, NT * D + n * D:NT * D + (n + 1) * D]

        h2, h2T, g2_rows, junk2, gT, w_r, b_dn = (unit(n) for n in range(7))
        w_r = w_r[:, 0:KT * NE].rearrange("p (k e) -> p k e", k=KT)
        wo_hi = region_d[:, 0:KT * D // 2].bitcast(FP16).rearrange("p (k c) -> p k c", k=KT)
        wo_lo = region_d[:, KT * D // 2:KT * D].bitcast(FP16).rearrange("p (k c) -> p k c", k=KT)
        SL = 160
        HS = SL // 2
        MAXC = -(-T // SL)
        ITEMS = NE + T * TOPK // SL
        TAB = ITEMS + 8
        rows_out = nc.dram_tensor("rows_out", (T + SL, D), F32, kind="Internal").ap()
        rows_h2 = nc.dram_tensor("rows_h2", (T, D), F32, kind="Internal").ap()
        logit = sb("logit", [P, NT, NE + TOPK], F32)
        b_r = sb("b_r", [P, NE], F32)
        s_x2, s_w7, s_wohi, s_wolo = sem("x_reloaded"), sem("router_loaded"), sem("wo_hi_ready"), sem("wo_lo_ready")
        s_pr, s_x2r, s_sq2, s_l2, s_rs2, s_h2 = sem("mix_product"), sem("x2_ready"), sem("x2_sumsq"), sem("x2_ln"), sem("x2_rstd"), sem("h2_ready")
        s_h2st, s_h2T, s_h2Tc, s_lgt, s_lgc, s_pad = sem("h2_stored"), sem("h2T_ready"), sem("h2T_copied"), sem("logits_ready"), sem("logits_copied"), sem("pad_ready")
        PAD = -3.0e38
        with nc.Block() as block:
            @block.sync
            def _(sp):
                for n in range(4):
                    sp.dma_start(x2_all[:, 2 * n:2 * n + 2, :],
                                 x[0, 2 * n * P:(2 * n + 2) * P, :].rearrange("(n p) d -> p n d", p=P)).then_inc(s_x2, 16)
                sp.dma_start(g2_rows, norm2_g[0:1, :].partition_broadcast(P)).then_inc(s_w7, 16)
                sp.dma_start(w_r, w_router[0].rearrange("(k p) e -> p k e", p=P)).then_inc(s_w7, 16)
                sp.dma_start(b_r[:, :], b_router[0:1, :].partition_broadcast(P)).then_inc(s_w7, 16)
                sp.dma_start(b_dn[0:NE, :], b_down[0]).then_inc(s_w7, 16)
                with sp.Fori(0, NT) as n:
                    sp.wait_ge(s_h2, n + 1)
                    sp.dma_start(rows_h2[ds(n * P, P), :], h2).then_inc(s_h2st, 16)
                sp.wait_ge(s_h2st, 16 * NT)
                sp.wait_ge(s_w7, 64)

            @block.gpsimd
            def _(pool):
                pool.memset(logit[:, :, :], PAD).then_inc(s_pad, 1)
                for k in range(KT):
                    pool.wait_ge(s_wohi, k + 1)
                    pool.tensor_tensor(wo_lo[:, k, :], wo_raw[:, k, :], wo_hi[:, k, :], ALU.subtract).then_inc(s_wolo, 1)

            @block.scalar
            def _(act):
                act.wait_ge(s_wo, 16)
                for k in range(KT):
                    act.activation(wo_hi[:, k, :], wo_raw[:, k, :], ACT.Copy).then_inc(s_wohi, 1)
                act.wait_ge(s_pad, 1)
                with act.Fori(0, NT) as n:
                    act.wait_ge(s_x2r, n * 2 + 2)
                    act.activation(junk2, x2_all[:, ds(n, 1), :].rearrange("p a d -> p (a d)"), ACT.Square,
                                   accum_out=sumsq[:, 0:1]).then_inc(s_sq2, 1)
                    act.wait_ge(s_sq2, n + 1)
                    act.activation(rstd[:, 0:1], sumsq[:, 0:1], ACT.Ln, bias=eps[:, :], scale=1.0 / D).then_inc(s_l2, 1)
                    act.wait_ge(s_l2, n + 1)
                    act.wait_ge(s_h2, n)
                    act.activation(rstd[:, 1:2], rstd[:, 0:1], ACT.Exp, scale=-0.5).then_inc(s_rs2, 1)
                    for half in range(2):
                        act.wait_ge(s_h2T, n * 2 + (half + 1))
                        act.activation(h2T[:, half * 512:half * 512 + 512], bank[2 + half][:, :], ACT.Copy).then_inc(s_h2Tc, 1)
                    act.wait_ge(s_lgt, n + 1)
                    act.activation(logit[:, ds(n, 1), 0:NE].rearrange("p a e -> p (a e)"), bank[4][:, 0:NE], ACT.Copy).then_inc(s_lgc, 1)

            @block.vector
            def _(dve):
                dve.wait_ge(s_x2, 64)
                dve.wait_ge(s_w7, 64)
                with dve.Fori(0, NT) as n:
                    for half in range(2):
                        part = x2_all[:, ds(n, 1), half * 512:half * 512 + 512].rearrange("p a d -> p (a d)")
                        dve.wait_ge(s_pr, n * 2 + (half + 1))
                        dve.tensor_tensor(part, part, bank[half][:, :], ALU.add).then_inc(s_x2r, 1)
                    dve.wait_ge(s_rs2, n + 1)
                    dve.wait_ge(s_h2T, n * 2)
                    dve.wait_ge(s_h2st, n * 16)
                    dve.scalar_tensor_tensor(out=h2, in0=x2_all[:, ds(n, 1), :].rearrange("p a d -> p (a d)"), scalar=rstd[:, 1:2],
                                             in1=g2_rows, op0=ALU.mult, op1=ALU.mult).then_inc(s_h2, 1)

            @block.tensor
            def _(pe):
                def project(n, half):
                    pe.wait_ge(s_x2r, n * 2 - 0 if isinstance(n, int) else n * 2)
                    for k in range(KT):
                        m = [t[:, k, ds(n * P, P)] for t in (mix_hi, mix_lo)]
                        w = [t[:, k, half * 512:half * 512 + 512] for t in (wo_hi, wo_lo)]
                        for j, (a, b) in enumerate(((m[0], w[0]), (m[0], w[1]), (m[1], w[0]))):
                            mm = pe.matmul(bank[half][:, :], a, b, start=(k == 0 and j == 0), stop=(k == KT - 1 and j == 2))
                    mm.then_inc(s_pr, 1)

                def turn_h2(n):
                    pe.wait_ge(s_h2, n + 1)
                    pe.wait_ge(s_h2Tc, n * 2)
                    for half in range(2):
                        for k in range(4):
                            mm = pe.transpose(bank[2 + half][:, k * P:(k + 1) * P], h2[:, (4 * half + k) * P:(4 * half + k + 1) * P], ident[:, :])
                        mm.then_inc(s_h2T, 1)

                def route(n):
                    pe.wait_ge(s_h2Tc, n * 2 + 2)
                    pe.wait_ge(s_lgc, n)
                    for k in range(KT):
                        mm = pe.matmul(bank[4][:, 0:NE], h2T[:, k * P:(k + 1) * P], w_r[:, k, :], start=(k == 0), stop=(k == KT - 1))
                    mm.then_inc(s_lgt, 1)

                pe.wait_ge(s_wolo, KT)
                pe.wait_ge(s_w7, 64)
                project(0, 0)
                project(0, 1)
                with pe.Fori(0, NT - 1) as n:
                    project(n + 1, 0)
                    turn_h2(n)
                    project(n + 1, 1)
                    route(n)
                turn_h2(NT - 1)
                route(NT - 1)

        gate = sb("gate", [P, NT, NE], F32)
        mask = sb("mask", [P, NT, NE], F32)
        slot = sb("slot", [P, NT, NE], F32)
        gate3 = sb("gate3", [P, NT, 3, NE], BF16)
        b_gu = sb("b_gu", [P, NE * 2 * KT], F32)
        iota = sb("iota", [P, MAXC * SL], F32)
        values = sb("values", [P, NT, 6], BF16)
        table = sb("table", [1, 2 * TAB + 2], I32)
        spare = sb("spare", [P, HS], F32)
        work = region_c[:, :]
        w_off = [0]

        def take(n):
            w_off[0] += n
            return work[:, w_off[0] - n:w_off[0]]

        top = take(NT * 8).rearrange("p (n k) -> p n k", n=NT)
        rep = take(NT * (NE + TOPK)).rearrange("p (n e) -> p n e", n=NT)
        lg = take(NT * NE).rearrange("p (n e) -> p n e", n=NT)
        ssum, rsum = take(NT), take(NT)
        res = take(NT * NE).rearrange("p (n e) -> p n e", n=NT)
        lt = take(P)
        n_col, code_e = take(1), take(1)
        thr, over, before, cum, pos_i = take(MAXC - 1), take(MAXC - 1), take(MAXC - 1), take(MAXC - 1), take(MAXC - 1)
        hot = take((MAXC - 1) * TAB).rearrange("p (c j) -> p c j", c=MAXC - 1)
        code_c = take(MAXC - 1)
        row_f = take(2 * TAB + 2)
        val_f = take(NT * 2).rearrange("p (n v) -> p n v", n=NT)
        bgu_rows = take(4 * P).rearrange("p (n c) -> p n c", n=4)
        zeros = take(D)
        hot_slots = ITEMS
        s_p8 = sem("constants8_ready")
        s_lt, s_d8, s_a8, s_t8 = sem("table_inputs"), sem("routing_steps"), sem("routing_exp"), sem("gate_turned")
        s_gTc, s_bd, s_base, s_bst, s_cnt = sem("gateT_copied"), sem("bias_product"), sem("base_ready"), sem("base_stored"), sem("counts_ready")
        s_bgl, s_bgt, s_bgc, s_tabp, s_trash = sem("bgu_loaded"), sem("bgu_turned"), sem("bgu_copied"), sem("table_product"), sem("trash_cleared")
        NP8 = 12
        with nc.Block() as block:
            @block.sync
            def _(sp):
                sp.dma_start(bgu_rows, b_gate_up[0].rearrange("e (j c) -> (e j) c", c=P).rearrange("(n p) c -> p n c", p=P)).then_inc(s_bgl, 16)
                sp.wait_ge(s_p8, NP8)
                sp.dma_start(rows_out[T:T + P, :], zeros).then_inc(s_trash, 16)
                sp.dma_start(rows_out[T + P:T + SL, :], zeros[0:SL - P, :]).then_inc(s_trash, 16)
                for n in range(NT):
                    sp.wait_ge(s_base, 2 * n + 2)
                    sp.dma_start(rows_out[n * P:(n + 1) * P, :], x2_all[:, n, :]).then_inc(s_bst, 16)
                sp.wait_ge(s_bst, 16 * NT)
                sp.wait_ge(s_trash, 32)

            @block.gpsimd
            def _(pool):
                pool.memset(lt, 1.0).then_inc(s_p8, 1)
                pool.memset(zeros, 0.0).then_inc(s_p8, 1)
                pool.memset(values[:, :, 2:3], -1.0).then_inc(s_p8, 1)
                pool.memset(row_f, 0.0).then_inc(s_p8, 1)
                pool.iota(iota[:, :], [[1, MAXC * SL]], base=0, channel_multiplier=0, allow_small_or_imprecise_dtypes=True).then_inc(s_p8, 1)
                pool.iota(val_f[:, :, 0:1], [[P, NT]], base=0, channel_multiplier=0, allow_small_or_imprecise_dtypes=True).then_inc(s_p8, 1)
                pool.iota(val_f[:, :, 1:2], [[0, NT]], base=0, channel_multiplier=1, allow_small_or_imprecise_dtypes=True).then_inc(s_p8, 1)
                pool.iota(code_e, [[0, 1]], base=0, channel_multiplier=1, allow_small_or_imprecise_dtypes=True).then_inc(s_p8, 1)
                pool.iota(thr, [[SL, MAXC - 1]], base=SL, channel_multiplier=0, allow_small_or_imprecise_dtypes=True).then_inc(s_p8, 1)
                pool.wait_ge(s_p8, 9)
                pool.affine_select(out=lt, in_=lt, compare_op=ALU.is_gt, fill=0.0, base=0, pattern=[[1, P]],
                                   channel_multiplier=-1).then_inc(s_p8, 1)
                pool.tensor_copy(values[:, :, 0:2], val_f).then_inc(s_p8, 1)
                pool.tensor_copy(code_c, thr).then_inc(s_p8, 1)

            @block.scalar
            def _(act):
                act.wait_ge(s_d8, 2 + NT + 1 + NT + 2)
                act.activation(lg, lg, ACT.Exp).then_inc(s_a8, 1)
                for b in range(2):
                    act.wait_ge(s_t8, b + 1)
                    act.activation(gT[0:NE, b * 512:(b + 1) * 512], bank[b][0:NE, :], ACT.Copy).then_inc(s_gTc, 1)
                act.wait_ge(s_bgt, 1)
                act.activation(b_gu[:, :], bank[6][:, :], ACT.Copy).then_inc(s_bgc, 1)

            @block.vector
            def _(dve):
                step = [0]

                def link(ins):
                    step[0] += 1
                    ins.then_inc(s_d8, 1)
                    dve.wait_ge(s_d8, step[0])

                link(dve.tensor_tensor(lg, logit[:, :, 0:NE], b_r[:, :].unsqueeze(1).to_broadcast([P, NT, NE]), ALU.add))
                link(dve.tensor_copy(logit[:, :, 0:NE], lg))
                for n in range(NT):
                    link(dve.max(out=top[:, n, :], in_=logit[:, n, :]))
                link(dve.tensor_tensor(lg, lg, top[:, :, 0:1].to_broadcast([P, NT, NE]), ALU.subtract))
                link(dve.memset(top[:, :, TOPK:8], PAD))
                for n in range(NT):
                    link(dve.match_replace(out=rep[:, n, :], in_to_replace=top[:, n, :], in_values=logit[:, n, :], imm_value=-PAD))
                link(dve.tensor_scalar(mask[:, :, :], rep[:, :, 0:NE], 1.0e38, None, ALU.is_ge))
                assert step[0] == 2 + NT + 1 + NT + 2
                dve.wait_ge(s_a8, 1)
                link(dve.tensor_tensor(lg, lg, mask[:, :, :], ALU.mult))
                link(dve.tensor_reduce(ssum, lg, AX_X, ALU.add))
                link(dve.reciprocal(rsum, ssum))
                link(dve.tensor_tensor(gate[:, :, :], lg, rsum.unsqueeze(2).to_broadcast([P, NT, NE]), ALU.mult))
                dve.nop().then_inc(s_lt, 1)
                link(dve.tensor_copy(gate3[:, :, 0, :], gate[:, :, :]))
                link(dve.tensor_tensor(res, gate[:, :, :], gate3[:, :, 0, :], ALU.subtract))
                link(dve.tensor_copy(gate3[:, :, 1, :], res))
                link(dve.tensor_tensor(res, res, gate3[:, :, 1, :], ALU.subtract))
                link(dve.tensor_copy(gate3[:, :, 2, :], res))
                dve.wait_ge(s_cnt, 1)
                pos = bank[2][:, 0:NT * NE].rearrange("p (n e) -> p n e", n=NT)
                link(dve.scalar_tensor_tensor(out=slot[:, :, :], in0=pos, scalar=1.0, in1=mask[:, :, :], op0=ALU.add, op1=ALU.mult))
                link(dve.tensor_scalar(slot[:, :, :], slot[:, :, :], -1.0, None, ALU.add))
                link(dve.tensor_copy(n_col[0:NE, :], bank[3][0:NE, 0:1]))
                dve.wait_ge(s_p8, NP8)
                link(dve.tensor_scalar(over[0:NE, :], thr[0:NE, :], n_col[0:NE, :], None, ALU.is_lt))
                dve.nop().then_inc(s_lt, 1)
                dve.wait_ge(s_cnt, 2)
                link(dve.tensor_copy(before[0:NE, :], bank[4][0:NE, 0:MAXC - 1]))
                link(dve.tensor_copy(cum[0:NE, :], bank[4][0:NE, MAXC - 1:2 * (MAXC - 1)]))
                for c in range(1, MAXC - 1):
                    link(dve.tensor_tensor(cum[0:NE, c:c + 1], cum[0:NE, c:c + 1], cum[0:NE, c - 1:c], ALU.add))
                link(dve.tensor_scalar(pos_i[0:NE, :], before[0:NE, :], float(NE + 1), None, ALU.add))
                link(dve.tensor_tensor(pos_i[0:NE, 1:MAXC - 1], pos_i[0:NE, 1:MAXC - 1], cum[0:NE, 0:MAXC - 2], ALU.add))
                link(dve.tensor_tensor(pos_i[0:NE, :], pos_i[0:NE, :], over[0:NE, :], ALU.mult))
                link(dve.tensor_scalar(pos_i[0:NE, :], pos_i[0:NE, :], -1.0, None, ALU.add))
                for c in range(MAXC - 1):
                    link(dve.tensor_scalar(hot[0:NE, c, :], iota[0:NE, 0:TAB], pos_i[0:NE, c:c + 1], None, ALU.is_equal))
                dve.nop().then_inc(s_lt, 1)
                dve.wait_ge(s_tabp, 1)
                link(dve.tensor_copy(row_f[0:1, NE:TAB], bank[5][0:1, NE:TAB]))
                link(dve.tensor_copy(row_f[0:1, 0:NE], iota[0:1, 0:NE]))
                link(dve.tensor_copy(row_f[0:1, TAB:2 * TAB], bank[5][0:1, TAB:2 * TAB]))
                link(dve.tensor_scalar(row_f[0:1, 2 * TAB:2 * TAB + 1], cum[0:1, MAXC - 2:MAXC - 1], float(NE), None, ALU.add))
                link(dve.tensor_copy(table[:, :], row_f[0:1, :]))
                for n in range(NT):
                    for half in range(2):
                        dve.wait_ge(s_bd, 2 * n + half + 1)
                        part = x2_all[:, n, half * 512:half * 512 + 512]
                        dve.tensor_tensor(part, part, bank[half][:, :], ALU.add).then_inc(s_base, 1)

            @block.tensor
            def _(pe):
                pe.wait_ge(s_bgl, 16)
                for n in range(4):
                    mm = pe.transpose(bank[6][:, n * P:(n + 1) * P], bgu_rows[:, n, :], ident[:, :])
                mm.then_inc(s_bgt, 1)
                pe.wait_ge(s_p8, NP8)
                pe.wait_ge(s_lt, 1)
                for n in range(NT):
                    mm = pe.transpose(bank[n // 4][0:NE, (n % 4) * P:(n % 4 + 1) * P], gate[:, n, :], ident[:, :])
                    if n % 4 == 3:
                        mm.then_inc(s_t8, 1)
                for n in range(NT):
                    pe.matmul(bank[2][:, n * NE:(n + 1) * NE], lt, mask[:, n, :], start=True, stop=(n == 0))
                    for m in range(n):
                        pe.matmul(bank[2][:, n * NE:(n + 1) * NE], ones[:, :], mask[:, m, :], start=False, stop=(m == n - 1))
                for n in range(NT):
                    mm = pe.matmul(bank[3][0:NE, 0:1], mask[:, n, :], ones[:, 0:1], start=(n == 0), stop=(n == NT - 1))
                mm.then_inc(s_cnt, 1)
                pe.wait_ge(s_lt, 2)
                pe.matmul(bank[4][0:NE, 0:MAXC - 1], lt[0:NE, 0:NE], over[0:NE, :], start=True, stop=True)
                pe.matmul(bank[4][0:NE, MAXC - 1:2 * (MAXC - 1)], ones[0:NE, 0:NE], over[0:NE, :], start=True, stop=True).then_inc(s_cnt, 1)
                pe.wait_ge(s_lt, 3)
                for c in range(MAXC - 1):
                    pe.matmul(bank[5][0:1, 0:TAB], code_e[0:NE, :], hot[0:NE, c, :], start=(c == 0), stop=(c == MAXC - 2))
                for c in range(MAXC - 1):
                    mm = pe.matmul(bank[5][0:1, TAB:2 * TAB], code_c[0:NE, c:c + 1], hot[0:NE, c, :], start=(c == 0), stop=(c == MAXC - 2))
                mm.then_inc(s_tabp, 1)
                pe.wait_ge(s_gTc, 2)
                for n in range(NT):
                    for half in range(2):
                        if n:
                            pe.wait_ge(s_base, 2 * n + half - 1)
                        pe.matmul(bank[half][:, :], gT[0:NE, n * P:(n + 1) * P], b_dn[0:NE, half * 512:(half + 1) * 512],
                                  start=True, stop=True).then_inc(s_bd, 1)
        if dbg is not None and dbg[0] == 8:
            s_dbg = sem("dbg")
            with nc.Block() as block:
                @block.sync
                def _(sp):
                    sp.dma_start(dbg[1][:, 0:8192], region_b[:, 0:8192]).then_inc(s_dbg, 16)
                    sp.dma_start(dbg[1][:, 8192:8192 + 256], gate[:, :, :].rearrange("p n e -> p (n e)")).then_inc(s_dbg, 16)
                    sp.dma_start(dbg[1][:, 8448:8448 + 256], slot[:, :, :].rearrange("p n e -> p (n e)")).then_inc(s_dbg, 16)
                    sp.dma_start(dbg[1][0:1, 8704:8704 + 2 * TAB + 2], table[:, :].bitcast(F32)).then_inc(s_dbg, 16)
                    sp.dma_start(out[0], x[0]).then_inc(s_dbg, 16)
                    sp.wait_ge(s_dbg, 80)
            return
        CH = 6
        GU = 4
        RING = 3
        DVE_K = 5
        CW = KT * 512
        raw = [region_b[:, r * CW:(r + 1) * CW].rearrange("p (k c) -> p k c", k=KT) for r in range(RING)]
        part_hi = [region_c[:, r * CW:r * CW + CW // 2].bitcast(FP16).rearrange("p (k c) -> p k c", k=KT) for r in range(RING)]
        part_lo = [region_c[:, r * CW + CW // 2:(r + 1) * CW].bitcast(FP16).rearrange("p (k c) -> p k c", k=KT) for r in range(RING)]
        xg = region_b[0:HS, RING * CW:RING * CW + 2 * D].rearrange("p (h d) -> p h d", h=2)
        yrow = region_b[0:HS, RING * CW + 2 * D:RING * CW + 4 * D].rearrange("p (h d) -> p h d", h=2)
        w9 = [0]

        def cut(n):
            w9[0] += n
            assert w9[0] <= 8192
            return region_a[:, w9[0] - n:w9[0]]

        xT_hi, xT_lo, aT_hi, aT_lo = (cut(KT * SL // 2).bitcast(FP16).rearrange("p (k t) -> p k t", k=KT) for _ in range(4))
        yT = cut(KT * SL).rearrange("p (k t) -> p k t", k=KT)
        pick = cut(NT * SL // 2).bitcast(BF16).rearrange("p (n t) -> p n t", n=NT)
        g_lin, u_lin, sig, g_act, act32 = ([cut(2 * SL) for _ in range(2)] for _ in range(5))
        b_cur = region_d[:, 0:2 * KT]
        trash = region_d[0:HS, 32:34]
        row_t, empty_t, g_t = region_d[0:HS, 34:36], region_d[0:HS, 36:38], region_d[0:HS, 38:40]
        sel_next = region_d[0:HS, 40:44]
        sel_cur = region_d[0:HS, 44:48]
        gate_prev = region_d[0:HS, 48:50]
        rows_prev = region_d[0:HS, 50:52].bitcast(I32)
        picked = region_d[0:HS, 54:66].rearrange("p (v h) -> p v h", v=6)
        carrier = region_d[0:HS, 66:68]
        rows_get = region_d[0:HS, 52:54].bitcast(I32)
        w_gu_v = w_gate_up[0].rearrange("e (k p) (g c) -> e p k g c", p=P, g=2)
        w_dn_v = w_down[0].rearrange("e (k p) c -> e p k c", p=P)

        s_raw = [sem(f"chunk_loaded{r}") for r in range(RING)]
        s_hi9, s_lod, s_lop = sem("part_hi_ready"), sem("part_lo_dve"), sem("part_lo_pool")
        s_gu, s_clamp, s_sig, s_act = sem("gu_ready"), sem("gu_clamped"), sem("sigmoid_ready"), sem("act_steps")
        s_dn, s_dnc, s_pi = sem("down_ready"), sem("down_copied"), sem("picked_copied")
        s_pick, s_idx, s_sel1, s_sel2, s_shift, s_bcur = sem("pick_ready"), sem("picked"), sem("rows_ready"), sem("sel_ready"), sem("sel_shifted"), sem("b_cur_ready")
        s_xg, s_xgT, s_xhi, s_xlo = sem("x_gathered"), sem("xg_turned"), sem("x_hi_ready"), sem("x_lo_ready")
        s_yT, s_yrow, s_scat, s_init, s_out = sem("y_turned"), sem("y_scaled"), sem("y_added"), sem("init9"), sem("out_stored")
        C1 = 1
        CGEV = 4
        CDN = 2
        CSC = 32

        def count_items(eng):
            return eng.value_load(table[0:1, 2 * TAB:2 * TAB + 1], min_val=NE, max_val=ITEMS)

        with nc.Block() as block:
            @block.sync
            def _(sp):
                def load(e, j):
                    r = j % RING
                    for g in range(2):
                        if j < GU:
                            src = w_gu_v[ds(e, 1), :, :, g, j * 256:j * 256 + 256].rearrange("a p k c -> p (a k) c")
                            dst = raw[r][:, :, g * 256:g * 256 + 256]
                        else:
                            src = w_dn_v[ds(e, 1), :, g * (KT // 2):(g + 1) * (KT // 2),
                                         (j - GU) * 512:(j - GU) * 512 + 512].rearrange("a p k c -> p (a k) c")
                            dst = raw[r][:, g * (KT // 2):(g + 1) * (KT // 2), :]
                        sp.dma_start(dst, src).then_inc(s_raw[r], 16)

                n_items = count_items(sp)
                for j in range(RING):
                    load(0, j)
                with sp.Fori(0, n_items) as i:
                    e = sp.value_load(table[0:1, ds(i, 1)], min_val=0, max_val=NE - 1)
                    e_next = sp.value_load(table[0:1, ds(i + 1, 1)], min_val=0, max_val=NE - 1)
                    for m in range(CH):
                        sp.wait_ge(s_lod, i * CH + (m + 1))
                        sp.wait_ge(s_lop, i * CH + (m + 1))
                        load(e if m < RING else e_next, (m + RING) % CH)
                sp.wait_ge(s_raw[2], n_items * 64 + 32)
                sp.wait_ge(s_scat, n_items * 32 + (CSC + 32))
                for q in range(4):
                    sp.dma_start(out[0, q * (T // 4):(q + 1) * (T // 4), :], rows_out[q * (T // 4):(q + 1) * (T // 4), :]).then_inc(s_out, 16)
                sp.wait_ge(s_out, 64)

            @block.gpsimd
            def _(pool):
                pool.memset(yT, 0.0).then_inc(s_init, 1)
                pool.memset(sel_cur[:, 0:2], 0.0).then_inc(s_init, 1)
                pool.iota(trash, [[HS, 2]], base=T, channel_multiplier=1, allow_small_or_imprecise_dtypes=True).then_inc(s_init, 1)
                pool.iota(sel_cur[:, 2:4], [[HS, 2]], base=T, channel_multiplier=1, allow_small_or_imprecise_dtypes=True).then_inc(s_init, 1)
                pool.memset(yrow, 0.0).then_inc(s_init, 1)
                pool.iota(rows_prev, [[HS, 2]], base=T, channel_multiplier=1).then_inc(s_init, 1)
                pool.wait_ge(s_init, 6)
                n_items = count_items(pool)

                def low_part(c, j):
                    r = j % RING
                    pool.wait_ge(s_hi9, c + 1)
                    pool.tensor_tensor(part_lo[r][:, DVE_K:, :], raw[r][:, DVE_K:, :], part_hi[r][:, DVE_K:, :],
                                       ALU.subtract).then_inc(s_lop, 1)

                def gather():
                    for h in range(2):
                        pool.indirect_dma_start(out=xg[:, h, :], out_offset=None, in_=rows_h2[:, :],
                                                in_offset=bass.IndirectOffsetOnAxis(ap=rows_get[:, h:h + 1], axis=0)).then_inc(s_xg, 16)

                def scatter(h):
                    pool.indirect_dma_start(out=rows_out[:, :], out_offset=bass.IndirectOffsetOnAxis(ap=rows_prev[:, h:h + 1], axis=0),
                                            in_=yrow[:, h, :], in_offset=None, compute_op=ALU.add).then_inc(s_scat, 16)

                scatter(0)
                low_part(0, 0)
                pool.wait_ge(s_sel1, 1)
                low_part(1, 1)
                gather()
                pool.wait_ge(s_scat, 16)
                scatter(1)
                with pool.Fori(0, n_items) as i:
                    low_part(i * CH + 2, 2)
                    pool.wait_ge(s_sel1, i + 2)
                    low_part(i * CH + 3, 0)
                    gather()
                    low_part(i * CH + 4, 1)
                    pool.wait_ge(s_yrow, i * 4 + (4 + C1))
                    low_part(i * CH + 5, 2)
                    scatter(0)
                    low_part(i * CH + 6, 0)
                    pool.wait_ge(s_scat, i * 32 + (CSC + 16))
                    low_part(i * CH + 7, 1)
                    scatter(1)
                pool.wait_ge(s_yrow, n_items * 4 + (4 + C1))
                pool.tensor_tensor(carrier[:, 0:1], trash[:, 0:1], trash[:, 0:1], ALU.add)
                scatter(0)
                pool.wait_ge(s_scat, n_items * 32 + (CSC + 16))
                pool.tensor_tensor(carrier[:, 1:2], trash[:, 0:1], trash[:, 0:1], ALU.add)
                scatter(1)

            @block.scalar
            def _(act):
                act.nop().then_inc(s_yrow, C1)
                act.nop().then_inc(s_dnc, CDN)
                n_items = count_items(act)

                def high_part(j, uses):
                    r = j % RING
                    act.wait_ge(s_raw[r], uses)
                    act.activation(part_hi[r], raw[r], ACT.Copy).then_inc(s_hi9, 1)

                def x_high(item, q):
                    act.wait_ge(s_xgT, item * 4 + (q + 1))
                    act.activation(xT_hi[:, 2 * q:2 * q + 2, :], bank[7 - q % 2][:, 0:2 * SL].rearrange("p (k t) -> p k t", k=2),
                                   ACT.Copy).then_inc(s_xhi, 1)

                def sigmoid(i, j):
                    act.wait_ge(s_clamp, i * 8 + (2 * j + 2 + CGEV))
                    act.activation(sig[j % 2], g_lin[j % 2], ACT.Sigmoid, scale=1.702).then_inc(s_sig, 1)

                def y_rows(i, g):
                    h, q = g // 2, g % 2
                    if g == 0:
                        act.wait_ge(s_shift, i * 2 + 1)
                        act.wait_ge(s_scat, i * 32 + CSC)
                    act.wait_ge(s_yT, i * 4 + (g + 1))
                    act.activation(yrow[:, h, q * 512:q * 512 + 512], bank[7 - g % 2][0:HS, :], ACT.Copy,
                                   scale=gate_prev[:, h:h + 1]).then_inc(s_yrow, 1)

                def y_copy(i, q):
                    act.wait_ge(s_dn, i * 4 + (q + 1 + C1))
                    act.activation(yT[:, 2 * q:2 * q + 2, :], bank[4 + q % 2][:, 0:2 * SL].rearrange("p (k t) -> p k t", k=2),
                                   ACT.Copy).then_inc(s_dnc, 1)

                high_part(0, 32)
                high_part(1, 32)
                for q in range(4):
                    x_high(0, q)
                with act.Fori(0, n_items) as i:
                    for j in range(CH):
                        if j == 0:
                            act.wait_ge(s_dn, i * 4 + C1)
                        elif j <= GU:
                            act.wait_ge(s_gu, i * 8 + 2 * j)
                        else:
                            act.wait_ge(s_dn, i * 4 + (2 + C1))
                        high_part(j + 2, i * 64 + 32 * ((j + 2) // RING + 1))
                        if j < GU:
                            sigmoid(i, j)
                        if j == 1 or j == 2:
                            y_rows(i, 2 * j - 2)
                            y_rows(i, 2 * j - 1)
                        if j >= GU:
                            y_copy(i, 2 * j - 8)
                            y_copy(i, 2 * j - 7)
                        if j == 3 or j == 4:
                            x_high(i + 1, 2 * j - 6)
                            x_high(i + 1, 2 * j - 5)
                for g in range(4):
                    y_rows(n_items, g)

            @block.vector
            def _(dve):
                dve.nop().then_inc(s_clamp, CGEV)
                n_items = count_items(dve)

                def choose(e, base):
                    at = iota[:, ds(base, SL)].unsqueeze(1).to_broadcast([P, NT, SL])
                    dve.tensor_tensor(pick, at, slot[:, :, ds(e, 1)].to_broadcast([P, NT, SL]), ALU.is_equal)
                    dve.tensor_copy(values[:, :, 3:6].unsqueeze(3), gate3[:, :, :, ds(e, 1)]).then_inc(s_pick, 1)

                def rows(item):
                    dve.wait_ge(s_idx, item + 1)
                    if not isinstance(item, int):
                        dve.wait_ge(s_xg, item * 32)
                    dve.tensor_copy(picked.rearrange("p v h -> p h v"), bank[6][0:HS, 0:12].rearrange("p (h v) -> p h v", h=2)).then_inc(s_pi, 1)
                    dve.wait_ge(s_pi, item + 1)
                    dve.tensor_tensor(row_t, picked[:, 0, :], picked[:, 1, :], ALU.add)
                    dve.scalar_tensor_tensor(out=empty_t, in0=picked[:, 2, :], scalar=1.0, in1=trash, op0=ALU.add, op1=ALU.mult)
                    dve.tensor_tensor(g_t, picked[:, 3, :], picked[:, 4, :], ALU.add)
                    dve.tensor_tensor(rows_get, picked[:, 0, :], picked[:, 1, :], ALU.add).then_inc(s_sel1, 1)
                    dve.wait_ge(s_sel1, item + 1)
                    if not isinstance(item, int):
                        dve.wait_ge(s_shift, item * 2)
                    dve.tensor_tensor(sel_next[:, 0:2], g_t, picked[:, 5, :], ALU.add)
                    dve.tensor_tensor(sel_next[:, 2:4], row_t, empty_t, ALU.add).then_inc(s_sel2, 1)

                def shift(i):
                    dve.wait_ge(s_yrow, i * 4 + C1)
                    dve.wait_ge(s_scat, i * 32 + CSC)
                    dve.wait_ge(s_sel2, i + 1)
                    dve.tensor_copy(gate_prev, sel_cur[:, 0:2])
                    dve.tensor_copy(rows_prev, sel_cur[:, 2:4]).then_inc(s_shift, 1)
                    dve.wait_ge(s_shift, i * 2 + 1)
                    dve.tensor_copy(sel_cur, sel_next).then_inc(s_shift, 1)

                def bias(e):
                    dve.tensor_copy(b_cur[:, 0:KT], b_gu[:, ds(e * (2 * KT), KT)])
                    dve.tensor_scalar(b_cur[:, KT:2 * KT], b_gu[:, ds(e * (2 * KT) + KT, KT)], 1.0, None, ALU.add).then_inc(s_bcur, 1)

                def low_part(c, j):
                    r = j % RING
                    dve.wait_ge(s_hi9, c + 1)
                    dve.tensor_tensor(part_lo[r][:, 0:DVE_K, :], raw[r][:, 0:DVE_K, :], part_hi[r][:, 0:DVE_K, :],
                                      ALU.subtract).then_inc(s_lod, 1)

                def x_low(item, q):
                    dve.wait_ge(s_xhi, item * 4 + (q + 1))
                    dve.tensor_tensor(xT_lo[:, 2 * q:2 * q + 2, :], bank[7 - q % 2][:, 0:2 * SL].rearrange("p (k t) -> p k t", k=2),
                                      xT_hi[:, 2 * q:2 * q + 2, :], ALU.subtract).then_inc(s_xlo, 1)

                def activate(i, j):
                    o = j % 2
                    for x in range(2):
                        f = 2 * j + x
                        dve.wait_ge(s_gu, i * 8 + (f + 1))
                        dve.tensor_scalar(g_lin[o][:, x * SL:x * SL + SL], bank[f % 4][:, 0:SL], b_cur[:, f:f + 1], 7.0, ALU.add, ALU.min)
                        dve.tensor_scalar(u_lin[o][:, x * SL:x * SL + SL], bank[f % 4][:, SL:2 * SL], b_cur[:, KT + f:KT + f + 1], 8.0,
                                          ALU.add, ALU.min).then_inc(s_clamp, 1)
                    hi = aT_hi[:, 2 * j:2 * j + 2, :].rearrange("p k t -> p (k t)")
                    lo = aT_lo[:, 2 * j:2 * j + 2, :].rearrange("p k t -> p (k t)")
                    dve.wait_ge(s_sig, i * 4 + (j + 1))
                    dve.tensor_tensor(g_act[o], g_lin[o], sig[o], ALU.mult).then_inc(s_act, 1)
                    dve.wait_ge(s_act, i * 12 + (3 * j + 1))
                    dve.scalar_tensor_tensor(out=act32[o], in0=u_lin[o], scalar=-6.0, in1=g_act[o], op0=ALU.max, op1=ALU.mult)
                    dve.scalar_tensor_tensor(out=hi, in0=u_lin[o], scalar=-6.0, in1=g_act[o], op0=ALU.max, op1=ALU.mult).then_inc(s_act, 1)
                    dve.wait_ge(s_act, i * 12 + (3 * j + 2))
                    dve.tensor_tensor(lo, act32[o], hi, ALU.subtract).then_inc(s_act, 1)

                dve.wait_ge(s_init, 6)
                choose(0, 0)
                bias(0)
                rows(0)
                low_part(0, 0)
                low_part(1, 1)
                for q in range(4):
                    x_low(0, q)
                with dve.Fori(0, n_items) as i:
                    e_next = dve.value_load(table[0:1, ds(i + 1, 1)], min_val=0, max_val=NE - 1)
                    base_next = dve.value_load(table[0:1, ds(i + (TAB + 1), 1)], min_val=0, max_val=(MAXC - 1) * SL)
                    shift(i)
                    choose(e_next, base_next)
                    for j in range(CH):
                        low_part(i * CH + (j + 2), j + 2)
                        if j < GU:
                            if j == 0:
                                dve.wait_ge(s_bcur, i + 1)
                            activate(i, j)
                        if j == 0:
                            rows(i + 1)
                        if j == 3:
                            bias(e_next)
                        if j == 3 or j == 4:
                            x_low(i + 1, 2 * j - 6)
                            x_low(i + 1, 2 * j - 5)
                shift(n_items)

            @block.tensor
            def _(pe):
                pe.nop().then_inc(s_dn, C1)
                pe.wait_ge(s_init, 6)
                n_items = count_items(pe)

                def find(item):
                    pe.wait_ge(s_pick, item + 1)
                    for h in range(2):
                        for n in range(NT):
                            mm = pe.matmul(bank[6][0:HS, h * 6:h * 6 + 6], pick[:, n, h * HS:h * HS + HS], values[:, n, :],
                                           start=(n == 0), stop=(n == NT - 1))
                    mm.then_inc(s_idx, 1)

                def turn_x(item, q):
                    if q == 0:
                        pe.wait_ge(s_xg, item * 32 + 32)
                    if q >= 2:
                        pe.wait_ge(s_xlo, item * 4 + (q - 1))
                    for x in range(2):
                        for h in range(2):
                            at = (2 * q + x) * P
                            mm = pe.transpose(bank[7 - q % 2][:, x * SL + h * HS:x * SL + h * HS + HS], xg[:, h, at:at + P], ident[0:HS, 0:HS])
                    mm.then_inc(s_xgT, 1)

                def turn_y(i, g):
                    h, q = g // 2, g % 2
                    if g == 0:
                        pe.wait_ge(s_dnc, i * 4 + CDN)
                    for d in range(4):
                        mm = pe.transpose(bank[7 - g % 2][0:HS, d * P:d * P + P], yT[:, 4 * q + d, h * HS:h * HS + HS], ident[:, :])
                    mm.then_inc(s_yT, 1)

                def parts_ready(c):
                    pe.wait_ge(s_lod, c + 1)
                    pe.wait_ge(s_lop, c + 1)

                def product(out_ap, r, col, k, hi, lo):
                    wh, wl = part_hi[r][:, k, col * P:col * P + P], part_lo[r][:, k, col * P:col * P + P]
                    for s, (a, b) in enumerate(((wh, hi[:, k, :]), (wh, lo[:, k, :]), (wl, hi[:, k, :]))):
                        mm = pe.matmul(out_ap, a, b, start=(k == 0 and s == 0), stop=(k == KT - 1 and s == 2))
                    return mm

                def gate_up(i, j):
                    parts_ready(i * CH + j)
                    for x in range(2):
                        f = 2 * j + x
                        pe.wait_ge(s_clamp, i * 8 + (f + 1))
                        for g in range(2):
                            for k in range(KT):
                                if f == 0 and g == 0 and k % 2 == 0:
                                    pe.wait_ge(s_xlo, i * 4 + (k // 2 + 1))
                                mm = product(bank[f % 4][:, g * SL:g * SL + SL], j % RING, 2 * g + x, k, xT_hi, xT_lo)
                        mm.then_inc(s_gu, 1)

                def down(i, j):
                    parts_ready(i * CH + j)
                    for x in range(2):
                        q = 2 * (j - GU) + x
                        pe.wait_ge(s_dnc, i * 4 + (q + 1))
                        for y in range(2):
                            for k in range(KT):
                                if q == 0 and y == 0 and k % 2 == 0:
                                    pe.wait_ge(s_act, i * 12 + 3 * (k // 2 + 1))
                                mm = product(bank[4 + q % 2][:, y * SL:y * SL + SL], j % RING, 2 * x + y, k, aT_hi, aT_lo)
                        mm.then_inc(s_dn, 1)

                find(0)
                pe.wait_ge(s_pi, 1)
                for q in range(4):
                    turn_x(0, q)
                with pe.Fori(0, n_items) as i:
                    gate_up(i, 0)
                    find(i + 1)
                    gate_up(i, 1)
                    turn_y(i, 0)
                    pe.wait_ge(s_pi, i + 2)
                    turn_y(i, 1)
                    gate_up(i, 2)
                    for g in (2, 3):
                        pe.wait_ge(s_yrow, i * 4 + (g - 1 + C1))
                        turn_y(i, g)
                    gate_up(i, 3)
                    for q in (0, 1):
                        pe.wait_ge(s_yrow, i * 4 + (q + 3 + C1))
                        turn_x(i + 1, q)
                    down(i, 4)
                    for q in (2, 3):
                        turn_x(i + 1, q)
                    down(i, 5)
                pe.wait_ge(s_xlo, n_items * 4 + 4)
                for g in range(4):
                    if g >= 2:
                        pe.wait_ge(s_yrow, n_items * 4 + (g - 1 + C1))
                    turn_y(n_items, g)

NAMES = ["x", "norm1_g", "w_in", "sb_q_norm_g", "sb_k_norm_g", "sb_out_norm_g", "hg_lb_logits", "hg_out_norm_g",
         "w_out", "norm2_g", "w_router", "b_router", "w_gate_up", "b_gate_up", "w_down", "b_down"]


def kernel(**inputs):
    import numpy as np
    import concourse.bacc as bacc
    from concourse.bass_utils import run_bass_kernel_spmd

    nc = bacc.Bacc("TRN2", target_bir_lowering=False, num_devices=1)
    arrays, args = {}, []
    for name in NAMES:
        a = np.ascontiguousarray(inputs[name])
        arrays[name + "_dram"] = a
        args.append(nc.dram_tensor(name + "_dram", a.shape, mybir.dt.from_np(a.dtype), kind="ExternalInput").ap())
    out = nc.dram_tensor("out_dram", inputs["x"].shape, F32, kind="ExternalOutput").ap()
    build_trunk(nc, *args, out)
    r = run_bass_kernel_spmd(nc, [arrays], core_ids=[0])
    return r.results[0]["out_dram"]
```

```python
from contextlib import ExitStack

import concourse.bass as bass
from concourse import mybir

F32 = mybir.dt.float32
BF16 = mybir.dt.bfloat16
FP16 = mybir.dt.float16
I32 = mybir.dt.int32
ALU = mybir.AluOpType
ACT = mybir.ActivationFunctionType
AX_X = mybir.AxisListType.X
ds = bass.ds

P = 128
FREE = 1


def build_trunk(nc, x, norm1_g, w_in, sb_q_norm_g, sb_k_norm_g, sb_out_norm_g, hg_lb_logits,
                hg_out_norm_g, w_out, norm2_g, w_router, b_router, w_gate_up, b_gate_up,
                w_down, b_down, out, dbg=None):
    T, D = x.shape[1], x.shape[2]
    KT = D // P
    NT = T // P
    SBW = sb_out_norm_g.shape[1]
    HGW = hg_out_norm_g.shape[1]
    DH = sb_q_norm_g.shape[1]
    HT = SBW // P
    NH = HGW // P
    RB = 32
    NB = P // RB
    EPS = 1e-6
    WC = 256
    with ExitStack() as ctx:
        def sb(name, shape, dt):
            return ctx.enter_context(nc.sbuf_tensor(name, shape, dt))

        def ps(name, shape, dt):
            return ctx.enter_context(nc.psum_tensor(name, shape, dt))

        def sem(name):
            return ctx.enter_context(nc.semaphore(name))

        region_a = sb("region_a", [P, 2 * KT * T // 2], F32)
        region_b = sb("region_b", [P, 16 * T], F32)
        region_c = sb("region_c", [P, NT * 3 * SBW], F32)
        region_d = sb("region_d", [P, 8192 + 2048], F32)

        hT_hi = region_a[:, 0:KT * T // 2].bitcast(FP16).rearrange("p (k t) -> p k t", k=KT)
        hT_lo = region_a[:, KT * T // 2:KT * T].bitcast(FP16).rearrange("p (k t) -> p k t", k=KT)
        x_all = region_b[:, 0:NT * D].rearrange("p (n d) -> p n d", n=NT)
        cm = region_b[:, :].rearrange("p (c t) -> p c t", c=16)
        tm = region_c[:, :].rearrange("p (n c) -> p n c", n=NT)

        ident = sb("ident", [P, P], F32)
        neg_tri = sb("neg_tri", [P, P], F32)
        neg_ones = sb("neg_ones", [P, P], F32)
        ones = sb("ones", [P, P], F32)
        head_ones = sb("head_ones", [P, P], F32)
        block_tri = sb("block_tri", [P, P], F32)
        keep = sb("keep", [P, P], F32)
        never = sb("never", [P, P], F32)
        eps = sb("eps", [P, 1], F32)
        g_q = sb("g_q", [P, 1], F32)
        g_k = sb("g_k", [P, 1], F32)
        g_mix = sb("g_mix", [P, 2 * HT], F32)
        sumsq = sb("sumsq", [P, 2 * NT], F32)
        rstd = sb("rstd", [P, 2 * NT], F32)

        bank = [ps(f"bank{i}", [P, 512], F32) for i in range(8)]

        g1_rows = region_d[:, 0:D]
        xn = [region_d[:, D:2 * D], region_d[:, 2 * D:3 * D]]
        sq_junk = region_d[:, 3 * D:4 * D]
        s_x, s_g1, s_small = sem("x_loaded"), sem("g1_loaded"), sem("gains_loaded")
        s_const, s_ss, s_rstd, s_xn = sem("const_ready"), sem("sumsq_ready"), sem("rstd_ready"), sem("xn_ready")
        s_xT, s_hhi, s_hlo = sem("xT_ready"), sem("h_hi_ready"), sem("h_lo_ready")
        with nc.Block() as block:
            @block.sync
            def _(sp):
                for n in range(4):
                    sp.dma_start(x_all[:, 2 * n:2 * n + 2, :],
                                 x[0, 2 * n * P:(2 * n + 2) * P, :].rearrange("(n p) d -> p n d", p=P)).then_inc(s_x, 16)
                sp.dma_start(g1_rows, norm1_g[0:1, :].partition_broadcast(P)).then_inc(s_g1, 16)
                for half in range(2):
                    sp.dma_start(g_q[64 * half:64 * half + 64, :], sb_q_norm_g[0, :].rearrange("(p a) -> p a", a=1)).then_inc(s_small, 16)
                    sp.dma_start(g_k[64 * half:64 * half + 64, :], sb_k_norm_g[0, :].rearrange("(p a) -> p a", a=1)).then_inc(s_small, 16)
                with nc.allow_non_contiguous_dma("gains, a few hundred words"):
                    sp.dma_start(g_mix[:, 0:HT], sb_out_norm_g[0, :].rearrange("(c p) -> p c", p=P)).then_inc(s_small, 16)
                    sp.dma_start(g_mix[:, HT:2 * HT], hg_out_norm_g[0, :].rearrange("(c p) -> p c", p=P)).then_inc(s_small, 16)
                sp.wait_ge(s_small, 96)

            @block.gpsimd
            def _(pool):
                pool.memset(ident[:, :], 0.0).then_inc(s_const, 1)
                pool.memset(neg_tri[:, :], -1.0).then_inc(s_const, 1)
                pool.memset(block_tri[:, :], 1.0).then_inc(s_const, 1)
                pool.memset(head_ones[:, :], 1.0).then_inc(s_const, 1)
                pool.memset(ones[:, :], 1.0).then_inc(s_const, 1)
                pool.memset(neg_ones[:, :], -1.0).then_inc(s_const, 1)
                pool.memset(eps[:, :], EPS).then_inc(s_const, 1)
                pool.memset(keep[:, :], 1.0).then_inc(s_const, 1)
                pool.memset(never[:, :], 0.0).then_inc(s_const, 1)
                pool.wait_ge(s_const, 9)
                pool.affine_select(out=never[:, :], in_=never[:, :], compare_op=ALU.is_gt, fill=-1.0e30, base=0,
                                   pattern=[[1, P]], channel_multiplier=-1).then_inc(s_const, 1)
                pool.affine_select(out=keep[:, :], in_=keep[:, :], compare_op=ALU.is_gt, fill=0.0, base=0,
                                   pattern=[[1, P]], channel_multiplier=-1).then_inc(s_const, 1)
                pool.affine_select(out=ident[:, :], in_=ident[:, :], compare_op=ALU.not_equal, fill=1.0, base=0,
                                   pattern=[[-1, P]], channel_multiplier=1).then_inc(s_const, 1)
                pool.affine_select(out=neg_tri[:, :], in_=neg_tri[:, :], compare_op=ALU.is_ge, fill=0.0, base=0,
                                   pattern=[[-1, P]], channel_multiplier=1).then_inc(s_const, 1)
                bt = block_tri[:, :].rearrange("p (c t) -> p c t", t=RB)
                ho = head_ones[:, :].rearrange("p (c t) -> p c t", t=DH)
                pool.affine_select(out=bt, in_=bt, compare_op=ALU.is_ge, fill=0.0, base=0,
                                   pattern=[[RB, NB], [1, RB]], channel_multiplier=-1).then_inc(s_const, 1)
                pool.affine_select(out=ho, in_=ho, compare_op=ALU.is_ge, fill=0.0, base=0,
                                   pattern=[[-DH, 2], [0, DH]], channel_multiplier=1).then_inc(s_const, 1)
                pool.wait_ge(s_const, 15)
                pool.affine_select(out=bt, in_=bt, compare_op=ALU.is_ge, fill=0.0, base=0,
                                   pattern=[[-RB, NB], [0, RB]], channel_multiplier=1).then_inc(s_const, 1)
                pool.affine_select(out=ho, in_=ho, compare_op=ALU.is_ge, fill=0.0, base=DH - 1,
                                   pattern=[[DH, 2], [0, DH]], channel_multiplier=-1).then_inc(s_const, 1)

            @block.scalar
            def _(act):
                act.preload_act_table_set("natural_log_exp_and_others")
                act.wait_ge(s_const, 9)
                act.wait_ge(s_x, 64)
                for n in range(NT):
                    if n >= 1:
                        act.wait_ge(s_ss, n)
                    act.activation(sq_junk, x_all[:, n, :], ACT.Square,
                                   accum_out=sumsq[:, n:n + 1]).then_inc(s_ss, 1)
                act.wait_ge(s_ss, NT)
                act.activation(rstd[:, 0:NT], sumsq[:, 0:NT], ACT.Ln, bias=eps[:, :], scale=1.0 / D).then_inc(s_rstd, 1)
                act.wait_ge(s_rstd, 1)
                act.activation(rstd[:, 0:NT], rstd[:, 0:NT], ACT.Exp, scale=-0.5).then_inc(s_rstd, 1)
                with act.Fori(0, NT) as n:
                    for half in range(2):
                        act.wait_ge(s_xT, 2 * n + half + 1 + FREE)
                        act.activation(hT_hi[:, 4 * half:4 * half + 4, ds(n * P, P)],
                                       bank[half][:, :].rearrange("p (k t) -> p k t", k=4), ACT.Copy).then_inc(s_hhi, 1)

            @block.vector
            def _(dve):
                for used in (s_hlo,):
                    dve.nop().then_inc(used, FREE)
                dve.wait_ge(s_rstd, 2)
                dve.wait_ge(s_g1, 16)

                def scaled_row(n, at):
                    dve.scalar_tensor_tensor(out=xn[at], in0=x_all[:, n, :] if isinstance(n, int) else x_all[:, ds(n, 1), :].rearrange("p a d -> p (a d)"),
                                             scalar=rstd[:, n:n + 1] if isinstance(n, int) else rstd[:, ds(n, 1)],
                                             in1=g1_rows, op0=ALU.mult, op1=ALU.mult).then_inc(s_xn, 1)

                with dve.Fori(0, NT // 2) as m:
                    for par in range(2):
                        n = m * 2 + par
                        dve.wait_ge(s_xT, 4 * m + 2 * par + FREE)
                        scaled_row(n, par)
                        for half in range(2):
                            dve.wait_ge(s_hhi, 4 * m + 2 * par + half + 1)
                            dve.tensor_tensor(hT_lo[:, 4 * half:4 * half + 4, ds(n * P, P)],
                                              bank[half][:, :].rearrange("p (k t) -> p k t", k=4),
                                              hT_hi[:, 4 * half:4 * half + 4, ds(n * P, P)], ALU.subtract).then_inc(s_hlo, 1)

            @block.tensor
            def _(pe):
                for used in (s_xT,):
                    pe.nop().then_inc(used, FREE)
                pe.wait_ge(s_const, 17)
                with pe.Fori(0, NT // 2) as m:
                    for par in range(2):
                        pe.wait_ge(s_xn, 2 * m + par + 1)
                        for half in range(2):
                            pe.wait_ge(s_hlo, 4 * m + 2 * par + FREE)
                            for k in range(4):
                                at = (4 * half + k) * P
                                mm = pe.transpose(bank[half][:, k * P:(k + 1) * P], xn[par][:, at:at + P], ident[:, :])
                            mm.then_inc(s_xT, 1)

        w_raw = [region_d[:, n * KT * WC:(n + 1) * KT * WC].rearrange("p (k c) -> p k c", k=KT) for n in range(2)]
        w_par = [region_d[:, 2 * KT * WC + n * KT * WC:2 * KT * WC + (n + 1) * KT * WC].bitcast(FP16)
                 .rearrange("p (s k c) -> p s k c", s=2, k=KT) for n in range(2)]
        s_w = [sem("w_in_loaded0"), sem("w_in_loaded1")]
        s_whi, s_wlo, s_piece, s_evac = sem("w_hi_ready"), sem("w_lo_ready"), sem("piece_ready"), sem("piece_copied")
        w_in_k = w_in[0].rearrange("(k p) c -> p k c", p=P)
        RUNS = [(0, 4, True, 0), (1024, 2, False, 0), (1536, 2, True, 8), (2048, 4, False, 512), (3072, 2, True, 12)]
        PC = 4

        def chunk_runs(eng):
            first = 0
            for c0, n, major, dst in RUNS:
                with eng.Fori(0, n // 2) as m:
                    for par in range(2):
                        yield m * 2 + (first + par), m + first // 2, m * 2 + par, par, c0, major, dst
                first += n

        with nc.Block() as block:
            @block.sync
            def _(sp):
                for at, uses, n, par, c0, major, dst in chunk_runs(sp):
                    sp.wait_ge(s_wlo, at + FREE)
                    sp.dma_start(w_raw[par], w_in_k[:, :, ds(n * WC + c0, WC)]).then_inc(s_w[par], 16)

            @block.scalar
            def _(act):
                for at, uses, n, par, c0, major, dst in chunk_runs(act):
                    act.wait_ge(s_w[par], uses * 16 + 16)
                    act.wait_ge(s_piece, at * PC + FREE)
                    act.activation(w_par[par][:, 0], w_raw[par], ACT.Copy).then_inc(s_whi, 1)

            @block.gpsimd
            def _(pool):
                for used in (s_wlo,):
                    pool.nop().then_inc(used, FREE)
                pool.nop().then_inc(s_wlo, 1)
                for at, uses, n, par, c0, major, dst in chunk_runs(pool):
                    pool.wait_ge(s_whi, at + 1)
                    pool.tensor_tensor(w_par[par][:, 1], w_raw[par], w_par[par][:, 0], ALU.subtract).then_inc(s_wlo, 1)

            @block.tensor
            def _(pe):
                for used in (s_piece,):
                    pe.nop().then_inc(used, FREE)
                pe.nop().then_inc(s_piece, PC)
                for at, uses, n, par, c0, major, dst in chunk_runs(pe):
                    pe.wait_ge(s_wlo, at + 2 + FREE)
                    for q in range(PC):
                        pe.wait_ge(s_evac, at * PC + q + FREE)
                        if major:
                            ct, half = q // 2, q % 2
                            for k in range(KT):
                                w = [w_par[par][:, s, k, ct * P:(ct + 1) * P] for s in range(2)]
                                h = [t[:, k, half * 512:(half + 1) * 512] for t in (hT_hi, hT_lo)]
                                for j, (a, b) in enumerate(((w[0], h[0]), (w[0], h[1]), (w[1], h[0]))):
                                    mm = pe.matmul(bank[q][:, :], a, b, start=(k == 0 and j == 0),
                                                   stop=(k == KT - 1 and j == 2))
                        else:
                            for tt in range(2):
                                for k in range(KT):
                                    t0 = (2 * q + tt) * P
                                    w = [w_par[par][:, s, k, :] for s in range(2)]
                                    h = [t[:, k, t0:t0 + P] for t in (hT_hi, hT_lo)]
                                    for j, (a, b) in enumerate(((h[0], w[0]), (h[0], w[1]), (h[1], w[0]))):
                                        mm = pe.matmul(bank[q][:, tt * WC:(tt + 1) * WC], a, b,
                                                       start=(k == 0 and j == 0), stop=(k == KT - 1 and j == 2))
                        mm.then_inc(s_piece, 1)

            @block.vector
            def _(dve):
                for used in (s_evac,):
                    dve.nop().then_inc(used, FREE)
                dve.nop().then_inc(s_evac, PC - 1)
                for at, uses, n, par, c0, major, dst in chunk_runs(dve):
                    for q in range(PC):
                        dve.wait_ge(s_piece, at * PC + (PC + q + 1) + FREE)
                        if major:
                            ct, half = q // 2, q % 2
                            dst_ap = cm[:, ds(n * 2 + (dst + ct), 1), half * 512:(half + 1) * 512].rearrange("p a t -> p (a t)")
                            dve.tensor_copy(dst_ap, bank[q][:, :]).then_inc(s_evac, 1)
                        else:
                            dve.tensor_copy(tm[:, 2 * q:2 * q + 2, ds(n * WC + dst, WC)],
                                            bank[q][:, :].rearrange("p (a c) -> p a c", a=2)).then_inc(s_evac, 1)
        if dbg is not None and dbg[0] == 2:
            s_dbg = sem("dbg")
            with nc.Block() as block:
                @block.sync
                def _(sp):
                    sp.dma_start(dbg[1][:, 0:16 * T], region_b[:, :]).then_inc(s_dbg, 16)
                    sp.dma_start(dbg[1][:, 16 * T:16 * T + NT * 3 * SBW], region_c[:, :]).then_inc(s_dbg, 16)
                    sp.dma_start(out[0], x[0]).then_inc(s_dbg, 16)
                    sp.wait_ge(s_dbg, 48)
            return

        def norm_buffers(base):
            sq = [region_d[:, base + n * 512:base + (n + 1) * 512] for n in range(2)]
            rs = [region_d[:, base + 1024 + n * 512:base + 1024 + (n + 1) * 512] for n in range(2)]
            return sq, rs

        gains = sb("gains", [P, 2 * HT], F32)
        s_gain = sem("gains_ready")
        s_sq, s_sumsq, s_ln, s_rs, s_nrm = sem("qk_sq"), sem("qk_sumsq"), sem("qk_ln"), sem("qk_rs"), sem("qk_normed")
        sq, rs = norm_buffers(0)
        with nc.Block() as block:
            @block.scalar
            def _(act):
                act.preload_act_table_set("natural_log_exp_and_others")
                for used in (s_ln,):
                    act.nop().then_inc(used, FREE)
                with act.Fori(0, 2 * HT) as c:
                    for half in range(2):
                        part = cm[:, ds(c, 1), half * 512:half * 512 + 512].rearrange("p a t -> p (a t)")
                        act.wait_ge(s_sumsq, c * 2 + FREE)
                        act.activation(sq[half], part, ACT.Square).then_inc(s_sq, 1)
                    for half in range(2):
                        act.wait_ge(s_sumsq, c * 2 + (half + 1) + FREE)
                        act.wait_ge(s_nrm, c * 2 + FREE)
                        act.activation(rs[half], bank[half][:, :], ACT.Ln, bias=eps[:, :], scale=1.0 / DH).then_inc(s_ln, 1)
                        act.wait_ge(s_ln, c * 2 + (half + 1) + FREE)
                        act.activation(rs[half], rs[half], ACT.Exp, scale=-0.5).then_inc(s_rs, 1)

            @block.tensor
            def _(pe):
                for used in (s_sumsq,):
                    pe.nop().then_inc(used, FREE)
                with pe.Fori(0, 2 * HT) as c:
                    for half in range(2):
                        pe.wait_ge(s_sq, c * 2 + (half + 1))
                        pe.wait_ge(s_ln, c * 2 + FREE)
                        pe.matmul(bank[half][:, :], head_ones[:, :], sq[half], start=True, stop=True).then_inc(s_sumsq, 1)

            @block.vector
            def _(dve):
                for used in (s_nrm,):
                    dve.nop().then_inc(used, FREE)
                dve.tensor_scalar(gains[:, 0:HT], ones[:, 0:HT], g_q[:, 0:1], DH ** -0.5, ALU.mult, ALU.mult).then_inc(s_gain, 1)
                dve.tensor_scalar(gains[:, HT:2 * HT], ones[:, 0:HT], g_k[:, 0:1], None, ALU.mult).then_inc(s_gain, 1)
                dve.wait_ge(s_gain, 2)
                with dve.Fori(0, 2 * HT) as c:
                    for half in range(2):
                        part = cm[:, ds(c, 1), half * 512:half * 512 + 512].rearrange("p a t -> p (a t)")
                        dve.wait_ge(s_rs, c * 2 + (half + 1))
                        dve.scalar_tensor_tensor(out=part, in0=part, scalar=gains[:, ds(c, 1)], in1=rs[half],
                                                 op0=ALU.mult, op1=ALU.mult).then_inc(s_nrm, 1)

        q_cur, k_cur = region_d[:, 0:T], region_d[:, T:2 * T]
        zc = [region_d[:, 2048 + n * 512:2560 + n * 512] for n in range(2)]
        lg = [region_d[:, 3072 + n * 512:3584 + n * 512] for n in range(2)]
        spl = [region_d[:, 4096 + n * 512:4608 + n * 512] for n in range(3)]
        wt = [region_d[:, 5632 + n * 512:6144 + n * 512] for n in range(2)]
        carry = [[region_d[:, 6656 + (2 * h + n) * 512:7168 + (2 * h + n) * 512] for n in range(2)] for h in range(2)]
        a_tm = [region_d[:, 8704 + n * 512:9216 + n * 512] for n in range(2)]
        SP_MAX = 40.0
        GB = 4
        steps = [(g, s, h) for g in range(NT // GB) for s in range(GB * (g + 1) - 1, -1, -1) for h in range(2)]
        NS = len(steps)
        diag = [s >= GB * g for g, s, h in steps]
        col = [max(0, s - GB * g) * P for g, s, h in steps]
        n_diag = [sum(diag[:n + 1]) for n in range(NS)]
        adds = [s > 0 for g, s, h in steps]
        n_adds = [sum(adds[:n + 1]) for n in range(NS)]
        ND, NA = n_diag[-1], n_adds[-1]
        turn = []
        seen = {}
        for g, s, h in steps:
            turn.append(seen.get((g, h), 0) % 2)
            seen[(g, h)] = seen.get((g, h), 0) + 1
        LAG_T, LAG_V = 2, 3
        zb, ab_bank, tb = bank[0:4], bank[4:6], bank[6]
        s_pair, s_z, s_cap, s_e, s_l = sem("pair_copied"), sem("z_ready"), sem("capped_ready"), sem("e_ready"), sem("log_ready")
        s_sp, s_spm, s_add, s_tri = sem("sp_ready"), sem("sp_masked"), sem("carry_ready"), sem("exponent_ready")
        s_wx, _, s_pv, s_asb, s_aT, s_acp = sem("w_ready"), None, sem("pv_done"), sem("a_rows_ready"), sem("aT_ready"), sem("aT_copied")
        with nc.Block() as block:
            @block.gpsimd
            def _(pool):
                with pool.Fori(0, HT) as c:
                    pool.wait_ge(s_z, c * NS + FREE)
                    pool.tensor_copy(q_cur, cm[:, ds(c, 1), :].rearrange("p a t -> p (a t)")).then_inc(s_pair, 1)
                    pool.tensor_copy(k_cur, cm[:, ds(c + HT, 1), :].rearrange("p a t -> p (a t)")).then_inc(s_pair, 1)

                    for n, (g, s, h) in enumerate(steps):
                        c0, size = col[n], GB * P - col[n]
                        pool.wait_ge(s_sp, c * NS + (n + 1))
                        if diag[n]:
                            pool.tensor_tensor(spl[n % 3][:, 0:P], spl[n % 3][:, 0:P], keep[:, :], ALU.mult).then_inc(s_spm, 1)
                            pool.wait_ge(s_spm, c * ND + n_diag[n])
                        if adds[n]:
                            if n >= 4:
                                pool.wait_ge(s_tri, c * NS + (n - 3))
                            new, old = carry[h][turn[n]], carry[h][1 - turn[n]]
                            if n >= 2 and adds[n - 2]:
                                pool.wait_ge(s_add, c * NA + n_adds[n - 2])
                            first = s == GB * (g + 1) - 1
                            edge = c0 + P if diag[n] else c0
                            if diag[n]:
                                cp = pool.tensor_tensor(new[:, c0:edge], spl[n % 3][:, 0:P], keep[:, :], ALU.mult)
                            if not first:
                                cp = pool.tensor_tensor(new[:, edge:512], old[:, edge:512], spl[n % 3][:, edge - c0:size], ALU.add)
                            cp.then_inc(s_add, 1)

            @block.vector
            def _(dve):
                for used in (s_acp,):
                    dve.nop().then_inc(used, FREE)
                with dve.Fori(0, HT) as c:
                    def capped(n):
                        size = GB * P - col[n]
                        dve.wait_ge(s_z, c * NS + (n + 1) + FREE)
                        if n >= 2:
                            dve.wait_ge(s_e, c * NS + (n - 1))
                        dve.tensor_scalar(zc[n % 2][:, 0:size], zb[n % 4][:, 0:size], SP_MAX, None, ALU.min).then_inc(s_cap, 1)

                    capped(0)
                    for n, (g, s, h) in enumerate(steps):
                        size = GB * P - col[n]
                        if n + 1 < NS:
                            capped(n + 1)
                        dve.wait_ge(s_l, c * NS + (n + 1))
                        if n >= 3:
                            dve.wait_ge(s_tri, c * NS + (n - 2))
                            if n_adds[n - 3]:
                                dve.wait_ge(s_add, c * NA + n_adds[n - 3])
                        dve.tensor_tensor(spl[n % 3][:, 0:size], zb[n % 4][:, 0:size], lg[n % 2][:, 0:size],
                                          ALU.max).then_inc(s_sp, 1)
                    for g in range(2):
                        dve.wait_ge(s_aT, c * 2 + (g + 1) + FREE)
                        dve.tensor_copy(cm[:, ds(c, 1), g * 512:g * 512 + 512].rearrange("p a t -> p (a t)"),
                                        tb[:, :]).then_inc(s_acp, 1)

            @block.scalar
            def _(act):
                act.preload_act_table_set("natural_log_exp_and_others")
                for used in (s_wx, s_asb,):
                    act.nop().then_inc(used, FREE)
                with act.Fori(0, HT) as c:
                    def weight(n):
                        size = GB * P - col[n]
                        act.wait_ge(s_tri, c * NS + (n + 1))
                        if n >= 2:
                            act.wait_ge(s_pv, c * NS + (n - 1))
                        act.activation(wt[n % 2][:, 0:size], zb[n % 4][:, 0:size], ACT.Exp).then_inc(s_wx, 1)

                    for n, (g, s, h) in enumerate(steps):
                        size = GB * P - col[n]
                        act.wait_ge(s_cap, c * NS + (n + 1))
                        if n >= 2:
                            act.wait_ge(s_sp, c * NS + (n - 1))
                        act.activation(lg[n % 2][:, 0:size], zc[n % 2][:, 0:size], ACT.Exp).then_inc(s_e, 1)
                        act.wait_ge(s_e, c * NS + (n + 1))
                        act.activation(lg[n % 2][:, 0:size], lg[n % 2][:, 0:size], ACT.Ln, bias=ones[:, 0:1]).then_inc(s_l, 1)
                        if n >= 2:
                            weight(n - 2)
                    weight(NS - 2)
                    weight(NS - 1)
                    for g in range(2):
                        last = max(n for n in range(NS) if steps[n][0] == g)
                        act.wait_ge(s_pv, c * NS + (last + 1))
                        act.wait_ge(s_aT, c * 2 + FREE)
                        act.activation(a_tm[g], ab_bank[g][:, :], ACT.Copy).then_inc(s_asb, 1)

            @block.tensor
            def _(pe):
                for used in (s_z, s_aT,):
                    pe.nop().then_inc(used, FREE)
                with pe.Fori(0, HT) as c:
                    pe.wait_ge(s_pair, c * 2 + 2)
                    for n in range(NS + LAG_V):
                        if n < NS:
                            g, s, h = steps[n]
                            size, t0 = GB * P - col[n], g * GB * P + col[n]
                            if n >= 4:
                                pe.wait_ge(s_wx, c * NS + (n - 3) + FREE)
                            elif n == 0:
                                pe.wait_ge(s_wx, c * NS + FREE)
                            pe.matmul(zb[n % 4][:, 0:size], k_cur[64 * h:64 * h + 64, s * P:(s + 1) * P],
                                      q_cur[64 * h:64 * h + 64, t0:t0 + size], start=True, stop=True,
                                      skip_group_check=True).then_inc(s_z, 1)
                        m = n - LAG_T
                        if 0 <= m < NS:
                            g, s, h = steps[m]
                            size, c0 = GB * P - col[m], col[m]
                            if diag[m]:
                                pe.wait_ge(s_spm, c * ND + n_diag[m])
                            pe.wait_ge(s_sp, c * NS + (m + 1))
                            first = s == GB * (g + 1) - 1
                            mm = pe.matmul(zb[m % 4][:, 0:size], neg_tri[:, :], spl[m % 3][:, 0:size], start=False, stop=True,
                                           skip_group_check=True)
                            if not first:
                                pe.wait_ge(s_add, c * NA + n_adds[m - 2])
                                edge = c0 + P if diag[m] else c0
                                mm = pe.matmul(zb[m % 4][:, edge - c0:size], neg_ones[:, :], carry[h][turn[m - 2]][:, edge:512],
                                               start=False, stop=True, skip_group_check=True)
                            if diag[m]:
                                mm = pe.matmul(zb[m % 4][:, 0:P], ident[:, :], never[:, :], start=False, stop=True,
                                               skip_group_check=True)
                            mm.then_inc(s_tri, 1)
                        m = n - LAG_V
                        if 0 <= m < NS:
                            g, s, h = steps[m]
                            c0 = col[m]
                            pe.wait_ge(s_wx, c * NS + (m + 1) + FREE)
                            if m == 0:
                                pe.wait_ge(s_asb, c * 2 + FREE)
                            for b in range(c0 // P, GB):
                                mm = pe.matmul(ab_bank[g][:, b * P + 64 * h:b * P + 64 * h + 64],
                                               wt[m % 2][:, b * P - c0:b * P - c0 + P],
                                               tm[:, s, ds(c * P + 64 * h, 64)],
                                               start=(s == GB * (g + 1) - 1 and h == 0), stop=(s == 0), skip_group_check=True)
                            mm.then_inc(s_pv, 1)
                    for g in range(2):
                        pe.wait_ge(s_asb, c * 2 + (g + 1) + FREE)
                        pe.wait_ge(s_acp, c * 2 + g + FREE)
                        for b in range(GB):
                            mm = pe.transpose(tb[:, b * P:(b + 1) * P], a_tm[g][:, b * P:(b + 1) * P], ident[:, :])
                        mm.then_inc(s_aT, 1)
        if dbg is not None and dbg[0] == 4:
            s_dbg = sem("dbg")
            with nc.Block() as block:
                @block.sync
                def _(sp):
                    sp.dma_start(dbg[1][:, 0:16 * T], region_b[:, :]).then_inc(s_dbg, 16)
                    sp.dma_start(out[0], x[0]).then_inc(s_dbg, 16)
                    sp.wait_ge(s_dbg, 32)
            return
        W4 = NH * P

        def tmp(n, count=1):
            return region_d[:, n * 512:(n + count) * 512]

        lb_rows, oml_rows = tmp(0), tmp(1)
        fc, e_f, r_f, k_tm, log_f = tmp(2), tmp(3), tmp(4), tmp(5), tmp(6)
        i_cur, eb, enb, qe, ke, kd, kd_tm, att = (tmp(n) for n in range(7, 15))
        state = [tmp(15 + n) for n in range(4)]
        b_bank, kt_bank, att_bank, o_bank = bank[0:4]
        u_bank = bank[4:8]
        F_MIN = -80.0
        heads = lambda ap: ap.rearrange("p (h t) -> p h t", h=NH)
        blocks = lambda ap: ap.rearrange("p (g t) -> p g t", t=RB)
        s_lbl, s_lb = sem("lb_logits_loaded"), sem("lb_steps")
        s_fc, s_ef, s_fd, s_lf1, s_lf = sem("f_capped"), sem("f_exp"), sem("f_steps"), sem("log_f_input"), sem("log_f_ready")
        s_icur, s_b, s_kT, s_ebr, s_qk, s_kd = sem("i_copied"), sem("b_ready"), sem("kT_ready"), sem("exp_b_ready"), sem("qe_ke_ready"), sem("kd_ready")
        s_kdT, s_kdtm, s_att, s_attm, s_u = sem("kdT_ready"), sem("kd_rows_ready"), sem("att_ready"), sem("att_masked"), sem("u_ready")
        s_st, s_o, s_or = sem("state_ready"), sem("o_ready"), sem("o_copied")
        with nc.Block() as block:
            @block.sync
            def _(sp):
                sp.dma_start(tmp(2), hg_lb_logits[0:1, :].partition_broadcast(P)).then_inc(s_lbl, 16)
                sp.dma_start(tmp(3), hg_lb_logits[1:2, :].partition_broadcast(P)).then_inc(s_lbl, 16)

            @block.gpsimd
            def _(pool):
                for used in (s_lf1,):
                    pool.nop().then_inc(used, FREE)
                with pool.Fori(0, NT) as n:
                    pool.wait_ge(s_o, n + FREE)
                    pool.tensor_copy(i_cur, tm[:, ds(n, 1), 2 * SBW:3 * SBW].rearrange("p a c -> p (a c)")).then_inc(s_icur, 1)
                    pool.wait_ge(s_fd, n * 4 + 2)
                    pool.wait_ge(s_b, n + FREE)
                    pool.tensor_tensor(log_f, r_f, oml_rows, ALU.mult).then_inc(s_lf1, 1)
                    pool.wait_ge(s_lf1, n * 2 + 1 + FREE)
                    pool.tensor_tensor(log_f, log_f, lb_rows, ALU.add).then_inc(s_lf1, 1)

            @block.scalar
            def _(act):
                act.preload_act_table_set("natural_log_exp_and_others")
                for used in (s_ef, s_or,):
                    act.nop().then_inc(used, FREE)
                act.wait_ge(s_lb, 3)
                act.activation(tmp(2), tmp(2), ACT.Exp).then_inc(s_lb, 1)
                act.activation(tmp(3), tmp(3), ACT.Exp).then_inc(s_lb, 1)
                with act.Fori(0, NT) as n:
                    act.wait_ge(s_fc, n + 1)
                    act.activation(e_f, fc, ACT.Exp, scale=-1.0).then_inc(s_ef, 1)
                    act.wait_ge(s_lf1, n * 2 + 2 + FREE)
                    act.activation(log_f, log_f, ACT.Ln).then_inc(s_lf, 1)
                    act.wait_ge(s_b, n + 1 + FREE)
                    act.activation(eb, b_bank[:, :], ACT.Exp).then_inc(s_ebr, 1)
                    act.activation(enb, b_bank[:, :], ACT.Exp, scale=-1.0).then_inc(s_ebr, 1)
                    act.wait_ge(s_kdT, n + 1)
                    act.activation(kd_tm, kt_bank[:, :], ACT.Copy).then_inc(s_kdtm, 1)
                    act.wait_ge(s_o, n + 1 + FREE)
                    act.activation(cm[:, 2 * HT:2 * HT + NH, ds(n * P, P)], heads(o_bank[:, :]), ACT.Copy).then_inc(s_or, 1)

            @block.vector
            def _(dve):
                for used in (s_st,):
                    dve.nop().then_inc(used, FREE)
                dve.wait_ge(s_lbl, 32)
                dve.tensor_tensor(tmp(4), tmp(2), tmp(3), ALU.max).then_inc(s_lb, 1)
                dve.wait_ge(s_lb, 1)
                dve.tensor_tensor(tmp(2), tmp(2), tmp(4), ALU.subtract).then_inc(s_lb, 1)
                dve.tensor_tensor(tmp(3), tmp(3), tmp(4), ALU.subtract).then_inc(s_lb, 1)
                dve.wait_ge(s_lb, 5)
                dve.tensor_tensor(tmp(4), tmp(2), tmp(3), ALU.add).then_inc(s_lb, 1)
                dve.wait_ge(s_lb, 6)
                dve.reciprocal(tmp(4), tmp(4)).then_inc(s_lb, 1)
                dve.wait_ge(s_lb, 7)
                dve.tensor_tensor(lb_rows, tmp(2), tmp(4), ALU.mult).then_inc(s_lb, 1)
                dve.wait_ge(s_lb, 8)
                dve.tensor_scalar(oml_rows, lb_rows, -1.0, 1.0, ALU.mult, ALU.add).then_inc(s_lb, 1)
                dve.memset(state[0], 0.0).then_inc(s_lb, 1)
                dve.wait_ge(s_lb, 10)
                with dve.Fori(0, NT) as n:
                    dve.wait_ge(s_ef, n + FREE)
                    dve.tensor_scalar(fc, tm[:, ds(n, 1), SBW:2 * SBW].rearrange("p a c -> p (a c)"), F_MIN, None, ALU.max).then_inc(s_fc, 1)
                    dve.wait_ge(s_ef, n + 1 + FREE)
                    dve.wait_ge(s_lf1, n * 2 + FREE)
                    dve.tensor_scalar(r_f, e_f, 1.0, None, ALU.add).then_inc(s_fd, 1)
                    dve.wait_ge(s_fd, n * 4 + 1)
                    dve.reciprocal(r_f, r_f).then_inc(s_fd, 1)
                    dve.wait_ge(s_fd, n * 4 + 2)
                    dve.tensor_tensor(k_tm, e_f, r_f, ALU.mult).then_inc(s_fd, 1)
                    dve.wait_ge(s_fd, n * 4 + 3)
                    dve.tensor_tensor(k_tm, k_tm, oml_rows, ALU.mult).then_inc(s_fd, 1)
                    dve.wait_ge(s_ebr, n * 2 + 2)
                    dve.tensor_tensor(heads(qe), cm[:, 2 * HT:2 * HT + NH, ds(n * P, P)], heads(eb), ALU.mult).then_inc(s_qk, 1)
                    dve.wait_ge(s_kT, n + 1)
                    dve.tensor_tensor(ke, kt_bank[:, :], enb, ALU.mult).then_inc(s_qk, 1)
                    dve.wait_ge(s_qk, n * 2 + 2)
                    dve.tensor_tensor(blocks(kd), blocks(ke), blocks(eb)[:, :, RB - 1:RB].to_broadcast([P, NH * NB, RB]),
                                      ALU.mult).then_inc(s_kd, 1)
                    dve.wait_ge(s_att, n + 1)
                    dve.tensor_tensor(heads(att), heads(att_bank[:, :]), block_tri[:, :].unsqueeze(1).to_broadcast([P, NH, P]),
                                      ALU.mult).then_inc(s_attm, 1)
                    dve.wait_ge(s_u, n + 1)
                    for c in range(NB):
                        if c:
                            dve.wait_ge(s_st, n * (NB * NH) + c * NH + FREE)
                        if c == NB - 1:
                            dve.wait_ge(s_o, n + 1 + FREE)
                        for h in range(NH):
                            last = h * P + c * RB + RB - 1
                            dve.scalar_tensor_tensor(out=state[(c + 1) % NB][:, h * P:(h + 1) * P], in0=state[c][:, h * P:(h + 1) * P],
                                                     scalar=eb[:, last:last + 1], in1=u_bank[c][:, h * P:(h + 1) * P],
                                                     op0=ALU.mult, op1=ALU.add).then_inc(s_st, 1)

            @block.tensor
            def _(pe):
                for used in (s_o, s_b,):
                    pe.nop().then_inc(used, FREE)
                with pe.Fori(0, NT) as n:
                    pe.wait_ge(s_lf, n + 1)
                    for h in range(NH):
                        mm = pe.matmul(b_bank[:, h * P:(h + 1) * P], log_f[:, h * P:(h + 1) * P], block_tri[:, :], start=True, stop=True)
                    mm.then_inc(s_b, 1)
                    pe.wait_ge(s_fd, n * 4 + 4)
                    for h in range(NH):
                        mm = pe.transpose(kt_bank[:, h * P:(h + 1) * P], k_tm[:, h * P:(h + 1) * P], ident[:, :])
                    mm.then_inc(s_kT, 1)
                    pe.wait_ge(s_kd, n + 1)
                    for h in range(NH):
                        mm = pe.transpose(kt_bank[:, h * P:(h + 1) * P], kd[:, h * P:(h + 1) * P], ident[:, :])
                    mm.then_inc(s_kdT, 1)
                    for h in range(NH):
                        mm = pe.matmul(att_bank[:, h * P:(h + 1) * P], ke[:, h * P:(h + 1) * P], qe[:, h * P:(h + 1) * P], start=True, stop=True)
                    mm.then_inc(s_att, 1)
                    pe.wait_ge(s_kdtm, n + 1)
                    pe.wait_ge(s_icur, n + 1)
                    pe.wait_ge(s_st, n * (NB * NH) + FREE)
                    for c in range(NB):
                        rows = slice(c * RB, (c + 1) * RB)
                        for h in range(NH):
                            mm = pe.matmul(u_bank[c][:, h * P:(h + 1) * P], kd_tm[rows, h * P:(h + 1) * P], i_cur[rows, h * P:(h + 1) * P],
                                           start=True, stop=True)
                    mm.then_inc(s_u, 1)
                    pe.wait_ge(s_attm, n + 1)
                    pe.wait_ge(s_or, n + FREE)
                    for h in range(NH):
                        pe.matmul(o_bank[:, h * P:(h + 1) * P], i_cur[:, h * P:(h + 1) * P], att[:, h * P:(h + 1) * P],
                                  start=(h == 0), stop=False, skip_group_check=True)
                    for c in range(NB):
                        if c:
                            pe.wait_ge(s_st, n * (NB * NH) + c * NH + FREE)
                        for h in range(NH):
                            at = h * P + c * RB
                            mm = pe.matmul(o_bank[:, at:at + RB], state[c][:, h * P:(h + 1) * P], qe[:, at:at + RB],
                                           start=False, stop=True, skip_group_check=True)
                    mm.then_inc(s_o, 1)

        mix_hi, mix_lo = hT_hi, hT_lo
        sq, rs = norm_buffers(0)
        gate_t = [tmp(4), tmp(5)]
        mixed = [tmp(6), tmp(7)]
        wo_raw = region_c[:, 0:KT * D].rearrange("p (k c) -> p k c", k=KT)
        s_wo, s_mq, s_ms, s_mln, s_mrs = sem("w_out_loaded"), sem("mix_sq"), sem("mix_sumsq"), sem("mix_ln"), sem("mix_rs")
        s_gs_r = sem("gate_times_rs")
        s_gc, s_ge, s_gs, s_mx, s_mhi, s_mlo = sem("gate_capped"), sem("gate_exp"), sem("gate_steps"), sem("mix_ready"), sem("mix_hi_ready"), sem("mix_lo_ready")
        with nc.Block() as block:
            @block.sync
            def _(sp):
                sp.dma_start(wo_raw, w_out[0].rearrange("(k p) c -> p k c", p=P)).then_inc(s_wo, 16)

            def tiles(eng):
                for first, src in ((0, 0), (HT, 2 * HT)):
                    with eng.Fori(0, HT) as c:
                        yield c, c + first, src, first > 0

            @block.scalar
            def _(act):
                act.preload_act_table_set("natural_log_exp_and_others")
                for used in (s_mln,):
                    act.nop().then_inc(used, FREE)
                for c, k, src, rec in tiles(act):
                    for half in range(2):
                        part = cm[:, ds(c + src, 1), half * 512:half * 512 + 512].rearrange("p a t -> p (a t)")
                        act.wait_ge(s_ms, k * 2 + FREE)
                        act.activation(sq[half], part, ACT.Square).then_inc(s_mq, 1)
                    if rec:
                        for half in range(2):
                            act.wait_ge(s_gc, c * 2 + (half + 1))
                            act.activation(gate_t[half], gate_t[half], ACT.Exp, scale=-1.0).then_inc(s_ge, 1)
                    for half in range(2):
                        act.wait_ge(s_ms, k * 2 + (half + 1) + FREE)
                        act.wait_ge(s_mx, k * 2 + FREE)
                        act.activation(rs[half], bank[half][:, :], ACT.Ln, bias=eps[:, :], scale=1.0 / (P if rec else DH)).then_inc(s_mln, 1)
                        act.wait_ge(s_mln, k * 2 + (half + 1) + FREE)
                        act.activation(rs[half], rs[half], ACT.Exp, scale=-0.5).then_inc(s_mrs, 1)
                    for half in range(2):
                        act.wait_ge(s_mx, k * 2 + (half + 1) + FREE)
                        act.activation(mix_hi[:, ds(k, 1), half * 512:half * 512 + 512].rearrange("p a t -> p (a t)"), mixed[half],
                                       ACT.Copy).then_inc(s_mhi, 1)

            @block.tensor
            def _(pe):
                for used in (s_ms,):
                    pe.nop().then_inc(used, FREE)
                for c, k, src, rec in tiles(pe):
                    for half in range(2):
                        pe.wait_ge(s_mq, k * 2 + (half + 1))
                        pe.wait_ge(s_mln, k * 2 + FREE)
                        pe.matmul(bank[half][:, :], (ones if rec else head_ones)[:, :], sq[half], start=True, stop=True).then_inc(s_ms, 1)

            @block.vector
            def _(dve):
                for used in (s_mx, s_mlo,):
                    dve.nop().then_inc(used, FREE)
                for c, k, src, rec in tiles(dve):
                    if rec:
                        for half in range(2):
                            part = cm[:, ds(c + 3 * HT, 1), half * 512:half * 512 + 512].rearrange("p a t -> p (a t)")
                            dve.wait_ge(s_mx, k * 2 + FREE)
                            dve.tensor_scalar(gate_t[half], part, F_MIN, None, ALU.max).then_inc(s_gc, 1)
                        for half in range(2):
                            part = cm[:, ds(c + 3 * HT, 1), half * 512:half * 512 + 512].rearrange("p a t -> p (a t)")
                            dve.wait_ge(s_ge, c * 2 + (half + 1))
                            dve.tensor_scalar(gate_t[half], gate_t[half], 1.0, None, ALU.add).then_inc(s_gs, 1)
                            dve.wait_ge(s_gs, c * 6 + (3 * half + 1))
                            dve.reciprocal(gate_t[half], gate_t[half]).then_inc(s_gs, 1)
                            dve.wait_ge(s_gs, c * 6 + (3 * half + 2))
                            dve.tensor_tensor(gate_t[half], gate_t[half], part, ALU.mult).then_inc(s_gs, 1)
                    for half in range(2):
                        part = cm[:, ds(c + src, 1), half * 512:half * 512 + 512].rearrange("p a t -> p (a t)")
                        dve.wait_ge(s_mrs, k * 2 + (half + 1))
                        dve.wait_ge(s_mlo, k * 2 + FREE)
                        if rec:
                            dve.wait_ge(s_gs, c * 6 + (3 * half + 3))
                            dve.tensor_tensor(rs[half], rs[half], gate_t[half], ALU.mult).then_inc(s_gs_r, 1)
                            dve.wait_ge(s_gs_r, c * 2 + (half + 1))
                        dve.scalar_tensor_tensor(out=mixed[half], in0=part, scalar=g_mix[:, ds(k, 1)], in1=rs[half],
                                                 op0=ALU.mult, op1=ALU.mult).then_inc(s_mx, 1)
                    for half in range(2):
                        dve.wait_ge(s_mhi, k * 2 + (half + 1))
                        hi, lo = (t[:, ds(k, 1), half * 512:half * 512 + 512].rearrange("p a t -> p (a t)") for t in (mix_hi, mix_lo))
                        dve.tensor_tensor(lo, mixed[half], hi, ALU.subtract).then_inc(s_mlo, 1)
        if dbg is not None and dbg[0] == 6:
            s_dbg = sem("dbg")
            with nc.Block() as block:
                @block.sync
                def _(sp):
                    sp.dma_start(dbg[1][:, 0:16 * T], region_b[:, :]).then_inc(s_dbg, 16)
                    sp.dma_start(dbg[1][:, 16 * T:16 * T + KT * T], region_a[:, :]).then_inc(s_dbg, 16)
                    sp.dma_start(out[0], x[0]).then_inc(s_dbg, 16)
                    sp.wait_ge(s_dbg, 48)
            return
        NE = w_router.shape[2]
        TOPK = 4
        x2_all = region_b[:, 0:NT * D].rearrange("p (n d) -> p n d", n=NT)

        def unit(n):
            return region_b[:, NT * D + n * D:NT * D + (n + 1) * D]

        h2, h2T, g2_rows, junk2, gT, w_r, b_dn, h2_pair = (unit(n) for n in range(8))
        h2_pair = h2_pair.bitcast(FP16).rearrange("p (s d) -> p s d", s=2)
        w_r = w_r[:, 0:KT * NE].rearrange("p (k e) -> p k e", k=KT)
        wo_hi = region_d[:, 0:KT * D // 2].bitcast(FP16).rearrange("p (k c) -> p k c", k=KT)
        wo_lo = region_d[:, KT * D // 2:KT * D].bitcast(FP16).rearrange("p (k c) -> p k c", k=KT)
        SL = 160
        HS = SL // 2
        MAXC = -(-T // SL)
        ITEMS = NE + T * TOPK // SL
        TAB = ITEMS + 8
        rows_out = nc.dram_tensor("rows_out", (T + SL, D), F32, kind="Internal").ap()
        rows_h2 = nc.dram_tensor("rows_h2", (T, 2 * D), FP16, kind="Internal").ap()
        logit = sb("logit", [P, NT, NE + TOPK], F32)
        b_r = sb("b_r", [P, NE], F32)
        s_x2, s_w7, s_wohi, s_wolo = sem("x_reloaded"), sem("router_loaded"), sem("wo_hi_ready"), sem("wo_lo_ready")
        s_pr, s_x2r, s_sq2, s_l2, s_rs2, s_h2 = sem("mix_product"), sem("x2_ready"), sem("x2_sumsq"), sem("x2_ln"), sem("x2_rstd"), sem("h2_ready")
        s_h2phi, s_h2plo = sem("h2_hi_ready"), sem("h2_lo_ready")
        s_h2st, s_h2T, s_h2Tc, s_lgt, s_lgc, s_pad = sem("h2_stored"), sem("h2T_ready"), sem("h2T_copied"), sem("logits_ready"), sem("logits_copied"), sem("pad_ready")
        PAD = -3.0e38
        with nc.Block() as block:
            @block.sync
            def _(sp):
                for used in (s_h2st,):
                    sp.nop().then_inc(used, FREE)
                for n in range(4):
                    sp.dma_start(x2_all[:, 2 * n:2 * n + 2, :],
                                 x[0, 2 * n * P:(2 * n + 2) * P, :].rearrange("(n p) d -> p n d", p=P)).then_inc(s_x2, 16)
                sp.dma_start(g2_rows, norm2_g[0:1, :].partition_broadcast(P)).then_inc(s_w7, 16)
                sp.dma_start(w_r, w_router[0].rearrange("(k p) e -> p k e", p=P)).then_inc(s_w7, 16)
                sp.dma_start(b_r[:, :], b_router[0:1, :].partition_broadcast(P)).then_inc(s_w7, 16)
                sp.dma_start(b_dn[0:NE, :], b_down[0]).then_inc(s_w7, 16)
                with sp.Fori(0, NT) as n:
                    sp.wait_ge(s_h2plo, n + 1 + FREE)
                    sp.dma_start(rows_h2[ds(n * P, P), :], h2_pair.rearrange("p s d -> p (s d)")).then_inc(s_h2st, 16)
                sp.wait_ge(s_h2st, 16 * NT + FREE)
                sp.wait_ge(s_w7, 64)

            @block.gpsimd
            def _(pool):
                for used in (s_h2plo,):
                    pool.nop().then_inc(used, FREE)
                pool.memset(logit[:, :, :], PAD).then_inc(s_pad, 1)
                for k in range(KT):
                    pool.wait_ge(s_wohi, k + 1)
                    pool.tensor_tensor(wo_lo[:, k, :], wo_raw[:, k, :], wo_hi[:, k, :], ALU.subtract).then_inc(s_wolo, 1)
                with pool.Fori(0, NT) as n:
                    pool.wait_ge(s_h2phi, n + 1)
                    pool.tensor_tensor(h2_pair[:, 1, :], h2, h2_pair[:, 0, :], ALU.subtract).then_inc(s_h2plo, 1)

            @block.scalar
            def _(act):
                act.preload_act_table_set("natural_log_exp_and_others")
                for used in (s_h2Tc, s_lgc,):
                    act.nop().then_inc(used, FREE)
                act.wait_ge(s_wo, 16)
                for k in range(KT):
                    act.activation(wo_hi[:, k, :], wo_raw[:, k, :], ACT.Copy).then_inc(s_wohi, 1)
                act.wait_ge(s_pad, 1)
                with act.Fori(0, NT) as n:
                    act.wait_ge(s_x2r, n * 2 + 2 + FREE)
                    act.activation(junk2, x2_all[:, ds(n, 1), :].rearrange("p a d -> p (a d)"), ACT.Square,
                                   accum_out=sumsq[:, 0:1]).then_inc(s_sq2, 1)
                    act.wait_ge(s_sq2, n + 1)
                    act.activation(rstd[:, 0:1], sumsq[:, 0:1], ACT.Ln, bias=eps[:, :], scale=1.0 / D).then_inc(s_l2, 1)
                    act.wait_ge(s_l2, n + 1)
                    act.wait_ge(s_h2, n + FREE)
                    act.activation(rstd[:, 1:2], rstd[:, 0:1], ACT.Exp, scale=-0.5).then_inc(s_rs2, 1)
                    act.wait_ge(s_h2, n + 1 + FREE)
                    act.wait_ge(s_h2st, n * 16 + FREE)
                    act.activation(h2_pair[:, 0, :], h2, ACT.Copy).then_inc(s_h2phi, 1)
                    for half in range(2):
                        act.wait_ge(s_h2T, n * 2 + (half + 1) + FREE)
                        act.activation(h2T[:, half * 512:half * 512 + 512], bank[2 + half][:, :], ACT.Copy).then_inc(s_h2Tc, 1)
                    act.wait_ge(s_lgt, n + 1)
                    act.activation(logit[:, ds(n, 1), 0:NE].rearrange("p a e -> p (a e)"), bank[4][:, 0:NE], ACT.Copy).then_inc(s_lgc, 1)

            @block.vector
            def _(dve):
                for used in (s_h2, s_x2r,):
                    dve.nop().then_inc(used, FREE)
                dve.wait_ge(s_x2, 64)
                dve.wait_ge(s_w7, 64)
                with dve.Fori(0, NT) as n:
                    for half in range(2):
                        part = x2_all[:, ds(n, 1), half * 512:half * 512 + 512].rearrange("p a d -> p (a d)")
                        dve.wait_ge(s_pr, n * 2 + (half + 1))
                        dve.tensor_tensor(part, part, bank[half][:, :], ALU.add).then_inc(s_x2r, 1)
                    dve.wait_ge(s_rs2, n + 1)
                    dve.wait_ge(s_h2T, n * 2 + FREE)
                    dve.wait_ge(s_h2plo, n + FREE)
                    dve.scalar_tensor_tensor(out=h2, in0=x2_all[:, ds(n, 1), :].rearrange("p a d -> p (a d)"), scalar=rstd[:, 1:2],
                                             in1=g2_rows, op0=ALU.mult, op1=ALU.mult).then_inc(s_h2, 1)

            @block.tensor
            def _(pe):
                for used in (s_h2T,):
                    pe.nop().then_inc(used, FREE)
                def project(n, half):
                    pe.wait_ge(s_x2r, n * 2 + FREE)
                    for k in range(KT):
                        m = [t[:, k, ds(n * P, P)] for t in (mix_hi, mix_lo)]
                        w = [t[:, k, half * 512:half * 512 + 512] for t in (wo_hi, wo_lo)]
                        for j, (a, b) in enumerate(((m[0], w[0]), (m[0], w[1]), (m[1], w[0]))):
                            mm = pe.matmul(bank[half][:, :], a, b, start=(k == 0 and j == 0), stop=(k == KT - 1 and j == 2))
                    mm.then_inc(s_pr, 1)

                def turn_h2(n):
                    pe.wait_ge(s_h2, n + 1 + FREE)
                    pe.wait_ge(s_h2Tc, n * 2 + FREE)
                    for half in range(2):
                        for k in range(4):
                            mm = pe.transpose(bank[2 + half][:, k * P:(k + 1) * P], h2[:, (4 * half + k) * P:(4 * half + k + 1) * P], ident[:, :])
                        mm.then_inc(s_h2T, 1)

                def route(n):
                    pe.wait_ge(s_h2Tc, n * 2 + 2 + FREE)
                    pe.wait_ge(s_lgc, n + FREE)
                    for k in range(KT):
                        mm = pe.matmul(bank[4][:, 0:NE], h2T[:, k * P:(k + 1) * P], w_r[:, k, :], start=(k == 0), stop=(k == KT - 1))
                    mm.then_inc(s_lgt, 1)

                pe.wait_ge(s_wolo, KT)
                pe.wait_ge(s_w7, 64)
                project(0, 0)
                project(0, 1)
                with pe.Fori(0, NT - 1) as n:
                    project(n + 1, 0)
                    turn_h2(n)
                    project(n + 1, 1)
                    route(n)
                turn_h2(NT - 1)
                route(NT - 1)

        gate = sb("gate", [P, NT, NE], F32)
        mask = sb("mask", [P, NT, NE], F32)
        slot = sb("slot", [P, NT, NE], F32)
        gate3 = sb("gate3", [P, NT, 3, NE], BF16)
        b_gu = sb("b_gu", [P, NE * 2 * KT], F32)
        iota = sb("iota", [P, MAXC * SL], F32)
        values = sb("values", [P, NT, 6], BF16)
        table = sb("table", [1, 2 * TAB + 2], I32)
        spare = sb("spare", [P, HS], F32)
        work = region_c[:, :]
        w_off = [0]

        def take(n):
            w_off[0] += n
            return work[:, w_off[0] - n:w_off[0]]

        top = take(NT * 8).rearrange("p (n k) -> p n k", n=NT)
        rep = take(NT * (NE + TOPK)).rearrange("p (n e) -> p n e", n=NT)
        lg = take(NT * NE).rearrange("p (n e) -> p n e", n=NT)
        ssum, rsum = take(NT), take(NT)
        res = take(NT * NE).rearrange("p (n e) -> p n e", n=NT)
        lt = take(P)
        n_col, code_e = take(1), take(1)
        thr, over, before, cum, pos_i = take(MAXC - 1), take(MAXC - 1), take(MAXC - 1), take(MAXC - 1), take(MAXC - 1)
        hot = take((MAXC - 1) * TAB).rearrange("p (c j) -> p c j", c=MAXC - 1)
        code_c = take(MAXC - 1)
        row_f = take(2 * TAB + 2)
        val_f = take(NT * 2).rearrange("p (n v) -> p n v", n=NT)
        bgu_rows = take(4 * P).rearrange("p (n c) -> p n c", n=4)
        zeros = take(D)
        hot_slots = ITEMS
        s_p8 = sem("constants8_ready")
        s_lt, s_d8, s_a8, s_t8 = sem("table_inputs"), sem("routing_steps"), sem("routing_exp"), sem("gate_turned")
        s_gTc, s_bd, s_base, s_bst, s_cnt = sem("gateT_copied"), sem("bias_product"), sem("base_ready"), sem("base_stored"), sem("counts_ready")
        s_bgl, s_bgt, s_bgc, s_tabp, s_trash = sem("bgu_loaded"), sem("bgu_turned"), sem("bgu_copied"), sem("table_product"), sem("trash_cleared")
        NP8 = 12
        with nc.Block() as block:
            @block.sync
            def _(sp):
                sp.dma_start(bgu_rows, b_gate_up[0].rearrange("e (j c) -> (e j) c", c=P).rearrange("(n p) c -> p n c", p=P)).then_inc(s_bgl, 16)
                sp.wait_ge(s_p8, NP8)
                sp.dma_start(rows_out[T:T + P, :], zeros).then_inc(s_trash, 16)
                sp.dma_start(rows_out[T + P:T + SL, :], zeros[0:SL - P, :]).then_inc(s_trash, 16)
                for n in range(NT):
                    sp.wait_ge(s_base, 2 * n + 2)
                    sp.dma_start(rows_out[n * P:(n + 1) * P, :], x2_all[:, n, :]).then_inc(s_bst, 16)
                sp.wait_ge(s_bst, 16 * NT)
                sp.wait_ge(s_trash, 32)

            @block.gpsimd
            def _(pool):
                pool.memset(lt, 1.0).then_inc(s_p8, 1)
                pool.memset(zeros, 0.0).then_inc(s_p8, 1)
                pool.memset(values[:, :, 2:3], -1.0).then_inc(s_p8, 1)
                pool.memset(row_f, 0.0).then_inc(s_p8, 1)
                pool.iota(iota[:, :], [[1, MAXC * SL]], base=0, channel_multiplier=0, allow_small_or_imprecise_dtypes=True).then_inc(s_p8, 1)
                pool.iota(val_f[:, :, 0:1], [[P, NT]], base=0, channel_multiplier=0, allow_small_or_imprecise_dtypes=True).then_inc(s_p8, 1)
                pool.iota(val_f[:, :, 1:2], [[0, NT]], base=0, channel_multiplier=1, allow_small_or_imprecise_dtypes=True).then_inc(s_p8, 1)
                pool.iota(code_e, [[0, 1]], base=0, channel_multiplier=1, allow_small_or_imprecise_dtypes=True).then_inc(s_p8, 1)
                pool.iota(thr, [[SL, MAXC - 1]], base=SL, channel_multiplier=0, allow_small_or_imprecise_dtypes=True).then_inc(s_p8, 1)
                pool.wait_ge(s_p8, 9)
                pool.affine_select(out=lt, in_=lt, compare_op=ALU.is_gt, fill=0.0, base=0, pattern=[[1, P]],
                                   channel_multiplier=-1).then_inc(s_p8, 1)
                pool.tensor_copy(values[:, :, 0:2], val_f).then_inc(s_p8, 1)
                pool.tensor_copy(code_c, thr).then_inc(s_p8, 1)

            @block.scalar
            def _(act):
                act.preload_act_table_set("natural_log_exp_and_others")
                act.wait_ge(s_d8, 2 + NT + 1 + NT + 2)
                act.activation(lg, lg, ACT.Exp).then_inc(s_a8, 1)
                for b in range(2):
                    act.wait_ge(s_t8, b + 1)
                    act.activation(gT[0:NE, b * 512:(b + 1) * 512], bank[b][0:NE, :], ACT.Copy).then_inc(s_gTc, 1)
                act.wait_ge(s_bgt, 1)
                act.activation(b_gu[:, :], bank[6][:, :], ACT.Copy).then_inc(s_bgc, 1)

            @block.vector
            def _(dve):
                step = [0]

                def link(ins):
                    step[0] += 1
                    ins.then_inc(s_d8, 1)
                    dve.wait_ge(s_d8, step[0])

                link(dve.tensor_tensor(lg, logit[:, :, 0:NE], b_r[:, :].unsqueeze(1).to_broadcast([P, NT, NE]), ALU.add))
                link(dve.tensor_copy(logit[:, :, 0:NE], lg))
                for n in range(NT):
                    link(dve.max(out=top[:, n, :], in_=logit[:, n, :]))
                link(dve.tensor_tensor(lg, lg, top[:, :, 0:1].to_broadcast([P, NT, NE]), ALU.subtract))
                link(dve.memset(top[:, :, TOPK:8], PAD))
                for n in range(NT):
                    link(dve.match_replace(out=rep[:, n, :], in_to_replace=top[:, n, :], in_values=logit[:, n, :], imm_value=-PAD))
                link(dve.tensor_scalar(mask[:, :, :], rep[:, :, 0:NE], 1.0e38, None, ALU.is_ge))
                assert step[0] == 2 + NT + 1 + NT + 2
                dve.wait_ge(s_a8, 1)
                link(dve.tensor_tensor(lg, lg, mask[:, :, :], ALU.mult))
                link(dve.tensor_reduce(ssum, lg, AX_X, ALU.add))
                link(dve.reciprocal(rsum, ssum))
                link(dve.tensor_tensor(gate[:, :, :], lg, rsum.unsqueeze(2).to_broadcast([P, NT, NE]), ALU.mult))
                dve.nop().then_inc(s_lt, 1)
                link(dve.tensor_copy(gate3[:, :, 0, :], gate[:, :, :]))
                link(dve.tensor_tensor(res, gate[:, :, :], gate3[:, :, 0, :], ALU.subtract))
                link(dve.tensor_copy(gate3[:, :, 1, :], res))
                link(dve.tensor_tensor(res, res, gate3[:, :, 1, :], ALU.subtract))
                link(dve.tensor_copy(gate3[:, :, 2, :], res))
                dve.wait_ge(s_cnt, 1)
                pos = bank[2][:, 0:NT * NE].rearrange("p (n e) -> p n e", n=NT)
                link(dve.scalar_tensor_tensor(out=slot[:, :, :], in0=pos, scalar=1.0, in1=mask[:, :, :], op0=ALU.add, op1=ALU.mult))
                link(dve.tensor_scalar(slot[:, :, :], slot[:, :, :], -1.0, None, ALU.add))
                link(dve.tensor_copy(n_col[0:NE, :], bank[3][0:NE, 0:1]))
                dve.wait_ge(s_p8, NP8)
                link(dve.tensor_scalar(over[0:NE, :], thr[0:NE, :], n_col[0:NE, :], None, ALU.is_lt))
                dve.nop().then_inc(s_lt, 1)
                dve.wait_ge(s_cnt, 2)
                link(dve.tensor_copy(before[0:NE, :], bank[4][0:NE, 0:MAXC - 1]))
                link(dve.tensor_copy(cum[0:NE, :], bank[4][0:NE, MAXC - 1:2 * (MAXC - 1)]))
                for c in range(1, MAXC - 1):
                    link(dve.tensor_tensor(cum[0:NE, c:c + 1], cum[0:NE, c:c + 1], cum[0:NE, c - 1:c], ALU.add))
                link(dve.tensor_scalar(pos_i[0:NE, :], before[0:NE, :], float(NE + 1), None, ALU.add))
                link(dve.tensor_tensor(pos_i[0:NE, 1:MAXC - 1], pos_i[0:NE, 1:MAXC - 1], cum[0:NE, 0:MAXC - 2], ALU.add))
                link(dve.tensor_tensor(pos_i[0:NE, :], pos_i[0:NE, :], over[0:NE, :], ALU.mult))
                link(dve.tensor_scalar(pos_i[0:NE, :], pos_i[0:NE, :], -1.0, None, ALU.add))
                for c in range(MAXC - 1):
                    link(dve.tensor_scalar(hot[0:NE, c, :], iota[0:NE, 0:TAB], pos_i[0:NE, c:c + 1], None, ALU.is_equal))
                dve.nop().then_inc(s_lt, 1)
                dve.wait_ge(s_tabp, 1)
                link(dve.tensor_copy(row_f[0:1, NE:TAB], bank[5][0:1, NE:TAB]))
                link(dve.tensor_copy(row_f[0:1, 0:NE], iota[0:1, 0:NE]))
                link(dve.tensor_copy(row_f[0:1, TAB:2 * TAB], bank[5][0:1, TAB:2 * TAB]))
                link(dve.tensor_scalar(row_f[0:1, 2 * TAB:2 * TAB + 1], cum[0:1, MAXC - 2:MAXC - 1], float(NE), None, ALU.add))
                link(dve.tensor_copy(table[:, :], row_f[0:1, :]))
                for n in range(NT):
                    for half in range(2):
                        dve.wait_ge(s_bd, 2 * n + half + 1)
                        part = x2_all[:, n, half * 512:half * 512 + 512]
                        dve.tensor_tensor(part, part, bank[half][:, :], ALU.add).then_inc(s_base, 1)

            @block.tensor
            def _(pe):
                pe.wait_ge(s_bgl, 16)
                for n in range(4):
                    mm = pe.transpose(bank[6][:, n * P:(n + 1) * P], bgu_rows[:, n, :], ident[:, :])
                mm.then_inc(s_bgt, 1)
                pe.wait_ge(s_p8, NP8)
                pe.wait_ge(s_lt, 1)
                for n in range(NT):
                    mm = pe.transpose(bank[n // 4][0:NE, (n % 4) * P:(n % 4 + 1) * P], gate[:, n, :], ident[:, :])
                    if n % 4 == 3:
                        mm.then_inc(s_t8, 1)
                for n in range(NT):
                    pe.matmul(bank[2][:, n * NE:(n + 1) * NE], lt, mask[:, n, :], start=True, stop=(n == 0))
                    for m in range(n):
                        pe.matmul(bank[2][:, n * NE:(n + 1) * NE], ones[:, :], mask[:, m, :], start=False, stop=(m == n - 1))
                for n in range(NT):
                    mm = pe.matmul(bank[3][0:NE, 0:1], mask[:, n, :], ones[:, 0:1], start=(n == 0), stop=(n == NT - 1))
                mm.then_inc(s_cnt, 1)
                pe.wait_ge(s_lt, 2)
                pe.matmul(bank[4][0:NE, 0:MAXC - 1], lt[0:NE, 0:NE], over[0:NE, :], start=True, stop=True)
                pe.matmul(bank[4][0:NE, MAXC - 1:2 * (MAXC - 1)], ones[0:NE, 0:NE], over[0:NE, :], start=True, stop=True).then_inc(s_cnt, 1)
                pe.wait_ge(s_lt, 3)
                for c in range(MAXC - 1):
                    pe.matmul(bank[5][0:1, 0:TAB], code_e[0:NE, :], hot[0:NE, c, :], start=(c == 0), stop=(c == MAXC - 2))
                for c in range(MAXC - 1):
                    mm = pe.matmul(bank[5][0:1, TAB:2 * TAB], code_c[0:NE, c:c + 1], hot[0:NE, c, :], start=(c == 0), stop=(c == MAXC - 2))
                mm.then_inc(s_tabp, 1)
                pe.wait_ge(s_gTc, 2)
                for n in range(NT):
                    for half in range(2):
                        if n:
                            pe.wait_ge(s_base, 2 * n + half - 1)
                        pe.matmul(bank[half][:, :], gT[0:NE, n * P:(n + 1) * P], b_dn[0:NE, half * 512:(half + 1) * 512],
                                  start=True, stop=True).then_inc(s_bd, 1)
        if dbg is not None and dbg[0] == 8:
            s_dbg = sem("dbg")
            with nc.Block() as block:
                @block.sync
                def _(sp):
                    sp.dma_start(dbg[1][:, 0:8192], region_b[:, 0:8192]).then_inc(s_dbg, 16)
                    sp.dma_start(dbg[1][:, 8192:8192 + 256], gate[:, :, :].rearrange("p n e -> p (n e)")).then_inc(s_dbg, 16)
                    sp.dma_start(dbg[1][:, 8448:8448 + 256], slot[:, :, :].rearrange("p n e -> p (n e)")).then_inc(s_dbg, 16)
                    sp.dma_start(dbg[1][0:1, 8704:8704 + 2 * TAB + 2], table[:, :].bitcast(F32)).then_inc(s_dbg, 16)
                    sp.dma_start(out[0], x[0]).then_inc(s_dbg, 16)
                    sp.wait_ge(s_dbg, 80)
            return
        CH = 6
        GU = 4
        RING = 3
        DVE_K = 5
        CW = KT * 512
        raw = [region_b[:, r * CW:(r + 1) * CW].rearrange("p (k c) -> p k c", k=KT) for r in range(RING)]
        part_hi = [region_c[:, r * CW:r * CW + CW // 2].bitcast(FP16).rearrange("p (k c) -> p k c", k=KT) for r in range(RING)]
        part_lo = [region_c[:, r * CW + CW // 2:(r + 1) * CW].bitcast(FP16).rearrange("p (k c) -> p k c", k=KT) for r in range(RING)]
        xg = region_b[0:HS, RING * CW:RING * CW + 2 * D].bitcast(FP16).rearrange("p (h d) -> p h d", h=2)
        yrow = region_b[0:HS, RING * CW + 2 * D:RING * CW + 4 * D].rearrange("p (h d) -> p h d", h=2)
        w9 = [0]

        def cut(n):
            w9[0] += n
            assert w9[0] <= 8192
            return region_a[:, w9[0] - n:w9[0]]

        xT_hi, xT_lo, aT_hi, aT_lo = (cut(KT * SL // 2).bitcast(FP16).rearrange("p (k t) -> p k t", k=KT) for _ in range(4))
        yT = cut(KT * SL).rearrange("p (k t) -> p k t", k=KT)
        pick = cut(NT * SL // 2).bitcast(BF16).rearrange("p (n t) -> p n t", n=NT)
        g_lin, u_lin, sig, g_act, act32 = ([cut(2 * SL) for _ in range(2)] for _ in range(5))
        b_cur = region_d[:, 0:2 * KT]
        trash = region_d[0:HS, 32:34]
        row_t, empty_t, g_t = region_d[0:HS, 34:36], region_d[0:HS, 36:38], region_d[0:HS, 38:40]
        sel_next = region_d[0:HS, 40:44]
        sel_cur = region_d[0:HS, 44:48]
        gate_prev = region_d[0:HS, 48:50]
        rows_prev = region_d[0:HS, 50:52].bitcast(I32)
        picked = region_d[0:HS, 54:66].rearrange("p (v h) -> p v h", v=6)
        carrier = region_d[0:HS, 68:72]
        ident16 = region_d[:, 72:136].bitcast(FP16)
        rows_get = region_d[0:HS, 52:54].bitcast(I32)
        w_gu_v = w_gate_up[0].rearrange("e (k p) (g c) -> e p k g c", p=P, g=2)
        w_dn_v = w_down[0].rearrange("e (k p) c -> e p k c", p=P)

        s_raw = [sem(f"chunk_loaded{r}") for r in range(RING)]
        s_hi9, s_lod, s_lop = sem("part_hi_ready"), sem("part_lo_dve"), sem("part_lo_pool")
        s_gu, s_clamp, s_sig, s_act = sem("gu_ready"), sem("gu_clamped"), sem("sigmoid_ready"), sem("act_steps")
        s_dn, s_dnc, s_pi = sem("down_ready"), sem("down_copied"), sem("picked_copied")
        s_pick, s_idx, s_sel1, s_sel2, s_shift, s_bcur = sem("pick_ready"), sem("picked"), sem("rows_ready"), sem("sel_ready"), sem("sel_shifted"), sem("b_cur_ready")
        s_xg, s_xgT, s_xhi, s_xlo = sem("x_gathered"), sem("xg_turned"), sem("x_hi_ready"), sem("x_lo_ready")
        s_yT, s_yrow, s_scat, s_init, s_out, s_id = sem("y_turned"), sem("y_scaled"), sem("y_added"), sem("init9"), sem("out_stored"), sem("ident16_ready")
        C1 = 1
        CGEV = 4
        CDN = 2
        CSC = 32

        Y_BANK = [4, 5, 7, 6]

        def turned(b):
            return bank[b][:, 0:2 * SL].bitcast(FP16).rearrange("p (k t) -> p k t", k=4)

        def count_items(eng):
            return eng.value_load(table[0:1, 2 * TAB:2 * TAB + 1], min_val=NE, max_val=ITEMS)

        with nc.Block() as block:
            @block.sync
            def _(sp):
                def load(e, j):
                    r = j % RING
                    for g in range(2):
                        if j < GU:
                            src = w_gu_v[ds(e, 1), :, :, g, j * 256:j * 256 + 256].rearrange("a p k c -> p (a k) c")
                            dst = raw[r][:, :, g * 256:g * 256 + 256]
                        else:
                            src = w_dn_v[ds(e, 1), :, g * (KT // 2):(g + 1) * (KT // 2),
                                         (j - GU) * 512:(j - GU) * 512 + 512].rearrange("a p k c -> p (a k) c")
                            dst = raw[r][:, g * (KT // 2):(g + 1) * (KT // 2), :]
                        sp.dma_start(dst, src).then_inc(s_raw[r], 16)

                n_items = count_items(sp)
                for j in range(RING):
                    load(0, j)
                with sp.Fori(0, n_items) as i:
                    e = sp.value_load(table[0:1, ds(i, 1)], min_val=0, max_val=NE - 1)
                    e_next = sp.value_load(table[0:1, ds(i + 1, 1)], min_val=0, max_val=NE - 1)
                    for m in range(CH):
                        sp.wait_ge(s_lod, i * CH + (m + 1))
                        sp.wait_ge(s_lop, i * CH + (m + 1))
                        load(e if m < RING else e_next, (m + RING) % CH)
                sp.wait_ge(s_raw[2], n_items * 64 + 32)
                sp.wait_ge(s_scat, n_items * 32 + (CSC + 32))
                for q in range(4):
                    sp.dma_start(out[0, q * (T // 4):(q + 1) * (T // 4), :], rows_out[q * (T // 4):(q + 1) * (T // 4), :]).then_inc(s_out, 16)
                sp.wait_ge(s_out, 64)

            @block.gpsimd
            def _(pool):
                pool.memset(yT, 0.0).then_inc(s_init, 1)
                pool.memset(sel_cur[:, 0:2], 0.0).then_inc(s_init, 1)
                pool.iota(trash, [[HS, 2]], base=T, channel_multiplier=1, allow_small_or_imprecise_dtypes=True).then_inc(s_init, 1)
                pool.iota(sel_cur[:, 2:4], [[HS, 2]], base=T, channel_multiplier=1, allow_small_or_imprecise_dtypes=True).then_inc(s_init, 1)
                pool.memset(yrow, 0.0).then_inc(s_init, 1)
                pool.iota(rows_prev, [[HS, 2]], base=T, channel_multiplier=1).then_inc(s_init, 1)
                pool.wait_ge(s_init, 6)
                n_items = count_items(pool)

                def low_part(c, j):
                    r = j % RING
                    pool.wait_ge(s_hi9, c + 1)
                    pool.tensor_tensor(part_lo[r][:, DVE_K:, :], raw[r][:, DVE_K:, :], part_hi[r][:, DVE_K:, :],
                                       ALU.subtract).then_inc(s_lop, 1)

                def gather():
                    for h in range(2):
                        pool.indirect_dma_start(out=xg[:, h, :], out_offset=None, in_=rows_h2[:, :],
                                                in_offset=bass.IndirectOffsetOnAxis(ap=rows_get[:, h:h + 1], axis=0)).then_inc(s_xg, 16)

                def scatter(h):
                    pool.indirect_dma_start(out=rows_out[:, :], out_offset=bass.IndirectOffsetOnAxis(ap=rows_prev[:, h:h + 1], axis=0),
                                            in_=yrow[:, h, :], in_offset=None, compute_op=ALU.add).then_inc(s_scat, 16)

                def carry_wait(c):
                    pool.tensor_tensor(carrier[:, c:c + 1], trash[:, 0:1], trash[:, 0:1], ALU.add)

                scatter(0)
                pool.wait_ge(s_sel1, 1)
                gather()
                low_part(0, 0)
                low_part(1, 1)
                pool.wait_ge(s_scat, 16)
                scatter(1)
                with pool.Fori(0, n_items) as i:
                    pool.wait_ge(s_sel1, i + 2)
                    carry_wait(0)
                    gather()
                    low_part(i * CH + 2, 2)
                    low_part(i * CH + 3, 0)
                    low_part(i * CH + 4, 1)
                    pool.wait_ge(s_yrow, i * 4 + (4 + C1))
                    carry_wait(1)
                    scatter(0)
                    low_part(i * CH + 5, 2)
                    pool.wait_ge(s_scat, i * 32 + (CSC + 16))
                    carry_wait(2)
                    scatter(1)
                    low_part(i * CH + 6, 0)
                    low_part(i * CH + 7, 1)
                pool.wait_ge(s_yrow, n_items * 4 + (4 + C1))
                carry_wait(3)
                scatter(0)
                pool.wait_ge(s_scat, n_items * 32 + (CSC + 16))
                carry_wait(1)
                scatter(1)

            @block.scalar
            def _(act):
                act.preload_act_table(ACT.Sigmoid)
                act.nop().then_inc(s_yrow, C1)
                act.nop().then_inc(s_dnc, CDN)
                n_items = count_items(act)

                def high_part(j, uses):
                    r = j % RING
                    act.wait_ge(s_raw[r], uses)
                    act.activation(part_hi[r], raw[r], ACT.Copy).then_inc(s_hi9, 1)

                def x_high(item, q):
                    act.wait_ge(s_xgT, item * 4 + (2 * q + 1))
                    act.activation(xT_hi[:, 4 * q:4 * q + 4, :], turned(7), ACT.Copy).then_inc(s_xhi, 1)

                def sigmoid(i, j):
                    act.wait_ge(s_clamp, i * 8 + (2 * j + 2 + CGEV))
                    act.activation(sig[j % 2], g_lin[j % 2], ACT.Sigmoid, scale=1.702).then_inc(s_sig, 1)

                def y_rows(i, g):
                    h, q = g // 2, g % 2
                    if g == 0:
                        act.wait_ge(s_shift, i * 2 + 1)
                        act.wait_ge(s_scat, i * 32 + CSC)
                    act.wait_ge(s_yT, i * 4 + (g + 1))
                    act.activation(yrow[:, h, q * 512:q * 512 + 512], bank[Y_BANK[g]][0:HS, :], ACT.Copy,
                                   scale=gate_prev[:, h:h + 1]).then_inc(s_yrow, 1)

                def y_copy(i, q):
                    act.wait_ge(s_dn, i * 4 + (q + 1 + C1))
                    act.activation(yT[:, 2 * q:2 * q + 2, :], bank[4 + q % 2][:, 0:2 * SL].rearrange("p (k t) -> p k t", k=2),
                                   ACT.Copy).then_inc(s_dnc, 1)

                high_part(0, 32)
                high_part(1, 32)
                for q in range(2):
                    x_high(0, q)
                with act.Fori(0, n_items) as i:
                    for j in range(CH):
                        if j == 0:
                            act.wait_ge(s_dn, i * 4 + C1)
                        elif j <= GU:
                            act.wait_ge(s_gu, i * 8 + 2 * j)
                        else:
                            act.wait_ge(s_dn, i * 4 + (2 + C1))
                        high_part(j + 2, i * 64 + 32 * ((j + 2) // RING + 1))
                        for g in {0: (0,), 1: (1, 2), 2: (3,)}.get(j, ()):
                            y_rows(i, g)
                        if j < GU:
                            sigmoid(i, j)
                        if j >= GU:
                            y_copy(i, 2 * j - 8)
                            y_copy(i, 2 * j - 7)
                        if j == 3 or j == 4:
                            x_high(i + 1, j - 3)
                for g in range(4):
                    y_rows(n_items, g)

            @block.vector
            def _(dve):
                dve.nop().then_inc(s_clamp, CGEV)
                n_items = count_items(dve)

                def choose(e, base):
                    at = iota[:, ds(base, SL)].unsqueeze(1).to_broadcast([P, NT, SL])
                    dve.tensor_tensor(pick, at, slot[:, :, ds(e, 1)].to_broadcast([P, NT, SL]), ALU.is_equal)
                    dve.tensor_copy(values[:, :, 3:6].unsqueeze(3), gate3[:, :, :, ds(e, 1)]).then_inc(s_pick, 1)

                def rows(item):
                    dve.wait_ge(s_idx, item + 1)
                    if not isinstance(item, int):
                        dve.wait_ge(s_xg, item * 32)
                    dve.tensor_copy(picked.rearrange("p v h -> p h v"), bank[6][0:HS, 0:12].rearrange("p (h v) -> p h v", h=2)).then_inc(s_pi, 1)
                    dve.wait_ge(s_pi, item + 1)
                    dve.tensor_tensor(row_t, picked[:, 0, :], picked[:, 1, :], ALU.add)
                    dve.scalar_tensor_tensor(out=empty_t, in0=picked[:, 2, :], scalar=1.0, in1=trash, op0=ALU.add, op1=ALU.mult)
                    dve.tensor_tensor(g_t, picked[:, 3, :], picked[:, 4, :], ALU.add)
                    dve.tensor_tensor(rows_get, picked[:, 0, :], picked[:, 1, :], ALU.add).then_inc(s_sel1, 1)
                    dve.wait_ge(s_sel1, item + 1)
                    if not isinstance(item, int):
                        dve.wait_ge(s_shift, item * 2)
                    dve.tensor_tensor(sel_next[:, 0:2], g_t, picked[:, 5, :], ALU.add)
                    dve.tensor_tensor(sel_next[:, 2:4], row_t, empty_t, ALU.add).then_inc(s_sel2, 1)

                def shift(i):
                    dve.wait_ge(s_yrow, i * 4 + C1)
                    dve.wait_ge(s_scat, i * 32 + CSC)
                    dve.wait_ge(s_sel2, i + 1)
                    dve.tensor_copy(gate_prev, sel_cur[:, 0:2])
                    dve.tensor_copy(rows_prev, sel_cur[:, 2:4]).then_inc(s_shift, 1)
                    dve.wait_ge(s_shift, i * 2 + 1)
                    dve.tensor_copy(sel_cur, sel_next).then_inc(s_shift, 1)

                def bias(e):
                    dve.tensor_copy(b_cur[:, 0:KT], b_gu[:, ds(e * (2 * KT), KT)])
                    dve.tensor_scalar(b_cur[:, KT:2 * KT], b_gu[:, ds(e * (2 * KT) + KT, KT)], 1.0, None, ALU.add).then_inc(s_bcur, 1)

                def low_part(c, j):
                    r = j % RING
                    dve.wait_ge(s_hi9, c + 1)
                    dve.tensor_tensor(part_lo[r][:, 0:DVE_K, :], raw[r][:, 0:DVE_K, :], part_hi[r][:, 0:DVE_K, :],
                                      ALU.subtract).then_inc(s_lod, 1)

                def x_low(item, q):
                    dve.wait_ge(s_xgT, item * 4 + (2 * q + 2))
                    dve.tensor_copy(xT_lo[:, 4 * q:4 * q + 4, :], turned(6)).then_inc(s_xlo, 1)

                def activate(i, j):
                    o = j % 2
                    for x in range(2):
                        f = 2 * j + x
                        dve.wait_ge(s_gu, i * 8 + (f + 1))
                        dve.tensor_scalar(g_lin[o][:, x * SL:x * SL + SL], bank[f % 4][:, 0:SL], b_cur[:, f:f + 1], 7.0, ALU.add, ALU.min)
                        dve.tensor_scalar(u_lin[o][:, x * SL:x * SL + SL], bank[f % 4][:, SL:2 * SL], b_cur[:, KT + f:KT + f + 1], 8.0,
                                          ALU.add, ALU.min).then_inc(s_clamp, 1)
                    hi = aT_hi[:, 2 * j:2 * j + 2, :].rearrange("p k t -> p (k t)")
                    lo = aT_lo[:, 2 * j:2 * j + 2, :].rearrange("p k t -> p (k t)")
                    dve.wait_ge(s_sig, i * 4 + (j + 1))
                    dve.tensor_tensor(g_act[o], g_lin[o], sig[o], ALU.mult).then_inc(s_act, 1)
                    dve.wait_ge(s_act, i * 12 + (3 * j + 1))
                    dve.scalar_tensor_tensor(out=act32[o], in0=u_lin[o], scalar=-6.0, in1=g_act[o], op0=ALU.max, op1=ALU.mult)
                    dve.scalar_tensor_tensor(out=hi, in0=u_lin[o], scalar=-6.0, in1=g_act[o], op0=ALU.max, op1=ALU.mult).then_inc(s_act, 1)
                    dve.wait_ge(s_act, i * 12 + (3 * j + 2))
                    dve.tensor_tensor(lo, act32[o], hi, ALU.subtract).then_inc(s_act, 1)

                dve.wait_ge(s_init, 6)
                dve.tensor_copy(ident16, ident[:, :]).then_inc(s_id, 1)
                choose(0, 0)
                bias(0)
                rows(0)
                low_part(0, 0)
                low_part(1, 1)
                for q in range(2):
                    x_low(0, q)
                choose(1, 0)
                with dve.Fori(0, n_items) as i:
                    e_next = dve.value_load(table[0:1, ds(i + 1, 1)], min_val=0, max_val=NE - 1)
                    e_after = dve.value_load(table[0:1, ds(i + 2, 1)], min_val=0, max_val=NE - 1)
                    base_after = dve.value_load(table[0:1, ds(i + (TAB + 2), 1)], min_val=0, max_val=(MAXC - 1) * SL)
                    shift(i)
                    rows(i + 1)
                    for j in range(CH):
                        if j == 0:
                            dve.wait_ge(s_bcur, i + 1)
                        if j == GU - 1:
                            activate(i, j)
                        low_part(i * CH + (j + 2), j + 2)
                        if j < GU - 1:
                            activate(i, j)
                        if j == 3:
                            bias(e_next)
                        if j == 3 or j == 4:
                            x_low(i + 1, j - 3)
                        if j == 4:
                            choose(e_after, base_after)
                shift(n_items)

            @block.tensor
            def _(pe):
                pe.nop().then_inc(s_dn, C1)
                pe.wait_ge(s_init, 6)
                n_items = count_items(pe)

                def find(item):
                    pe.wait_ge(s_pick, item + 1)
                    for h in range(2):
                        for n in range(NT):
                            mm = pe.matmul(bank[6][0:HS, h * 6:h * 6 + 6], pick[:, n, h * HS:h * HS + HS], values[:, n, :],
                                           start=(n == 0), stop=(n == NT - 1))
                    mm.then_inc(s_idx, 1)

                def turn_x(item, q):
                    if q == 0:
                        pe.wait_ge(s_xg, item * 32 + 32)
                    for s in range(2):
                        if q == 1:
                            pe.wait_ge((s_xhi, s_xlo)[s], item * 2 + 1)
                        for k in range(4):
                            for h in range(2):
                                at = s * D + (4 * q + k) * P
                                mm = pe.transpose(turned(7 - s)[:, k, h * HS:h * HS + HS], xg[:, h, at:at + P], ident16[0:HS, 0:HS])
                        mm.then_inc(s_xgT, 1)

                def turn_y(i, g):
                    h, q = g // 2, g % 2
                    if g == 0:
                        pe.wait_ge(s_dnc, i * 4 + CDN)
                    for d in range(4):
                        mm = pe.transpose(bank[Y_BANK[g]][0:HS, d * P:d * P + P], yT[:, 4 * q + d, h * HS:h * HS + HS], ident[:, :])
                    mm.then_inc(s_yT, 1)

                def parts_ready(c):
                    pe.wait_ge(s_lod, c + 1)
                    pe.wait_ge(s_lop, c + 1)

                def product(out_ap, r, col, k, hi, lo, clear=True):
                    wh, wl = part_hi[r][:, k, col * P:col * P + P], part_lo[r][:, k, col * P:col * P + P]
                    for s, (a, b) in enumerate(((wh, hi[:, k, :]), (wh, lo[:, k, :]), (wl, hi[:, k, :]))):
                        mm = pe.matmul(out_ap, a, b, start=(clear and k == 0 and s == 0), stop=(k == KT - 1 and s == 2),
                                       skip_group_check=True)
                    return mm

                def gate_up(i, j):
                    parts_ready(i * CH + j)
                    for x in range(2):
                        f = 2 * j + x
                        pe.wait_ge(s_clamp, i * 8 + (f + 1))
                        for g in range(2):
                            for k in range(KT):
                                if f == 0 and g == 0 and k % 4 == 0:
                                    pe.wait_ge(s_xhi, i * 2 + (k // 4 + 1))
                                    pe.wait_ge(s_xlo, i * 2 + (k // 4 + 1))
                                mm = product(bank[f % 4][:, g * SL:g * SL + SL], j % RING, 2 * g + x, k, xT_hi, xT_lo)
                        mm.then_inc(s_gu, 1)
                        if f == 0:
                            find(i + 1)

                def down(i, j):
                    parts_ready(i * CH + j)
                    for k0, k1 in ((0, KT - 2), (KT - 2, KT)) if j == GU else ((0, KT),):
                        for x in range(2):
                            q = 2 * (j - GU) + x
                            if k0 == 0:
                                pe.wait_ge(s_dnc, i * 4 + (q + 1))
                            for y in range(2):
                                for k in range(k0, k1):
                                    if j == GU and x == 0 and y == 0 and k % 2 == 0:
                                        pe.wait_ge(s_act, i * 12 + 3 * (k // 2 + 1))
                                    mm = product(bank[4 + q % 2][:, y * SL:y * SL + SL], j % RING, 2 * x + y, k, aT_hi, aT_lo, y == 0)
                            if k1 == KT:
                                mm.then_inc(s_dn, 1)

                pe.wait_ge(s_id, 1)
                find(0)
                pe.wait_ge(s_pi, 1)
                for q in range(2):
                    turn_x(0, q)
                with pe.Fori(0, n_items) as i:
                    gate_up(i, 0)
                    for g in range(3):
                        turn_y(i, g)
                    gate_up(i, 1)
                    pe.wait_ge(s_pi, i + 2)
                    turn_y(i, 3)
                    gate_up(i, 2)
                    gate_up(i, 3)
                    pe.wait_ge(s_yrow, i * 4 + (4 + C1))
                    turn_x(i + 1, 0)
                    down(i, 4)
                    turn_x(i + 1, 1)
                    down(i, 5)
                pe.wait_ge(s_xhi, n_items * 2 + 2)
                pe.wait_ge(s_xlo, n_items * 2 + 2)
                for g in range(4):
                    turn_y(n_items, g)

NAMES = ["x", "norm1_g", "w_in", "sb_q_norm_g", "sb_k_norm_g", "sb_out_norm_g", "hg_lb_logits", "hg_out_norm_g",
         "w_out", "norm2_g", "w_router", "b_router", "w_gate_up", "b_gate_up", "w_down", "b_down"]


def kernel(**inputs):
    import numpy as np
    import concourse.bacc as bacc
    from concourse.bass_utils import run_bass_kernel_spmd

    nc = bacc.Bacc("TRN2", target_bir_lowering=False, num_devices=1)
    arrays, args = {}, []
    for name in NAMES:
        a = np.ascontiguousarray(inputs[name])
        arrays[name + "_dram"] = a
        args.append(nc.dram_tensor(name + "_dram", a.shape, mybir.dt.from_np(a.dtype), kind="ExternalInput").ap())
    out = nc.dram_tensor("out_dram", inputs["x"].shape, F32, kind="ExternalOutput").ap()
    build_trunk(nc, *args, out)
    r = run_bass_kernel_spmd(nc, [arrays], core_ids=[0])
    return r.results[0]["out_dram"]
```

```python
from contextlib import ExitStack

import concourse.bass as bass
from concourse import mybir

F32 = mybir.dt.float32
BF16 = mybir.dt.bfloat16
FP16 = mybir.dt.float16
I32 = mybir.dt.int32
ALU = mybir.AluOpType
ACT = mybir.ActivationFunctionType
AX_X = mybir.AxisListType.X
ds = bass.ds

P = 128
FREE = 1


def build_trunk(nc, x, norm1_g, w_in, sb_q_norm_g, sb_k_norm_g, sb_out_norm_g, hg_lb_logits,
                hg_out_norm_g, w_out, norm2_g, w_router, b_router, w_gate_up, b_gate_up,
                w_down, b_down, out):
    T, D = x.shape[1], x.shape[2]
    KT = D // P
    NT = T // P
    SBW = sb_out_norm_g.shape[1]
    HGW = hg_out_norm_g.shape[1]
    DH = sb_q_norm_g.shape[1]
    HT = SBW // P
    NH = HGW // P
    RB = 32
    NB = P // RB
    EPS = 1e-6
    WC = 256
    with ExitStack() as ctx:
        def sb(name, shape, dt):
            return ctx.enter_context(nc.sbuf_tensor(name, shape, dt))

        def ps(name, shape, dt):
            return ctx.enter_context(nc.psum_tensor(name, shape, dt))

        def sem(name):
            return ctx.enter_context(nc.semaphore(name))

        region_a = sb("region_a", [P, 2 * KT * T // 2], F32)
        region_b = sb("region_b", [P, 16 * T], F32)
        region_c = sb("region_c", [P, NT * 3 * SBW], F32)
        region_d = sb("region_d", [P, 8192 + 2048], F32)

        hT_hi = region_a[:, 0:KT * T // 2].bitcast(FP16).rearrange("p (k t) -> p k t", k=KT)
        hT_lo = region_a[:, KT * T // 2:KT * T].bitcast(FP16).rearrange("p (k t) -> p k t", k=KT)
        x_all = region_b[:, 0:NT * D].rearrange("p (n d) -> p n d", n=NT)
        cm = region_b[:, :].rearrange("p (c t) -> p c t", c=16)
        tm = region_c[:, :].rearrange("p (n c) -> p n c", n=NT)

        ident = sb("ident", [P, P], F32)
        neg_tri = sb("neg_tri", [P, P], F32)
        neg_ones = sb("neg_ones", [P, P], F32)
        ones = sb("ones", [P, P], F32)
        head_ones = sb("head_ones", [P, P], F32)
        block_tri = sb("block_tri", [P, P], F32)
        keep = sb("keep", [P, P], F32)
        never = sb("never", [P, P], F32)
        eps = sb("eps", [P, 1], F32)
        g_q = sb("g_q", [P, 1], F32)
        g_k = sb("g_k", [P, 1], F32)
        g_mix = sb("g_mix", [P, 2 * HT], F32)
        sumsq = sb("sumsq", [P, 2 * NT], F32)
        rstd = sb("rstd", [P, 2 * NT], F32)

        bank = [ps(f"bank{i}", [P, 512], F32) for i in range(8)]

        g1_rows = region_c[:, 0:D]
        xn = [region_c[:, D:2 * D], region_c[:, 2 * D:3 * D]]
        sq_junk = region_c[:, 3 * D:4 * D]
        s_x = [sem(f"x_loaded{n}") for n in range(NT // 2)]
        s_g1, s_small = sem("g1_loaded"), sem("gains_loaded")
        s_const, s_ss, s_rstd, s_xn = sem("const_ready"), sem("sumsq_ready"), sem("rstd_ready"), sem("xn_ready")
        s_xT, s_hhi, s_hlo = sem("xT_ready"), sem("h_hi_ready"), sem("h_lo_ready")
        w_raw = [region_d[:, n * KT * WC:(n + 1) * KT * WC].rearrange("p (k c) -> p k c", k=KT) for n in range(2)]
        w_in_k = w_in[0].rearrange("(k p) c -> p k c", p=P)
        s_w = [sem("w_in_loaded0"), sem("w_in_loaded1")]
        with nc.Block() as block:
            @block.sync
            def _(sp):
                for n in range(4):
                    sp.dma_start(x_all[:, 2 * n:2 * n + 2, :],
                                 x[0, 2 * n * P:(2 * n + 2) * P, :].rearrange("(n p) d -> p n d", p=P)).then_inc(s_x[n], 16)
                    if n == 0:
                        sp.dma_start(g1_rows, norm1_g[0:1, :].partition_broadcast(P)).then_inc(s_g1, 16)
                for half in range(2):
                    sp.dma_start(g_q[64 * half:64 * half + 64, :], sb_q_norm_g[0, :].rearrange("(p a) -> p a", a=1)).then_inc(s_small, 16)
                    sp.dma_start(g_k[64 * half:64 * half + 64, :], sb_k_norm_g[0, :].rearrange("(p a) -> p a", a=1)).then_inc(s_small, 16)
                with nc.allow_non_contiguous_dma("gains, a few hundred words"):
                    sp.dma_start(g_mix[:, 0:HT], sb_out_norm_g[0, :].rearrange("(c p) -> p c", p=P)).then_inc(s_small, 16)
                    sp.dma_start(g_mix[:, HT:2 * HT], hg_out_norm_g[0, :].rearrange("(c p) -> p c", p=P)).then_inc(s_small, 16)
                for n in range(2):
                    sp.dma_start(w_raw[n], w_in_k[:, :, n * WC:(n + 1) * WC]).then_inc(s_w[n], 16)
                sp.wait_ge(s_small, 96)

            @block.gpsimd
            def _(pool):
                pool.memset(ident[:, :], 0.0).then_inc(s_const, 1)
                pool.memset(neg_tri[:, :], -1.0).then_inc(s_const, 1)
                pool.memset(block_tri[:, :], 1.0).then_inc(s_const, 1)
                pool.memset(head_ones[:, :], 1.0).then_inc(s_const, 1)
                pool.memset(ones[:, :], 1.0).then_inc(s_const, 1)
                pool.memset(neg_ones[:, :], -1.0).then_inc(s_const, 1)
                pool.memset(eps[:, :], EPS).then_inc(s_const, 1)
                pool.memset(keep[:, :], 1.0).then_inc(s_const, 1)
                pool.memset(never[:, :], 0.0).then_inc(s_const, 1)
                pool.wait_ge(s_const, 9)
                pool.affine_select(out=never[:, :], in_=never[:, :], compare_op=ALU.is_gt, fill=-1.0e30, base=0,
                                   pattern=[[1, P]], channel_multiplier=-1).then_inc(s_const, 1)
                pool.affine_select(out=keep[:, :], in_=keep[:, :], compare_op=ALU.is_gt, fill=0.0, base=0,
                                   pattern=[[1, P]], channel_multiplier=-1).then_inc(s_const, 1)
                pool.affine_select(out=ident[:, :], in_=ident[:, :], compare_op=ALU.not_equal, fill=1.0, base=0,
                                   pattern=[[-1, P]], channel_multiplier=1).then_inc(s_const, 1)
                pool.affine_select(out=neg_tri[:, :], in_=neg_tri[:, :], compare_op=ALU.is_ge, fill=0.0, base=0,
                                   pattern=[[-1, P]], channel_multiplier=1).then_inc(s_const, 1)
                bt = block_tri[:, :].rearrange("p (c t) -> p c t", t=RB)
                ho = head_ones[:, :].rearrange("p (c t) -> p c t", t=DH)
                pool.affine_select(out=bt, in_=bt, compare_op=ALU.is_ge, fill=0.0, base=0,
                                   pattern=[[RB, NB], [1, RB]], channel_multiplier=-1).then_inc(s_const, 1)
                pool.affine_select(out=ho, in_=ho, compare_op=ALU.is_ge, fill=0.0, base=0,
                                   pattern=[[-DH, 2], [0, DH]], channel_multiplier=1).then_inc(s_const, 1)
                pool.wait_ge(s_const, 15)
                pool.affine_select(out=bt, in_=bt, compare_op=ALU.is_ge, fill=0.0, base=0,
                                   pattern=[[-RB, NB], [0, RB]], channel_multiplier=1).then_inc(s_const, 1)
                pool.affine_select(out=ho, in_=ho, compare_op=ALU.is_ge, fill=0.0, base=DH - 1,
                                   pattern=[[DH, 2], [0, DH]], channel_multiplier=-1).then_inc(s_const, 1)

            @block.scalar
            def _(act):
                act.preload_act_table_set("natural_log_exp_and_others")
                act.wait_ge(s_const, 9)

                def factors(m):
                    act.wait_ge(s_x[m], 16)
                    for par in range(2):
                        if not (isinstance(m, int) and par == 0):
                            act.wait_ge(s_ss, m * 2 + par)
                        act.activation(sq_junk, x_all[:, ds(m * 2 + par, 1), :].rearrange("p a d -> p (a d)"), ACT.Square,
                                       accum_out=sumsq[:, ds(m * 2 + par, 1)]).then_inc(s_ss, 1)
                    pair = ds(m * 2, 2)
                    act.wait_ge(s_ss, m * 2 + 2)
                    act.activation(rstd[:, pair], sumsq[:, pair], ACT.Ln, bias=eps[:, :], scale=1.0 / D).then_inc(s_rstd, 1)
                    act.wait_ge(s_rstd, m * 2 + 1)
                    act.activation(rstd[:, pair], rstd[:, pair], ACT.Exp, scale=-0.5).then_inc(s_rstd, 1)

                def high(m):
                    for par in range(2):
                        n = m * 2 + par
                        for half in range(2):
                            act.wait_ge(s_xT, n * 2 + (half + 1 + FREE))
                            act.activation(hT_hi[:, 4 * half:4 * half + 4, ds(n * P, P)],
                                           bank[2 * par + half][:, :].rearrange("p (k t) -> p k t", k=4), ACT.Copy).then_inc(s_hhi, 1)

                factors(0)
                for m in range(NT // 2 - 1):
                    factors(m + 1)
                    high(m)
                high(NT // 2 - 1)

            @block.vector
            def _(dve):
                dve.nop().then_inc(s_hlo, 3 + FREE)
                dve.wait_ge(s_g1, 16)

                def scaled_row(n, at, pair):
                    dve.wait_ge(s_rstd, pair * 2 + 2)
                    if not isinstance(n, int) or n > 0:
                        dve.wait_ge(s_xT, n * 2 + (FREE - 2))
                    dve.scalar_tensor_tensor(out=xn[at], in0=x_all[:, ds(n, 1), :].rearrange("p a d -> p (a d)"),
                                             scalar=rstd[:, ds(n, 1)], in1=g1_rows, op0=ALU.mult, op1=ALU.mult).then_inc(s_xn, 1)

                def low(n, par):
                    for half in range(2):
                        dve.wait_ge(s_hhi, n * 2 + (half + 1))
                        dve.tensor_tensor(hT_lo[:, 4 * half:4 * half + 4, ds(n * P, P)],
                                          bank[2 * par + half][:, :].rearrange("p (k t) -> p k t", k=4),
                                          hT_hi[:, 4 * half:4 * half + 4, ds(n * P, P)], ALU.subtract).then_inc(s_hlo, 1)

                scaled_row(0, 0, 0)
                with dve.Fori(0, NT // 2 - 1) as m:
                    scaled_row(m * 2 + 1, 1, m)
                    low(m * 2, 0)
                    scaled_row(m * 2 + 2, 0, m + 1)
                    low(m * 2 + 1, 1)
                scaled_row(NT - 1, 1, NT // 2 - 1)
                low(NT - 2, 0)
                low(NT - 1, 1)

            @block.tensor
            def _(pe):
                pe.nop().then_inc(s_xT, FREE)
                pe.wait_ge(s_const, 17)
                with pe.Fori(0, NT // 2) as m:
                    for par in range(2):
                        n = m * 2 + par
                        pe.wait_ge(s_xn, n + 1)
                        for half in range(2):
                            pe.wait_ge(s_hlo, n * 2 + (half + FREE))
                            for k in range(4):
                                at = (4 * half + k) * P
                                mm = pe.transpose(bank[2 * par + half][:, k * P:(k + 1) * P], xn[par][:, at:at + P], ident[:, :])
                            mm.then_inc(s_xT, 1)

        w_par = [region_d[:, 2 * KT * WC + n * KT * WC:2 * KT * WC + (n + 1) * KT * WC].bitcast(FP16)
                 .rearrange("p (s k c) -> p s k c", s=2, k=KT) for n in range(2)]
        s_whi, s_wlo, s_piece, s_evac = sem("w_hi_ready"), sem("w_lo_ready"), sem("piece_ready"), sem("piece_copied")
        RUNS = [(0, 4, True, 0), (1024, 2, False, 0), (1536, 2, True, 8), (2048, 4, False, 512), (3072, 2, True, 12)]
        PC = 4

        def chunk_runs(eng, loaded=0):
            first = 0
            for c0, n, major, dst in RUNS:
                if first < loaded:
                    c0, n, first = c0 + loaded * WC, n - loaded, loaded
                with eng.Fori(0, n // 2) as m:
                    for par in range(2):
                        yield m * 2 + (first + par), m + first // 2, m * 2 + par, par, c0, major, dst
                first += n

        with nc.Block() as block:
            @block.sync
            def _(sp):
                for at, uses, n, par, c0, major, dst in chunk_runs(sp, 2):
                    sp.wait_ge(s_wlo, at + FREE)
                    sp.dma_start(w_raw[par], w_in_k[:, :, ds(n * WC + c0, WC)]).then_inc(s_w[par], 16)

            @block.scalar
            def _(act):
                for at, uses, n, par, c0, major, dst in chunk_runs(act):
                    act.wait_ge(s_w[par], uses * 16 + 16)
                    act.wait_ge(s_piece, at * PC + FREE)
                    act.activation(w_par[par][:, 0], w_raw[par], ACT.Copy).then_inc(s_whi, 1)

            @block.gpsimd
            def _(pool):
                pool.nop().then_inc(s_wlo, 1 + FREE)
                for at, uses, n, par, c0, major, dst in chunk_runs(pool):
                    pool.wait_ge(s_whi, at + 1)
                    pool.tensor_tensor(w_par[par][:, 1], w_raw[par], w_par[par][:, 0], ALU.subtract).then_inc(s_wlo, 1)

            @block.tensor
            def _(pe):
                pe.nop().then_inc(s_piece, PC + FREE)
                for at, uses, n, par, c0, major, dst in chunk_runs(pe):
                    pe.wait_ge(s_wlo, at + 2 + FREE)
                    for q in range(PC):
                        pe.wait_ge(s_evac, at * PC + q + FREE)
                        if major:
                            ct, half = q // 2, q % 2
                            for k in range(KT):
                                w = [w_par[par][:, s, k, ct * P:(ct + 1) * P] for s in range(2)]
                                h = [t[:, k, half * 512:(half + 1) * 512] for t in (hT_hi, hT_lo)]
                                for j, (a, b) in enumerate(((w[0], h[0]), (w[0], h[1]), (w[1], h[0]))):
                                    mm = pe.matmul(bank[q][:, :], a, b, start=(k == 0 and j == 0),
                                                   stop=(k == KT - 1 and j == 2))
                        else:
                            for tt in range(2):
                                for k in range(KT):
                                    t0 = (2 * q + tt) * P
                                    w = [w_par[par][:, s, k, :] for s in range(2)]
                                    h = [t[:, k, t0:t0 + P] for t in (hT_hi, hT_lo)]
                                    for j, (a, b) in enumerate(((h[0], w[0]), (h[0], w[1]), (h[1], w[0]))):
                                        mm = pe.matmul(bank[q][:, tt * WC:(tt + 1) * WC], a, b,
                                                       start=(k == 0 and j == 0), stop=(k == KT - 1 and j == 2))
                        mm.then_inc(s_piece, 1)

            @block.vector
            def _(dve):
                dve.nop().then_inc(s_evac, PC - 1 + FREE)
                for at, uses, n, par, c0, major, dst in chunk_runs(dve):
                    for q in range(PC):
                        dve.wait_ge(s_piece, at * PC + (PC + q + 1) + FREE)
                        if major:
                            ct, half = q // 2, q % 2
                            dst_ap = cm[:, ds(n * 2 + (dst + ct), 1), half * 512:(half + 1) * 512].rearrange("p a t -> p (a t)")
                            dve.tensor_copy(dst_ap, bank[q][:, :]).then_inc(s_evac, 1)
                        else:
                            dve.tensor_copy(tm[:, 2 * q:2 * q + 2, ds(n * WC + dst, WC)],
                                            bank[q][:, :].rearrange("p (a c) -> p a c", a=2)).then_inc(s_evac, 1)

        gains = sb("gains", [P, 2 * HT], F32)
        s_gain = sem("gains_ready")
        s_sq, s_sumsq, s_ln, s_rs, s_nrm = sem("qk_sq"), sem("qk_sumsq"), sem("qk_ln"), sem("qk_rs"), sem("qk_normed")
        def tmp(n, count=1):
            if n < 20:
                return region_d[:, n * 512:(n + count) * 512]
            return region_a[:, (n - 20) * 512:(n - 20 + count) * 512]

        sq_of, rs_of = ([[tmp(4 * n + 2 * par + half) for half in range(2)] for par in range(2)] for n in range(2))
        l_0, l_1, l_s, lb_rows, oml_rows = (tmp(31 + n) for n in range(5))
        s_lbl, s_lb = sem("lb_logits_loaded"), sem("lb_steps")
        with nc.Block() as block:
            @block.sync
            def _(sp):
                sp.dma_start(l_0, hg_lb_logits[0:1, :].partition_broadcast(P)).then_inc(s_lbl, 16)
                sp.dma_start(l_1, hg_lb_logits[1:2, :].partition_broadcast(P)).then_inc(s_lbl, 16)

            @block.scalar
            def _(act):
                act.preload_act_table_set("natural_log_exp_and_others")
                act.wait_ge(s_lb, 3)
                act.activation(l_0, l_0, ACT.Exp).then_inc(s_lb, 1)
                act.activation(l_1, l_1, ACT.Exp).then_inc(s_lb, 1)

                def squares(c, par):
                    for half in range(2):
                        part = cm[:, ds(c, 1), half * 512:half * 512 + 512].rearrange("p a t -> p (a t)")
                        act.activation(sq_of[par][half], part, ACT.Square).then_inc(s_sq, 1)

                def factors(c, par):
                    for half in range(2):
                        act.wait_ge(s_sumsq, c * 2 + (half + 1))
                        act.wait_ge(s_nrm, c * 2 + FREE)
                        act.activation(rs_of[par][half], bank[2 * par + half][:, :], ACT.Ln, bias=eps[:, :],
                                       scale=1.0 / DH).then_inc(s_ln, 1)
                        act.wait_ge(s_ln, c * 2 + (half + 1))
                        act.activation(rs_of[par][half], rs_of[par][half], ACT.Exp, scale=-0.5).then_inc(s_rs, 1)

                squares(0, 0)
                with act.Fori(0, HT - 1) as m:
                    squares(m * 2 + 1, 1)
                    factors(m * 2, 0)
                    squares(m * 2 + 2, 0)
                    factors(m * 2 + 1, 1)
                squares(2 * HT - 1, 1)
                factors(2 * HT - 2, 0)
                factors(2 * HT - 1, 1)

            @block.tensor
            def _(pe):
                with pe.Fori(0, HT) as m:
                    for par in range(2):
                        for half in range(2):
                            pe.wait_ge(s_sq, m * 4 + (2 * par + half + 1))
                            pe.matmul(bank[2 * par + half][:, :], head_ones[:, :], sq_of[par][half],
                                      start=True, stop=True).then_inc(s_sumsq, 1)

            @block.vector
            def _(dve):
                dve.nop().then_inc(s_nrm, 2 + FREE)
                dve.wait_ge(s_lbl, 32)
                dve.tensor_tensor(l_s, l_0, l_1, ALU.max).then_inc(s_lb, 1)
                dve.wait_ge(s_lb, 1)
                dve.tensor_tensor(l_0, l_0, l_s, ALU.subtract).then_inc(s_lb, 1)
                dve.tensor_tensor(l_1, l_1, l_s, ALU.subtract).then_inc(s_lb, 1)
                dve.wait_ge(s_lb, 5)
                dve.tensor_tensor(l_s, l_0, l_1, ALU.add).then_inc(s_lb, 1)
                dve.wait_ge(s_lb, 6)
                dve.reciprocal(l_s, l_s).then_inc(s_lb, 1)
                dve.wait_ge(s_lb, 7)
                dve.tensor_tensor(lb_rows, l_0, l_s, ALU.mult).then_inc(s_lb, 1)
                dve.wait_ge(s_lb, 8)
                dve.tensor_scalar(oml_rows, lb_rows, -1.0, 1.0, ALU.mult, ALU.add).then_inc(s_lb, 1)
                dve.tensor_scalar(gains[:, 0:HT], ones[:, 0:HT], g_q[:, 0:1], DH ** -0.5, ALU.mult, ALU.mult).then_inc(s_gain, 1)
                dve.tensor_scalar(gains[:, HT:2 * HT], ones[:, 0:HT], g_k[:, 0:1], None, ALU.mult).then_inc(s_gain, 1)
                dve.wait_ge(s_gain, 2)
                with dve.Fori(0, HT) as m:
                    for par in range(2):
                        for half in range(2):
                            c = m * 2 + par
                            part = cm[:, ds(c, 1), half * 512:half * 512 + 512].rearrange("p a t -> p (a t)")
                            dve.wait_ge(s_rs, c * 2 + (half + 1))
                            dve.scalar_tensor_tensor(out=part, in0=part, scalar=gains[:, ds(c, 1)], in1=rs_of[par][half],
                                                     op0=ALU.mult, op1=ALU.mult).then_inc(s_nrm, 1)

        q_cur, k_cur = region_d[:, 0:T], region_d[:, T:2 * T]
        zc = [region_d[:, 2048 + n * 512:2560 + n * 512] for n in range(2)]
        lg = [region_d[:, 3072 + n * 512:3584 + n * 512] for n in range(2)]
        spl = [region_d[:, 4096 + n * 512:4608 + n * 512] for n in range(3)]
        wt = [region_d[:, 5632 + n * 512:6144 + n * 512] for n in range(2)]
        carry = [[region_d[:, 6656 + (2 * h + n) * 512:7168 + (2 * h + n) * 512] for n in range(2)] for h in range(2)]
        a_tm = [region_d[:, 8704 + n * 512:9216 + n * 512] for n in range(2)]
        SP_MAX = 40.0
        GB = 4
        steps = [(g, s, h) for g in range(NT // GB) for s in range(GB * (g + 1) - 1, -1, -1) for h in range(2)]
        NS = len(steps)
        diag = [s >= GB * g for g, s, h in steps]
        col = [max(0, s - GB * g) * P for g, s, h in steps]
        n_diag = [sum(diag[:n + 1]) for n in range(NS)]
        adds = [s > 0 for g, s, h in steps]
        n_adds = [sum(adds[:n + 1]) for n in range(NS)]
        ND, NA = n_diag[-1], n_adds[-1]
        turn = []
        seen = {}
        for g, s, h in steps:
            turn.append(seen.get((g, h), 0) % 2)
            seen[(g, h)] = seen.get((g, h), 0) + 1
        LAG_T, LAG_V = 2, 3
        zb, ab_bank, tb = bank[0:4], bank[4:6], bank[6]
        s_pair, s_z, s_cap, s_e, s_l = sem("pair_copied"), sem("z_ready"), sem("capped_ready"), sem("e_ready"), sem("log_ready")
        s_sp, s_spm, s_add, s_tri = sem("sp_ready"), sem("sp_masked"), sem("carry_ready"), sem("exponent_ready")
        s_wx, s_pv, s_asb, s_aT, s_acp = sem("w_ready"), sem("pv_done"), sem("a_rows_ready"), sem("aT_ready"), sem("aT_copied")
        with nc.Block() as block:
            @block.gpsimd
            def _(pool):
                with pool.Fori(0, HT) as c:
                    pool.wait_ge(s_z, c * NS + FREE)
                    pool.tensor_copy(q_cur, cm[:, ds(c, 1), :].rearrange("p a t -> p (a t)")).then_inc(s_pair, 1)
                    pool.tensor_copy(k_cur, cm[:, ds(c + HT, 1), :].rearrange("p a t -> p (a t)")).then_inc(s_pair, 1)

                    for n, (g, s, h) in enumerate(steps):
                        c0, size = col[n], GB * P - col[n]
                        pool.wait_ge(s_sp, c * NS + (n + 1))
                        if diag[n]:
                            pool.tensor_tensor(spl[n % 3][:, 0:P], spl[n % 3][:, 0:P], keep[:, :], ALU.mult).then_inc(s_spm, 1)
                            pool.wait_ge(s_spm, c * ND + n_diag[n])
                        if adds[n]:
                            if n >= 4:
                                pool.wait_ge(s_tri, c * NS + (n - 3))
                            new, old = carry[h][turn[n]], carry[h][1 - turn[n]]
                            if n >= 2 and adds[n - 2]:
                                pool.wait_ge(s_add, c * NA + n_adds[n - 2])
                            first = s == GB * (g + 1) - 1
                            edge = c0 + P if diag[n] else c0
                            if diag[n]:
                                cp = pool.tensor_tensor(new[:, c0:edge], spl[n % 3][:, 0:P], keep[:, :], ALU.mult)
                            if not first:
                                cp = pool.tensor_tensor(new[:, edge:512], old[:, edge:512], spl[n % 3][:, edge - c0:size], ALU.add)
                            cp.then_inc(s_add, 1)

            @block.vector
            def _(dve):
                dve.nop().then_inc(s_acp, FREE)
                with dve.Fori(0, HT) as c:
                    def capped(n):
                        size = GB * P - col[n]
                        dve.wait_ge(s_z, c * NS + (n + 1) + FREE)
                        if n >= 2:
                            dve.wait_ge(s_e, c * NS + (n - 1))
                        dve.tensor_scalar(zc[n % 2][:, 0:size], zb[n % 4][:, 0:size], SP_MAX, None, ALU.min).then_inc(s_cap, 1)

                    capped(0)
                    for n, (g, s, h) in enumerate(steps):
                        size = GB * P - col[n]
                        if n + 1 < NS:
                            capped(n + 1)
                        dve.wait_ge(s_l, c * NS + (n + 1))
                        if n >= 3:
                            dve.wait_ge(s_tri, c * NS + (n - 2))
                            if n_adds[n - 3]:
                                dve.wait_ge(s_add, c * NA + n_adds[n - 3])
                        dve.tensor_tensor(spl[n % 3][:, 0:size], zb[n % 4][:, 0:size], lg[n % 2][:, 0:size],
                                          ALU.max).then_inc(s_sp, 1)
                    for g in range(2):
                        dve.wait_ge(s_aT, c * 2 + (g + 1) + FREE)
                        dve.tensor_copy(cm[:, ds(c, 1), g * 512:g * 512 + 512].rearrange("p a t -> p (a t)"),
                                        tb[:, :]).then_inc(s_acp, 1)

            @block.scalar
            def _(act):
                act.preload_act_table_set("natural_log_exp_and_others")
                for used in (s_wx, s_asb):
                    act.nop().then_inc(used, FREE)
                with act.Fori(0, HT) as c:
                    def weight(n):
                        size = GB * P - col[n]
                        act.wait_ge(s_tri, c * NS + (n + 1))
                        if n >= 2:
                            act.wait_ge(s_pv, c * NS + (n - 1))
                        act.activation(wt[n % 2][:, 0:size], zb[n % 4][:, 0:size], ACT.Exp).then_inc(s_wx, 1)

                    for n, (g, s, h) in enumerate(steps):
                        size = GB * P - col[n]
                        act.wait_ge(s_cap, c * NS + (n + 1))
                        if n >= 2:
                            act.wait_ge(s_sp, c * NS + (n - 1))
                        act.activation(lg[n % 2][:, 0:size], zc[n % 2][:, 0:size], ACT.Exp).then_inc(s_e, 1)
                        act.wait_ge(s_e, c * NS + (n + 1))
                        act.activation(lg[n % 2][:, 0:size], lg[n % 2][:, 0:size], ACT.Ln, bias=ones[:, 0:1]).then_inc(s_l, 1)
                        if n >= 2:
                            weight(n - 2)
                    weight(NS - 2)
                    weight(NS - 1)
                    for g in range(2):
                        last = max(n for n in range(NS) if steps[n][0] == g)
                        act.wait_ge(s_pv, c * NS + (last + 1))
                        act.wait_ge(s_aT, c * 2 + FREE)
                        act.activation(a_tm[g], ab_bank[g][:, :], ACT.Copy).then_inc(s_asb, 1)

            @block.tensor
            def _(pe):
                for used in (s_z, s_aT):
                    pe.nop().then_inc(used, FREE)
                with pe.Fori(0, HT) as c:
                    pe.wait_ge(s_pair, c * 2 + 2)
                    for n in range(NS + LAG_V):
                        if n < NS:
                            g, s, h = steps[n]
                            size, t0 = GB * P - col[n], g * GB * P + col[n]
                            if n >= 4:
                                pe.wait_ge(s_wx, c * NS + (n - 3) + FREE)
                            elif n == 0:
                                pe.wait_ge(s_wx, c * NS + FREE)
                            pe.matmul(zb[n % 4][:, 0:size], k_cur[64 * h:64 * h + 64, s * P:(s + 1) * P],
                                      q_cur[64 * h:64 * h + 64, t0:t0 + size], start=True, stop=True,
                                      skip_group_check=True).then_inc(s_z, 1)
                        m = n - LAG_T
                        if 0 <= m < NS:
                            g, s, h = steps[m]
                            size, c0 = GB * P - col[m], col[m]
                            if diag[m]:
                                pe.wait_ge(s_spm, c * ND + n_diag[m])
                            pe.wait_ge(s_sp, c * NS + (m + 1))
                            first = s == GB * (g + 1) - 1
                            mm = pe.matmul(zb[m % 4][:, 0:size], neg_tri[:, :], spl[m % 3][:, 0:size], start=False, stop=True,
                                           skip_group_check=True)
                            if not first:
                                pe.wait_ge(s_add, c * NA + n_adds[m - 2])
                                edge = c0 + P if diag[m] else c0
                                mm = pe.matmul(zb[m % 4][:, edge - c0:size], neg_ones[:, :], carry[h][turn[m - 2]][:, edge:512],
                                               start=False, stop=True, skip_group_check=True)
                            if diag[m]:
                                mm = pe.matmul(zb[m % 4][:, 0:P], ident[:, :], never[:, :], start=False, stop=True,
                                               skip_group_check=True)
                            mm.then_inc(s_tri, 1)
                        m = n - LAG_V
                        if 0 <= m < NS:
                            g, s, h = steps[m]
                            c0 = col[m]
                            pe.wait_ge(s_wx, c * NS + (m + 1) + FREE)
                            if m == 0:
                                pe.wait_ge(s_asb, c * 2 + FREE)
                            for b in range(c0 // P, GB):
                                mm = pe.matmul(ab_bank[g][:, b * P + 64 * h:b * P + 64 * h + 64],
                                               wt[m % 2][:, b * P - c0:b * P - c0 + P],
                                               tm[:, s, ds(c * P + 64 * h, 64)],
                                               start=(s == GB * (g + 1) - 1 and h == 0), stop=(s == 0), skip_group_check=True)
                            mm.then_inc(s_pv, 1)
                    for g in range(2):
                        pe.wait_ge(s_asb, c * 2 + (g + 1) + FREE)
                        pe.wait_ge(s_acp, c * 2 + g + FREE)
                        for b in range(GB):
                            mm = pe.transpose(tb[:, b * P:(b + 1) * P], a_tm[g][:, b * P:(b + 1) * P], ident[:, :])
                        mm.then_inc(s_aT, 1)
        fc, e_f, r_f, enb, kd = (tmp(2 + n) for n in range(5))
        log_f, k_tm, i_cur, eb, qe, ke, kd_tm, att, start = ([tmp(7 + 2 * n), tmp(8 + 2 * n)] for n in range(9))
        state = [None] + [tmp(25 + n) for n in range(3)]
        b_bank, kt_bank, att_bank, o_bank = bank[0:4]
        u_bank = bank[4:8]
        F_MIN = -80.0
        heads = lambda ap: ap.rearrange("p (h t) -> p h t", h=NH)
        blocks = lambda ap: ap.rearrange("p (g t) -> p g t", t=RB)
        SPT = NB * NH
        s_fc, s_ef, s_fd, s_lf1, s_lf = sem("f_capped"), sem("f_exp"), sem("f_steps"), sem("log_f_input"), sem("log_f_ready")
        s_icur, s_b, s_kT, s_ebr, s_qk, s_kd = sem("i_copied"), sem("b_ready"), sem("kT_ready"), sem("exp_b_ready"), sem("qe_ke_ready"), sem("kd_ready")
        s_kdT, s_kdtm, s_att, s_attm, s_u = sem("kdT_ready"), sem("kd_rows_ready"), sem("att_ready"), sem("att_masked"), sem("u_ready")
        s_st, s_o, s_or, s_rf = sem("state_ready"), sem("o_ready"), sem("o_copied"), sem("r_steps")

        def tile_steps(eng, step):
            with eng.Fori(0, NT // 2 - 1) as m:
                for par in range(2):
                    step(m * 2 + par, par, True, True)
            step(NT - 2, 0, False, True)
            step(NT - 1, 1, False, False)

        with nc.Block() as block:
            @block.gpsimd
            def _(pool):
                pool.nop().then_inc(s_lf1, FREE)

                def copy_i(n, par):
                    if not isinstance(n, int) or n > 1:
                        pool.wait_ge(s_o, n + (FREE - 1))
                    pool.tensor_copy(i_cur[par], tm[:, ds(n, 1), 2 * SBW:3 * SBW].rearrange("p a c -> p (a c)")).then_inc(s_icur, 1)

                def gates(n, par):
                    pool.wait_ge(s_rf, n * 2 + 2)
                    if not isinstance(n, int):
                        pool.wait_ge(s_b, n + (FREE - 1))
                    pool.tensor_tensor(log_f[par], r_f, oml_rows, ALU.mult).then_inc(s_lf1, 1)
                    pool.wait_ge(s_lf1, n * 2 + (1 + FREE))
                    pool.tensor_tensor(log_f[par], log_f[par], lb_rows, ALU.add).then_inc(s_lf1, 1)

                def step(t, par, with_gates, with_blocks):
                    if with_blocks:
                        copy_i(t + 1, 1 - par)
                    if with_gates:
                        gates(t + 2, par)

                gates(0, 0)
                copy_i(0, 0)
                gates(1, 1)
                tile_steps(pool, step)

            @block.scalar
            def _(act):
                act.preload_act_table_set("natural_log_exp_and_others")
                for used in (s_ef, s_or):
                    act.nop().then_inc(used, FREE)

                def exp_f(n):
                    act.wait_ge(s_fc, n + 1)
                    act.activation(e_f, fc, ACT.Exp, scale=-1.0).then_inc(s_ef, 1)

                def sigmoid_f(n):
                    act.wait_ge(s_ef, n + (1 + FREE))
                    act.wait_ge(s_lf1, n * 2 + FREE)
                    act.wait_ge(s_fd, n * 2)
                    act.activation(r_f, e_f, ACT.Ln, bias=ones[:, 0:1]).then_inc(s_rf, 1)
                    act.wait_ge(s_rf, n * 2 + 1)
                    act.activation(r_f, r_f, ACT.Exp, scale=-1.0).then_inc(s_rf, 1)

                def ln_f(n, par):
                    act.wait_ge(s_lf1, n * 2 + (2 + FREE))
                    act.activation(log_f[par], log_f[par], ACT.Ln).then_inc(s_lf, 1)

                def exp_b(n, par):
                    act.wait_ge(s_b, n + (1 + FREE))
                    if not isinstance(n, int) or n > 1:
                        act.wait_ge(s_st, (n - 1) * SPT + FREE)
                    act.activation(eb[par], b_bank[:, :], ACT.Exp).then_inc(s_ebr, 1)
                    act.wait_ge(s_qk, n * 2)
                    act.activation(enb, b_bank[:, :], ACT.Exp, scale=-1.0).then_inc(s_ebr, 1)

                def copy_kd(n, par):
                    act.wait_ge(s_kdT, n + 1)
                    act.activation(kd_tm[par], kt_bank[:, :], ACT.Copy).then_inc(s_kdtm, 1)

                def step(t, par, with_gates, with_blocks):
                    if with_gates:
                        exp_f(t + 2)
                    if with_blocks:
                        exp_b(t + 1, 1 - par)
                    if with_gates:
                        sigmoid_f(t + 2)
                        ln_f(t + 2, par)
                    if with_blocks:
                        copy_kd(t + 1, 1 - par)
                    act.wait_ge(s_o, t + (1 + FREE))
                    act.activation(cm[:, 2 * HT:2 * HT + NH, ds(t * P, P)], heads(o_bank[:, :]), ACT.Copy).then_inc(s_or, 1)

                exp_f(0)
                sigmoid_f(0)
                ln_f(0, 0)
                exp_f(1)
                sigmoid_f(1)
                exp_b(0, 0)
                ln_f(1, 1)
                copy_kd(0, 0)
                tile_steps(act, step)

            @block.vector
            def _(dve):
                dve.nop().then_inc(s_st, FREE)
                dve.memset(start[0], 0.0).then_inc(s_lb, 1)

                def cap_f(n):
                    dve.wait_ge(s_ef, n + FREE)
                    dve.tensor_scalar(fc, tm[:, ds(n, 1), SBW:2 * SBW].rearrange("p a c -> p (a c)"), F_MIN, None, ALU.max).then_inc(s_fc, 1)

                def gate_k(n, par):
                    dve.wait_ge(s_rf, n * 2 + 2)
                    dve.tensor_tensor(k_tm[par], e_f, r_f, ALU.mult).then_inc(s_fd, 1)
                    dve.wait_ge(s_fd, n * 2 + 1)
                    dve.tensor_tensor(k_tm[par], k_tm[par], oml_rows, ALU.mult).then_inc(s_fd, 1)

                def scale_qk(n, par):
                    dve.wait_ge(s_ebr, n * 2 + 2)
                    if not isinstance(n, int) or n > 1:
                        dve.wait_ge(s_o, n + (FREE - 1))
                    dve.tensor_tensor(heads(qe[par]), cm[:, 2 * HT:2 * HT + NH, ds(n * P, P)], heads(eb[par]), ALU.mult).then_inc(s_qk, 1)
                    dve.wait_ge(s_kT, n + 1)
                    dve.tensor_tensor(ke[par], kt_bank[:, :], enb, ALU.mult).then_inc(s_qk, 1)
                    dve.wait_ge(s_qk, n * 2 + 2)
                    dve.wait_ge(s_kdT, n)
                    dve.tensor_tensor(blocks(kd), blocks(ke[par]), blocks(eb[par])[:, :, RB - 1:RB].to_broadcast([P, NH * NB, RB]),
                                      ALU.mult).then_inc(s_kd, 1)

                def mask_att(n, par):
                    dve.wait_ge(s_att, n + 1)
                    dve.tensor_tensor(heads(att[par]), heads(att_bank[:, :]), block_tri[:, :].unsqueeze(1).to_broadcast([P, NH, P]),
                                      ALU.mult).then_inc(s_attm, 1)

                def states(n, par):
                    here = [start[par]] + state[1:] + [start[1 - par]]
                    dve.wait_ge(s_u, n + 1)
                    for c in range(NB):
                        if c:
                            dve.wait_ge(s_st, n * SPT + (c * NH + FREE))
                        for h in range(NH):
                            last = h * P + c * RB + RB - 1
                            dve.scalar_tensor_tensor(out=here[c + 1][:, h * P:(h + 1) * P], in0=here[c][:, h * P:(h + 1) * P],
                                                     scalar=eb[par][:, last:last + 1], in1=u_bank[c][:, h * P:(h + 1) * P],
                                                     op0=ALU.mult, op1=ALU.add).then_inc(s_st, 1)

                def step(t, par, with_gates, with_blocks):
                    if with_gates:
                        cap_f(t + 2)
                    if with_blocks:
                        scale_qk(t + 1, 1 - par)
                    if with_gates:
                        gate_k(t + 2, par)
                    states(t, par)
                    if with_blocks:
                        mask_att(t + 1, 1 - par)

                for n in range(2):
                    cap_f(n)
                    gate_k(n, n)
                scale_qk(0, 0)
                mask_att(0, 0)
                tile_steps(dve, step)

            @block.tensor
            def _(pe):
                for used in (s_o, s_b):
                    pe.nop().then_inc(used, FREE)

                def sums(n, par):
                    pe.wait_ge(s_lf, n + 1)
                    pe.wait_ge(s_ebr, n * 2)
                    for h in range(NH):
                        mm = pe.matmul(b_bank[:, h * P:(h + 1) * P], log_f[par][:, h * P:(h + 1) * P], block_tri[:, :], start=True, stop=True)
                    mm.then_inc(s_b, 1)
                    pe.wait_ge(s_fd, n * 2 + 2)
                    pe.wait_ge(s_kdtm, n)
                    for h in range(NH):
                        mm = pe.transpose(kt_bank[:, h * P:(h + 1) * P], k_tm[par][:, h * P:(h + 1) * P], ident[:, :])
                    mm.then_inc(s_kT, 1)

                def inner(n, par):
                    pe.wait_ge(s_kd, n + 1)
                    for h in range(NH):
                        mm = pe.transpose(kt_bank[:, h * P:(h + 1) * P], kd[:, h * P:(h + 1) * P], ident[:, :])
                    mm.then_inc(s_kdT, 1)
                    pe.wait_ge(s_attm, n)
                    for h in range(NH):
                        mm = pe.matmul(att_bank[:, h * P:(h + 1) * P], ke[par][:, h * P:(h + 1) * P], qe[par][:, h * P:(h + 1) * P],
                                       start=True, stop=True)
                    mm.then_inc(s_att, 1)

                def updates(n, par):
                    pe.wait_ge(s_kdtm, n + 1)
                    pe.wait_ge(s_icur, n + 1)
                    pe.wait_ge(s_st, n * SPT + FREE)
                    for c in range(NB):
                        rows = slice(c * RB, (c + 1) * RB)
                        for h in range(NH):
                            mm = pe.matmul(u_bank[c][:, h * P:(h + 1) * P], kd_tm[par][rows, h * P:(h + 1) * P],
                                           i_cur[par][rows, h * P:(h + 1) * P], start=True, stop=True)
                    mm.then_inc(s_u, 1)

                def out_att(n, par):
                    pe.wait_ge(s_attm, n + 1)
                    pe.wait_ge(s_or, n + FREE)
                    for h in range(NH):
                        pe.matmul(o_bank[:, h * P:(h + 1) * P], i_cur[par][:, h * P:(h + 1) * P], att[par][:, h * P:(h + 1) * P],
                                  start=(h == 0), stop=False, skip_group_check=True)

                def out_states(n, par):
                    here = [start[par]] + state[1:]
                    for c in range(NB):
                        if c:
                            pe.wait_ge(s_st, n * SPT + (c * NH + FREE))
                        for h in range(NH):
                            at = h * P + c * RB
                            mm = pe.matmul(o_bank[:, at:at + RB], here[c][:, h * P:(h + 1) * P], qe[par][:, at:at + RB],
                                           start=False, stop=True, skip_group_check=True)
                    mm.then_inc(s_o, 1)

                def step(t, par, with_gates, with_blocks):
                    if with_blocks:
                        sums(t + 1, 1 - par)
                    updates(t, par)
                    out_att(t, par)
                    if with_blocks:
                        inner(t + 1, 1 - par)
                    out_states(t, par)

                sums(0, 0)
                inner(0, 0)
                tile_steps(pe, step)

        mix_hi, mix_lo = hT_hi, hT_lo
        sq, rs = [tmp(0), tmp(1)], [tmp(2), tmp(3)]
        gate_t = [tmp(4), tmp(5)]
        mixed = [tmp(6), tmp(7)]
        wo_raw = region_c[:, 0:KT * D].rearrange("p (k c) -> p k c", k=KT)
        wo_hi = region_c[:, KT * D:KT * D + KT * D // 2].bitcast(FP16).rearrange("p (k c) -> p k c", k=KT)
        wo_lo = region_d[:, 10240 - KT * D // 2:10240].bitcast(FP16).rearrange("p (k c) -> p k c", k=KT)
        s_wohi, s_wolo, s_x2 = sem("wo_hi_ready"), sem("wo_lo_ready"), sem("x_reloaded")
        x2_all = region_b[:, 0:NT * D].rearrange("p (n d) -> p n d", n=NT)
        s_wo, s_mq, s_ms, s_mln, s_mrs = sem("w_out_loaded"), sem("mix_sq"), sem("mix_sumsq"), sem("mix_ln"), sem("mix_rs")
        s_gate_rs = sem("gate_times_rs")
        s_gc, s_ge, s_gs, s_mx, s_mhi, s_mlo = sem("gate_capped"), sem("gate_exp"), sem("gate_steps"), sem("mix_ready"), sem("mix_hi_ready"), sem("mix_lo_ready")
        with nc.Block() as block:
            @block.sync
            def _(sp):
                sp.dma_start(wo_raw, w_out[0].rearrange("(k p) c -> p k c", p=P)).then_inc(s_wo, 16)
                sp.wait_ge(s_mx, 2 * HT + FREE)
                for n in range(4):
                    sp.dma_start(x2_all[:, 2 * n:2 * n + 2, :],
                                 x[0, 2 * n * P:(2 * n + 2) * P, :].rearrange("(n p) d -> p n d", p=P)).then_inc(s_x2, 16)

            @block.gpsimd
            def _(pool):
                pool.wait_ge(s_wo, 16)
                for k in range(KT):
                    pool.tensor_copy(wo_hi[:, k, :], wo_raw[:, k, :]).then_inc(s_wohi, 1)
                    pool.wait_ge(s_wohi, k + 1)
                    pool.tensor_tensor(wo_lo[:, k, :], wo_raw[:, k, :], wo_hi[:, k, :], ALU.subtract).then_inc(s_wolo, 1)

            def tiles(eng):
                for first, src in ((0, 0), (HT, 2 * HT)):
                    with eng.Fori(0, HT) as c:
                        yield c, c + first, src, first > 0

            @block.scalar
            def _(act):
                act.preload_act_table_set("natural_log_exp_and_others")
                act.nop().then_inc(s_mln, FREE)

                def squares(c, k, src):
                    for half in range(2):
                        part = cm[:, ds(c + src, 1), half * 512:half * 512 + 512].rearrange("p a t -> p (a t)")
                        if not isinstance(k, int):
                            act.wait_ge(s_ms, k * 2 + FREE)
                        act.activation(sq[half], part, ACT.Square).then_inc(s_mq, 1)

                def high(k):
                    for half in range(2):
                        act.wait_ge(s_mx, k * 2 + (half + 1 + FREE))
                        act.activation(mix_hi[:, ds(k, 1), half * 512:half * 512 + 512].rearrange("p a t -> p (a t)"), mixed[half],
                                       ACT.Copy).then_inc(s_mhi, 1)

                def output_gate(c):
                    for half in range(2):
                        act.wait_ge(s_gc, c * 2 + (half + 1))
                        act.activation(gate_t[half], gate_t[half], ACT.Exp, scale=-1.0).then_inc(s_ge, 1)
                        act.wait_ge(s_ge, c * 6 + (3 * half + 1))
                        act.activation(gate_t[half], gate_t[half], ACT.Ln, bias=ones[:, 0:1]).then_inc(s_ge, 1)
                        act.wait_ge(s_ge, c * 6 + (3 * half + 2))
                        act.activation(gate_t[half], gate_t[half], ACT.Exp, scale=-1.0).then_inc(s_ge, 1)

                def factors(k, width):
                    for half in range(2):
                        act.wait_ge(s_ms, k * 2 + (half + 1 + FREE))
                        act.wait_ge(s_mx, k * 2 + FREE)
                        act.activation(rs[half], bank[half][:, :], ACT.Ln, bias=eps[:, :], scale=1.0 / width).then_inc(s_mln, 1)
                        act.wait_ge(s_mln, k * 2 + (half + 1 + FREE))
                        act.activation(rs[half], rs[half], ACT.Exp, scale=-0.5).then_inc(s_mrs, 1)

                squares(0, 0, 0)
                factors(0, DH)
                with act.Fori(1, HT) as c:
                    squares(c, c, 0)
                    high(c - 1)
                    factors(c, DH)
                with act.Fori(0, HT) as c:
                    squares(c, c + HT, 2 * HT)
                    high(c + (HT - 1))
                    output_gate(c)
                    factors(c + HT, P)
                high(2 * HT - 1)

            @block.tensor
            def _(pe):
                pe.nop().then_inc(s_ms, FREE)
                for c, k, src, rec in tiles(pe):
                    for half in range(2):
                        pe.wait_ge(s_mq, k * 2 + (half + 1))
                        pe.wait_ge(s_mln, k * 2 + FREE)
                        pe.matmul(bank[half][:, :], (ones if rec else head_ones)[:, :], sq[half], start=True, stop=True).then_inc(s_ms, 1)

            @block.vector
            def _(dve):
                for used in (s_mx, s_mlo):
                    dve.nop().then_inc(used, FREE)
                for c, k, src, rec in tiles(dve):
                    if rec:
                        for half in range(2):
                            part = cm[:, ds(c + 3 * HT, 1), half * 512:half * 512 + 512].rearrange("p a t -> p (a t)")
                            dve.wait_ge(s_mx, k * 2 + FREE)
                            dve.tensor_scalar(gate_t[half], part, F_MIN, None, ALU.max).then_inc(s_gc, 1)
                        for half in range(2):
                            part = cm[:, ds(c + 3 * HT, 1), half * 512:half * 512 + 512].rearrange("p a t -> p (a t)")
                            dve.wait_ge(s_ge, c * 6 + (3 * half + 3))
                            dve.tensor_tensor(gate_t[half], gate_t[half], part, ALU.mult).then_inc(s_gs, 1)
                    for half in range(2):
                        part = cm[:, ds(c + src, 1), half * 512:half * 512 + 512].rearrange("p a t -> p (a t)")
                        dve.wait_ge(s_mrs, k * 2 + (half + 1))
                        dve.wait_ge(s_mlo, k * 2 + FREE)
                        if rec:
                            dve.wait_ge(s_gs, c * 2 + (half + 1))
                            dve.tensor_tensor(rs[half], rs[half], gate_t[half], ALU.mult).then_inc(s_gate_rs, 1)
                            dve.wait_ge(s_gate_rs, c * 2 + (half + 1))
                        dve.scalar_tensor_tensor(out=mixed[half], in0=part, scalar=g_mix[:, ds(k, 1)], in1=rs[half],
                                                 op0=ALU.mult, op1=ALU.mult).then_inc(s_mx, 1)
                    for half in range(2):
                        dve.wait_ge(s_mhi, k * 2 + (half + 1))
                        hi, lo = (t[:, ds(k, 1), half * 512:half * 512 + 512].rearrange("p a t -> p (a t)") for t in (mix_hi, mix_lo))
                        dve.tensor_tensor(lo, mixed[half], hi, ALU.subtract).then_inc(s_mlo, 1)
        NE = w_router.shape[2]
        TOPK = 4

        def unit(n):
            return region_b[:, NT * D + n * D:NT * D + (n + 1) * D]

        h2, h2T, g2_rows, junk2, gT, w_r, b_dn, h2_pair = (unit(n) for n in range(8))
        h2_pair = h2_pair.bitcast(FP16).rearrange("p (s d) -> p s d", s=2)
        w_r = w_r[:, 0:KT * NE].rearrange("p (k e) -> p k e", k=KT)
        SL = 160
        HS = SL // 2
        MAXC = -(-T // SL)
        ITEMS = NE + T * TOPK // SL
        TAB = ITEMS + 8
        rows_out = nc.dram_tensor("rows_out", (T + SL, D), F32, kind="Internal").ap()
        rows_h2 = nc.dram_tensor("rows_h2", (T, 2 * D), FP16, kind="Internal").ap()
        logit = sb("logit", [P, NT, NE + TOPK], F32)
        b_r = sb("b_r", [P, NE], F32)
        s_w7 = sem("router_loaded")
        s_pr, s_x2r, s_sq2, s_l2, s_rs2, s_h2 = sem("mix_product"), sem("x2_ready"), sem("x2_sumsq"), sem("x2_ln"), sem("x2_rstd"), sem("h2_ready")
        s_h2phi, s_h2plo = sem("h2_hi_ready"), sem("h2_lo_ready")
        s_h2st, s_h2T, s_h2Tc, s_lgt, s_lgc, s_pad = sem("h2_stored"), sem("h2T_ready"), sem("h2T_copied"), sem("logits_ready"), sem("logits_copied"), sem("pad_ready")
        PAD = -3.0e38
        with nc.Block() as block:
            @block.sync
            def _(sp):
                sp.nop().then_inc(s_h2st, FREE)
                sp.dma_start(g2_rows, norm2_g[0:1, :].partition_broadcast(P)).then_inc(s_w7, 16)
                sp.dma_start(w_r, w_router[0].rearrange("(k p) e -> p k e", p=P)).then_inc(s_w7, 16)
                sp.dma_start(b_r[:, :], b_router[0:1, :].partition_broadcast(P)).then_inc(s_w7, 16)
                sp.dma_start(b_dn[0:NE, :], b_down[0]).then_inc(s_w7, 16)
                with sp.Fori(0, NT) as n:
                    sp.wait_ge(s_h2plo, n + 1 + FREE)
                    sp.dma_start(rows_h2[ds(n * P, P), :], h2_pair.rearrange("p s d -> p (s d)")).then_inc(s_h2st, 16)
                sp.wait_ge(s_h2st, 16 * NT + FREE)
                sp.wait_ge(s_w7, 64)

            @block.gpsimd
            def _(pool):
                pool.nop().then_inc(s_h2plo, FREE)
                pool.memset(logit[:, :, :], PAD).then_inc(s_pad, 1)
                with pool.Fori(0, NT) as n:
                    pool.wait_ge(s_h2phi, n + 1)
                    pool.tensor_tensor(h2_pair[:, 1, :], h2, h2_pair[:, 0, :], ALU.subtract).then_inc(s_h2plo, 1)

            @block.scalar
            def _(act):
                act.preload_act_table_set("natural_log_exp_and_others")
                for used in (s_h2Tc, s_lgc):
                    act.nop().then_inc(used, FREE)
                act.wait_ge(s_pad, 1)
                with act.Fori(0, NT) as n:
                    act.wait_ge(s_x2r, n * 2 + 2 + FREE)
                    act.activation(junk2, x2_all[:, ds(n, 1), :].rearrange("p a d -> p (a d)"), ACT.Square,
                                   accum_out=sumsq[:, 0:1]).then_inc(s_sq2, 1)
                    act.wait_ge(s_sq2, n + 1)
                    act.activation(rstd[:, 0:1], sumsq[:, 0:1], ACT.Ln, bias=eps[:, :], scale=1.0 / D).then_inc(s_l2, 1)
                    act.wait_ge(s_l2, n + 1)
                    act.wait_ge(s_h2, n + FREE)
                    act.activation(rstd[:, 1:2], rstd[:, 0:1], ACT.Exp, scale=-0.5).then_inc(s_rs2, 1)
                    act.wait_ge(s_h2, n + 1 + FREE)
                    act.wait_ge(s_h2st, n * 16 + FREE)
                    act.activation(h2_pair[:, 0, :], h2, ACT.Copy).then_inc(s_h2phi, 1)
                    for half in range(2):
                        act.wait_ge(s_h2T, n * 2 + (half + 1) + FREE)
                        act.activation(h2T[:, half * 512:half * 512 + 512], bank[2 + half][:, :], ACT.Copy).then_inc(s_h2Tc, 1)
                    act.wait_ge(s_lgt, n + 1)
                    act.activation(logit[:, ds(n, 1), 0:NE].rearrange("p a e -> p (a e)"), bank[4][:, 0:NE], ACT.Copy).then_inc(s_lgc, 1)

            @block.vector
            def _(dve):
                for used in (s_h2, s_x2r):
                    dve.nop().then_inc(used, FREE)
                dve.wait_ge(s_x2, 64)
                dve.wait_ge(s_w7, 64)
                with dve.Fori(0, NT) as n:
                    for half in range(2):
                        part = x2_all[:, ds(n, 1), half * 512:half * 512 + 512].rearrange("p a d -> p (a d)")
                        dve.wait_ge(s_pr, n * 2 + (half + 1))
                        dve.tensor_tensor(part, part, bank[half][:, :], ALU.add).then_inc(s_x2r, 1)
                    dve.wait_ge(s_rs2, n + 1)
                    dve.wait_ge(s_h2T, n * 2 + FREE)
                    dve.wait_ge(s_h2plo, n + FREE)
                    dve.scalar_tensor_tensor(out=h2, in0=x2_all[:, ds(n, 1), :].rearrange("p a d -> p (a d)"), scalar=rstd[:, 1:2],
                                             in1=g2_rows, op0=ALU.mult, op1=ALU.mult).then_inc(s_h2, 1)

            @block.tensor
            def _(pe):
                pe.nop().then_inc(s_h2T, FREE)
                def project(n, half):
                    pe.wait_ge(s_x2r, n * 2 + FREE)
                    for k in range(KT):
                        m = [t[:, k, ds(n * P, P)] for t in (mix_hi, mix_lo)]
                        w = [t[:, k, half * 512:half * 512 + 512] for t in (wo_hi, wo_lo)]
                        for j, (a, b) in enumerate(((m[0], w[0]), (m[0], w[1]), (m[1], w[0]))):
                            mm = pe.matmul(bank[half][:, :], a, b, start=(k == 0 and j == 0), stop=(k == KT - 1 and j == 2))
                    mm.then_inc(s_pr, 1)

                def turn_h2(n):
                    pe.wait_ge(s_h2, n + 1 + FREE)
                    pe.wait_ge(s_h2Tc, n * 2 + FREE)
                    for half in range(2):
                        for k in range(4):
                            mm = pe.transpose(bank[2 + half][:, k * P:(k + 1) * P], h2[:, (4 * half + k) * P:(4 * half + k + 1) * P], ident[:, :])
                        mm.then_inc(s_h2T, 1)

                def route(n):
                    pe.wait_ge(s_h2Tc, n * 2 + 2 + FREE)
                    pe.wait_ge(s_lgc, n + FREE)
                    for k in range(KT):
                        mm = pe.matmul(bank[4][:, 0:NE], h2T[:, k * P:(k + 1) * P], w_r[:, k, :], start=(k == 0), stop=(k == KT - 1))
                    mm.then_inc(s_lgt, 1)

                project(0, 0)
                project(0, 1)
                pe.wait_ge(s_w7, 64)
                with pe.Fori(0, NT - 1) as n:
                    project(n + 1, 0)
                    turn_h2(n)
                    project(n + 1, 1)
                    route(n)
                turn_h2(NT - 1)
                route(NT - 1)

        gate = sb("gate", [P, NT, NE], F32)
        mask = sb("mask", [P, NT, NE], F32)
        slot = sb("slot", [P, NT, NE], F32)
        gate3 = sb("gate3", [P, NT, 3, NE], BF16)
        b_gu = sb("b_gu", [P, NE * 2 * KT], F32)
        iota = sb("iota", [P, MAXC * SL], F32)
        values = sb("values", [P, NT, 6], BF16)
        table = sb("table", [1, 2 * TAB + 2], I32)
        work = region_c[:, :]
        w_off = [0]

        def take(n):
            w_off[0] += n
            return work[:, w_off[0] - n:w_off[0]]

        top = take(NT * 8).rearrange("p (n k) -> p n k", n=NT)
        rep = take(NT * (NE + TOPK)).rearrange("p (n e) -> p n e", n=NT)
        lg = take(NT * NE).rearrange("p (n e) -> p n e", n=NT)
        ssum, rsum = take(NT), take(NT)
        res = take(NT * NE).rearrange("p (n e) -> p n e", n=NT)
        lt = take(P)
        n_col, code_e = take(1), take(1)
        thr, over, before, cum, pos_i = take(MAXC - 1), take(MAXC - 1), take(MAXC - 1), take(MAXC - 1), take(MAXC - 1)
        hot = take((MAXC - 1) * TAB).rearrange("p (c j) -> p c j", c=MAXC - 1)
        code_c = take(MAXC - 1)
        row_f = take(2 * TAB + 2)
        val_f = take(NT * 2).rearrange("p (n v) -> p n v", n=NT)
        bgu_rows = take(4 * P).rearrange("p (n c) -> p n c", n=4)
        zeros = take(D)
        s_p8 = sem("constants8_ready")
        s_lt, s_d8, s_a8, s_t8 = sem("table_inputs"), sem("routing_steps"), sem("routing_exp"), sem("gate_turned")
        s_gTc, s_bd, s_base, s_bst, s_cnt = sem("gateT_copied"), sem("bias_product"), sem("base_ready"), sem("base_stored"), sem("counts_ready")
        s_bgl, s_bgt, s_bgc, s_tabp, s_trash = sem("bgu_loaded"), sem("bgu_turned"), sem("bgu_copied"), sem("table_product"), sem("trash_cleared")
        NP8 = 12
        CH = 6
        GU = 4
        RING = 3
        CW = KT * 512
        raw = [t.rearrange("p (k c) -> p k c", k=KT) for t in (region_a[:, 0:CW], region_a[:, CW:2 * CW], region_d[:, 0:CW])]
        w_gu_v = w_gate_up[0].rearrange("e (k p) (g c) -> e p k g c", p=P, g=2)
        w_dn_v = w_down[0].rearrange("e (k p) c -> e p k c", p=P)
        s_raw = [sem(f"chunk_loaded{r}") for r in range(RING)]

        def load(sp, e, j):
            r = j % RING
            for g in range(2):
                if j < GU:
                    src = w_gu_v[ds(e, 1), :, :, g, j * 256:j * 256 + 256].rearrange("a p k c -> p (a k) c")
                    dst = raw[r][:, :, g * 256:g * 256 + 256]
                else:
                    src = w_dn_v[ds(e, 1), :, g * (KT // 2):(g + 1) * (KT // 2),
                                 (j - GU) * 512:(j - GU) * 512 + 512].rearrange("a p k c -> p (a k) c")
                    dst = raw[r][:, g * (KT // 2):(g + 1) * (KT // 2), :]
                sp.dma_start(dst, src).then_inc(s_raw[r], 16)

        with nc.Block() as block:
            @block.sync
            def _(sp):
                sp.dma_start(bgu_rows, b_gate_up[0].rearrange("e (j c) -> (e j) c", c=P).rearrange("(n p) c -> p n c", p=P)).then_inc(s_bgl, 16)
                for j in range(RING):
                    load(sp, 0, j)
                sp.wait_ge(s_p8, NP8)
                sp.dma_start(rows_out[T:T + P, :], zeros).then_inc(s_trash, 16)
                sp.dma_start(rows_out[T + P:T + SL, :], zeros[0:SL - P, :]).then_inc(s_trash, 16)
                for n in range(NT):
                    sp.wait_ge(s_base, 2 * n + 2)
                    sp.dma_start(rows_out[n * P:(n + 1) * P, :], x2_all[:, n, :]).then_inc(s_bst, 16)
                sp.wait_ge(s_bst, 16 * NT)
                sp.wait_ge(s_trash, 32)

            @block.gpsimd
            def _(pool):
                pool.memset(lt, 1.0).then_inc(s_p8, 1)
                pool.memset(zeros, 0.0).then_inc(s_p8, 1)
                pool.memset(values[:, :, 2:3], -1.0).then_inc(s_p8, 1)
                pool.memset(row_f, 0.0).then_inc(s_p8, 1)
                pool.iota(iota[:, :], [[1, MAXC * SL]], base=0, channel_multiplier=0, allow_small_or_imprecise_dtypes=True).then_inc(s_p8, 1)
                pool.iota(val_f[:, :, 0:1], [[P, NT]], base=0, channel_multiplier=0, allow_small_or_imprecise_dtypes=True).then_inc(s_p8, 1)
                pool.iota(val_f[:, :, 1:2], [[0, NT]], base=0, channel_multiplier=1, allow_small_or_imprecise_dtypes=True).then_inc(s_p8, 1)
                pool.iota(code_e, [[0, 1]], base=0, channel_multiplier=1, allow_small_or_imprecise_dtypes=True).then_inc(s_p8, 1)
                pool.iota(thr, [[SL, MAXC - 1]], base=SL, channel_multiplier=0, allow_small_or_imprecise_dtypes=True).then_inc(s_p8, 1)
                pool.wait_ge(s_p8, 9)
                pool.affine_select(out=lt, in_=lt, compare_op=ALU.is_gt, fill=0.0, base=0, pattern=[[1, P]],
                                   channel_multiplier=-1).then_inc(s_p8, 1)
                pool.tensor_copy(values[:, :, 0:2], val_f).then_inc(s_p8, 1)
                pool.tensor_copy(code_c, thr).then_inc(s_p8, 1)

            @block.scalar
            def _(act):
                act.preload_act_table_set("natural_log_exp_and_others")
                act.wait_ge(s_d8, 2 + NT + 1 + NT + 2)
                act.activation(lg, lg, ACT.Exp).then_inc(s_a8, 1)
                for b in range(2):
                    act.wait_ge(s_t8, b + 1)
                    act.activation(gT[0:NE, b * 512:(b + 1) * 512], bank[b][0:NE, :], ACT.Copy).then_inc(s_gTc, 1)
                act.wait_ge(s_bgt, 1)
                act.activation(b_gu[:, :], bank[6][:, :], ACT.Copy).then_inc(s_bgc, 1)

            @block.vector
            def _(dve):
                step = [0]

                def link(ins):
                    step[0] += 1
                    ins.then_inc(s_d8, 1)
                    dve.wait_ge(s_d8, step[0])

                link(dve.tensor_tensor(lg, logit[:, :, 0:NE], b_r[:, :].unsqueeze(1).to_broadcast([P, NT, NE]), ALU.add))
                link(dve.tensor_copy(logit[:, :, 0:NE], lg))
                for n in range(NT):
                    link(dve.max(out=top[:, n, :], in_=logit[:, n, :]))
                link(dve.tensor_tensor(lg, lg, top[:, :, 0:1].to_broadcast([P, NT, NE]), ALU.subtract))
                link(dve.memset(top[:, :, TOPK:8], PAD))
                for n in range(NT):
                    link(dve.match_replace(out=rep[:, n, :], in_to_replace=top[:, n, :], in_values=logit[:, n, :], imm_value=-PAD))
                link(dve.tensor_scalar(mask[:, :, :], rep[:, :, 0:NE], 1.0e38, None, ALU.is_ge))
                assert step[0] == 2 + NT + 1 + NT + 2
                dve.wait_ge(s_a8, 1)
                link(dve.tensor_tensor(lg, lg, mask[:, :, :], ALU.mult))
                link(dve.tensor_reduce(ssum, lg, AX_X, ALU.add))
                link(dve.reciprocal(rsum, ssum))
                link(dve.tensor_tensor(gate[:, :, :], lg, rsum.unsqueeze(2).to_broadcast([P, NT, NE]), ALU.mult))
                dve.nop().then_inc(s_lt, 1)
                link(dve.tensor_copy(gate3[:, :, 0, :], gate[:, :, :]))
                link(dve.tensor_tensor(res, gate[:, :, :], gate3[:, :, 0, :], ALU.subtract))
                link(dve.tensor_copy(gate3[:, :, 1, :], res))
                link(dve.tensor_tensor(res, res, gate3[:, :, 1, :], ALU.subtract))
                link(dve.tensor_copy(gate3[:, :, 2, :], res))
                dve.wait_ge(s_cnt, 1)
                pos = bank[2][:, 0:NT * NE].rearrange("p (n e) -> p n e", n=NT)
                link(dve.scalar_tensor_tensor(out=slot[:, :, :], in0=pos, scalar=1.0, in1=mask[:, :, :], op0=ALU.add, op1=ALU.mult))
                link(dve.tensor_scalar(slot[:, :, :], slot[:, :, :], -1.0, None, ALU.add))
                link(dve.tensor_copy(n_col[0:NE, :], bank[3][0:NE, 0:1]))
                dve.wait_ge(s_p8, NP8)
                link(dve.tensor_scalar(over[0:NE, :], thr[0:NE, :], n_col[0:NE, :], None, ALU.is_lt))
                dve.nop().then_inc(s_lt, 1)
                dve.wait_ge(s_cnt, 2)
                link(dve.tensor_copy(before[0:NE, :], bank[4][0:NE, 0:MAXC - 1]))
                link(dve.tensor_copy(cum[0:NE, :], bank[4][0:NE, MAXC - 1:2 * (MAXC - 1)]))
                for c in range(1, MAXC - 1):
                    link(dve.tensor_tensor(cum[0:NE, c:c + 1], cum[0:NE, c:c + 1], cum[0:NE, c - 1:c], ALU.add))
                link(dve.tensor_scalar(pos_i[0:NE, :], before[0:NE, :], float(NE + 1), None, ALU.add))
                link(dve.tensor_tensor(pos_i[0:NE, 1:MAXC - 1], pos_i[0:NE, 1:MAXC - 1], cum[0:NE, 0:MAXC - 2], ALU.add))
                link(dve.tensor_tensor(pos_i[0:NE, :], pos_i[0:NE, :], over[0:NE, :], ALU.mult))
                link(dve.tensor_scalar(pos_i[0:NE, :], pos_i[0:NE, :], -1.0, None, ALU.add))
                for c in range(MAXC - 1):
                    link(dve.tensor_scalar(hot[0:NE, c, :], iota[0:NE, 0:TAB], pos_i[0:NE, c:c + 1], None, ALU.is_equal))
                dve.nop().then_inc(s_lt, 1)
                dve.wait_ge(s_tabp, 1)
                link(dve.tensor_copy(row_f[0:1, NE:TAB], bank[5][0:1, NE:TAB]))
                link(dve.tensor_copy(row_f[0:1, 0:NE], iota[0:1, 0:NE]))
                link(dve.tensor_copy(row_f[0:1, TAB:2 * TAB], bank[5][0:1, TAB:2 * TAB]))
                link(dve.tensor_scalar(row_f[0:1, 2 * TAB:2 * TAB + 1], cum[0:1, MAXC - 2:MAXC - 1], float(NE), None, ALU.add))
                link(dve.tensor_copy(table[:, :], row_f[0:1, :]))
                for n in range(NT):
                    for half in range(2):
                        dve.wait_ge(s_bd, 2 * n + half + 1)
                        part = x2_all[:, n, half * 512:half * 512 + 512]
                        dve.tensor_tensor(part, part, bank[half][:, :], ALU.add).then_inc(s_base, 1)

            @block.tensor
            def _(pe):
                pe.wait_ge(s_bgl, 16)
                for n in range(4):
                    mm = pe.transpose(bank[6][:, n * P:(n + 1) * P], bgu_rows[:, n, :], ident[:, :])
                mm.then_inc(s_bgt, 1)
                pe.wait_ge(s_p8, NP8)
                pe.wait_ge(s_lt, 1)
                for n in range(NT):
                    mm = pe.transpose(bank[n // 4][0:NE, (n % 4) * P:(n % 4 + 1) * P], gate[:, n, :], ident[:, :])
                    if n % 4 == 3:
                        mm.then_inc(s_t8, 1)
                pe.matmul(bank[2][:, 0:NT * NE], lt, mask[:, :, :].rearrange("p n e -> p (n e)"), start=True, stop=False)
                for m in range(NT - 1):
                    pe.matmul(bank[2][:, (m + 1) * NE:NT * NE], ones[:, :], mask[:, m:m + 1, :].to_broadcast([P, NT - 1 - m, NE]),
                              start=False, stop=(m == NT - 2))
                for n in range(NT):
                    mm = pe.matmul(bank[3][0:NE, 0:1], mask[:, n, :], ones[:, 0:1], start=(n == 0), stop=(n == NT - 1))
                mm.then_inc(s_cnt, 1)
                pe.wait_ge(s_lt, 2)
                pe.matmul(bank[4][0:NE, 0:MAXC - 1], lt[0:NE, 0:NE], over[0:NE, :], start=True, stop=True)
                pe.matmul(bank[4][0:NE, MAXC - 1:2 * (MAXC - 1)], ones[0:NE, 0:NE], over[0:NE, :], start=True, stop=True).then_inc(s_cnt, 1)
                pe.wait_ge(s_lt, 3)
                for c in range(MAXC - 1):
                    pe.matmul(bank[5][0:1, 0:TAB], code_e[0:NE, :], hot[0:NE, c, :], start=(c == 0), stop=(c == MAXC - 2))
                for c in range(MAXC - 1):
                    mm = pe.matmul(bank[5][0:1, TAB:2 * TAB], code_c[0:NE, c:c + 1], hot[0:NE, c, :], start=(c == 0), stop=(c == MAXC - 2))
                mm.then_inc(s_tabp, 1)
                pe.wait_ge(s_gTc, 2)
                for n in range(NT):
                    for half in range(2):
                        if n:
                            pe.wait_ge(s_base, 2 * n + half - 1)
                        pe.matmul(bank[half][:, :], gT[0:NE, n * P:(n + 1) * P], b_dn[0:NE, half * 512:(half + 1) * 512],
                                  start=True, stop=True).then_inc(s_bd, 1)
        DVE_K = 5
        part_hi = [region_c[:, r * CW:r * CW + CW // 2].bitcast(FP16).rearrange("p (k c) -> p k c", k=KT) for r in range(RING)]
        part_lo = [region_c[:, r * CW + CW // 2:(r + 1) * CW].bitcast(FP16).rearrange("p (k c) -> p k c", k=KT) for r in range(RING)]
        xg = region_b[0:HS, 8192:8192 + 2 * D].bitcast(FP16).rearrange("p (h d) -> p h d", h=2)
        yrow = region_b[0:HS, 8192 + 2 * D:8192 + 4 * D].rearrange("p (h d) -> p h d", h=2)
        w9 = [0]

        def cut(n):
            w9[0] += n
            assert w9[0] <= 8192
            return region_b[:, w9[0] - n:w9[0]]

        xT_hi, xT_lo, aT_hi, aT_lo = (cut(KT * SL // 2).bitcast(FP16).rearrange("p (k t) -> p k t", k=KT) for _ in range(4))
        yT = cut(KT * SL).rearrange("p (k t) -> p k t", k=KT)
        pick = cut(NT * SL // 2).bitcast(BF16).rearrange("p (n t) -> p n t", n=NT)
        g_lin, u_lin, sig, g_act, act32 = ([cut(2 * SL) for _ in range(2)] for _ in range(5))
        b_cur = region_d[:, CW:CW + 2 * KT]
        trash = region_d[0:HS, CW + 32:CW + 34]
        row_t, empty_t, g_t = region_d[0:HS, CW + 34:CW + 36], region_d[0:HS, CW + 36:CW + 38], region_d[0:HS, CW + 38:CW + 40]
        sel_next = region_d[0:HS, CW + 40:CW + 44]
        sel_cur = region_d[0:HS, CW + 44:CW + 48]
        gate_prev = region_d[0:HS, CW + 48:CW + 50]
        rows_prev = region_d[0:HS, CW + 50:CW + 52].bitcast(I32)
        picked = region_d[0:HS, CW + 54:CW + 66].rearrange("p (v h) -> p v h", v=6)
        carrier = region_d[0:HS, CW + 68:CW + 72]
        ident16 = region_d[:, CW + 72:CW + 136].bitcast(FP16)
        rows_get = region_d[0:HS, CW + 52:CW + 54].bitcast(I32)

        s_hi9, s_lod, s_lop = sem("part_hi_ready"), sem("part_lo_dve"), sem("part_lo_pool")
        s_gu, s_clamp, s_sig, s_act = sem("gu_ready"), sem("gu_clamped"), sem("sigmoid_ready"), sem("act_steps")
        s_dn, s_dnc, s_pi = sem("down_ready"), sem("down_copied"), sem("picked_copied")
        s_pick, s_idx, s_sel1, s_sel2, s_shift, s_bcur = sem("pick_ready"), sem("picked"), sem("rows_ready"), sem("sel_ready"), sem("sel_shifted"), sem("b_cur_ready")
        s_xg, s_xgT, s_xhi, s_xlo = sem("x_gathered"), sem("xg_turned"), sem("x_hi_ready"), sem("x_lo_ready")
        s_yT, s_yrow, s_scat, s_init, s_out, s_id = sem("y_turned"), sem("y_scaled"), sem("y_added"), sem("init9"), sem("out_stored"), sem("ident16_ready")
        C1 = 1
        CGEV = 4
        CDN = 2
        CSC = 32

        Y_BANK = [4, 5, 7, 6]

        def turned(b):
            return bank[b][:, 0:2 * SL].bitcast(FP16).rearrange("p (k t) -> p k t", k=4)

        def count_items(eng):
            return eng.value_load(table[0:1, 2 * TAB:2 * TAB + 1], min_val=NE, max_val=ITEMS)

        with nc.Block() as block:
            @block.sync
            def _(sp):
                n_items = count_items(sp)
                with sp.Fori(0, n_items) as i:
                    e = sp.value_load(table[0:1, ds(i, 1)], min_val=0, max_val=NE - 1)
                    e_next = sp.value_load(table[0:1, ds(i + 1, 1)], min_val=0, max_val=NE - 1)
                    for m in range(CH):
                        sp.wait_ge(s_lod, i * CH + (m + 1))
                        sp.wait_ge(s_lop, i * CH + (m + 1))
                        load(sp, e if m < RING else e_next, (m + RING) % CH)
                sp.wait_ge(s_raw[2], n_items * 64 + 32)
                sp.wait_ge(s_scat, n_items * 32 + (CSC + 32))
                for q in range(4):
                    sp.dma_start(out[0, q * (T // 4):(q + 1) * (T // 4), :], rows_out[q * (T // 4):(q + 1) * (T // 4), :]).then_inc(s_out, 16)
                sp.wait_ge(s_out, 64)

            @block.gpsimd
            def _(pool):
                pool.memset(yT, 0.0).then_inc(s_init, 1)
                pool.memset(sel_cur[:, 0:2], 0.0).then_inc(s_init, 1)
                pool.iota(trash, [[HS, 2]], base=T, channel_multiplier=1, allow_small_or_imprecise_dtypes=True).then_inc(s_init, 1)
                pool.iota(sel_cur[:, 2:4], [[HS, 2]], base=T, channel_multiplier=1, allow_small_or_imprecise_dtypes=True).then_inc(s_init, 1)
                pool.memset(yrow, 0.0).then_inc(s_init, 1)
                pool.iota(rows_prev, [[HS, 2]], base=T, channel_multiplier=1).then_inc(s_init, 1)
                pool.wait_ge(s_init, 6)
                n_items = count_items(pool)

                def low_part(c, j):
                    r = j % RING
                    pool.wait_ge(s_hi9, c + 1)
                    pool.tensor_tensor(part_lo[r][:, DVE_K:, :], raw[r][:, DVE_K:, :], part_hi[r][:, DVE_K:, :],
                                       ALU.subtract).then_inc(s_lop, 1)

                def gather():
                    for h in range(2):
                        pool.indirect_dma_start(out=xg[:, h, :], out_offset=None, in_=rows_h2[:, :],
                                                in_offset=bass.IndirectOffsetOnAxis(ap=rows_get[:, h:h + 1], axis=0)).then_inc(s_xg, 16)

                def scatter(h):
                    pool.indirect_dma_start(out=rows_out[:, :], out_offset=bass.IndirectOffsetOnAxis(ap=rows_prev[:, h:h + 1], axis=0),
                                            in_=yrow[:, h, :], in_offset=None, compute_op=ALU.add).then_inc(s_scat, 16)

                def carry_wait(c):
                    pool.tensor_tensor(carrier[:, c:c + 1], trash[:, 0:1], trash[:, 0:1], ALU.add)

                scatter(0)
                pool.wait_ge(s_sel1, 1)
                gather()
                low_part(0, 0)
                low_part(1, 1)
                pool.wait_ge(s_scat, 16)
                scatter(1)
                with pool.Fori(0, n_items) as i:
                    pool.wait_ge(s_sel1, i + 2)
                    carry_wait(0)
                    gather()
                    low_part(i * CH + 2, 2)
                    low_part(i * CH + 3, 0)
                    low_part(i * CH + 4, 1)
                    pool.wait_ge(s_yrow, i * 4 + (4 + C1))
                    carry_wait(1)
                    scatter(0)
                    low_part(i * CH + 5, 2)
                    pool.wait_ge(s_scat, i * 32 + (CSC + 16))
                    carry_wait(2)
                    scatter(1)
                    low_part(i * CH + 6, 0)
                    low_part(i * CH + 7, 1)
                pool.wait_ge(s_yrow, n_items * 4 + (4 + C1))
                carry_wait(3)
                scatter(0)
                pool.wait_ge(s_scat, n_items * 32 + (CSC + 16))
                carry_wait(1)
                scatter(1)

            @block.scalar
            def _(act):
                act.preload_act_table(ACT.Sigmoid)
                act.nop().then_inc(s_yrow, C1)
                act.nop().then_inc(s_dnc, CDN)
                n_items = count_items(act)

                def high_part(j, uses):
                    r = j % RING
                    act.wait_ge(s_raw[r], uses)
                    act.activation(part_hi[r], raw[r], ACT.Copy).then_inc(s_hi9, 1)

                def x_high(item, q):
                    act.wait_ge(s_xgT, item * 4 + (2 * q + 1))
                    act.activation(xT_hi[:, 4 * q:4 * q + 4, :], turned(7), ACT.Copy).then_inc(s_xhi, 1)

                def sigmoid(i, j):
                    act.wait_ge(s_clamp, i * 8 + (2 * j + 2 + CGEV))
                    act.activation(sig[j % 2], g_lin[j % 2], ACT.Sigmoid, scale=1.702).then_inc(s_sig, 1)

                def y_rows(i, g):
                    h, q = g // 2, g % 2
                    if g == 0:
                        act.wait_ge(s_shift, i * 2 + 1)
                        act.wait_ge(s_scat, i * 32 + CSC)
                    act.wait_ge(s_yT, i * 4 + (g + 1))
                    act.activation(yrow[:, h, q * 512:q * 512 + 512], bank[Y_BANK[g]][0:HS, :], ACT.Copy,
                                   scale=gate_prev[:, h:h + 1]).then_inc(s_yrow, 1)

                def y_copy(i, q):
                    act.wait_ge(s_dn, i * 4 + (q + 1 + C1))
                    act.activation(yT[:, 2 * q:2 * q + 2, :], bank[4 + q % 2][:, 0:2 * SL].rearrange("p (k t) -> p k t", k=2),
                                   ACT.Copy).then_inc(s_dnc, 1)

                high_part(0, 32)
                high_part(1, 32)
                for q in range(2):
                    x_high(0, q)
                with act.Fori(0, n_items) as i:
                    for j in range(CH):
                        if j == 0:
                            act.wait_ge(s_dn, i * 4 + C1)
                        elif j <= GU:
                            act.wait_ge(s_gu, i * 8 + 2 * j)
                        else:
                            act.wait_ge(s_dn, i * 4 + (2 + C1))
                        high_part(j + 2, i * 64 + 32 * ((j + 2) // RING + 1))
                        for g in {0: (0,), 1: (1, 2), 2: (3,)}.get(j, ()):
                            y_rows(i, g)
                        if j < GU:
                            sigmoid(i, j)
                        if j >= GU:
                            y_copy(i, 2 * j - 8)
                            y_copy(i, 2 * j - 7)
                        if j == 3 or j == 4:
                            x_high(i + 1, j - 3)
                for g in range(4):
                    y_rows(n_items, g)

            @block.vector
            def _(dve):
                dve.nop().then_inc(s_clamp, CGEV)
                n_items = count_items(dve)

                def choose(e, base):
                    at = iota[:, ds(base, SL)].unsqueeze(1).to_broadcast([P, NT, SL])
                    dve.tensor_tensor(pick, at, slot[:, :, ds(e, 1)].to_broadcast([P, NT, SL]), ALU.is_equal)
                    dve.tensor_copy(values[:, :, 3:6].unsqueeze(3), gate3[:, :, :, ds(e, 1)]).then_inc(s_pick, 1)

                def rows(item):
                    dve.wait_ge(s_idx, item + 1)
                    if not isinstance(item, int):
                        dve.wait_ge(s_xg, item * 32)
                    dve.tensor_copy(picked.rearrange("p v h -> p h v"), bank[6][0:HS, 0:12].rearrange("p (h v) -> p h v", h=2)).then_inc(s_pi, 1)
                    dve.wait_ge(s_pi, item + 1)
                    dve.tensor_tensor(row_t, picked[:, 0, :], picked[:, 1, :], ALU.add)
                    dve.scalar_tensor_tensor(out=empty_t, in0=picked[:, 2, :], scalar=1.0, in1=trash, op0=ALU.add, op1=ALU.mult)
                    dve.tensor_tensor(g_t, picked[:, 3, :], picked[:, 4, :], ALU.add)
                    dve.tensor_tensor(rows_get, picked[:, 0, :], picked[:, 1, :], ALU.add).then_inc(s_sel1, 1)
                    dve.wait_ge(s_sel1, item + 1)
                    if not isinstance(item, int):
                        dve.wait_ge(s_shift, item * 2)
                    dve.tensor_tensor(sel_next[:, 0:2], g_t, picked[:, 5, :], ALU.add)
                    dve.tensor_tensor(sel_next[:, 2:4], row_t, empty_t, ALU.add).then_inc(s_sel2, 1)

                def shift(i):
                    dve.wait_ge(s_yrow, i * 4 + C1)
                    dve.wait_ge(s_scat, i * 32 + CSC)
                    dve.wait_ge(s_sel2, i + 1)
                    dve.tensor_copy(gate_prev, sel_cur[:, 0:2])
                    dve.tensor_copy(rows_prev, sel_cur[:, 2:4]).then_inc(s_shift, 1)
                    dve.wait_ge(s_shift, i * 2 + 1)
                    dve.tensor_copy(sel_cur, sel_next).then_inc(s_shift, 1)

                def bias(e):
                    dve.tensor_copy(b_cur[:, 0:KT], b_gu[:, ds(e * (2 * KT), KT)])
                    dve.tensor_scalar(b_cur[:, KT:2 * KT], b_gu[:, ds(e * (2 * KT) + KT, KT)], 1.0, None, ALU.add).then_inc(s_bcur, 1)

                def low_part(c, j):
                    r = j % RING
                    dve.wait_ge(s_hi9, c + 1)
                    dve.tensor_tensor(part_lo[r][:, 0:DVE_K, :], raw[r][:, 0:DVE_K, :], part_hi[r][:, 0:DVE_K, :],
                                      ALU.subtract).then_inc(s_lod, 1)

                def x_low(item, q):
                    dve.wait_ge(s_xgT, item * 4 + (2 * q + 2))
                    dve.tensor_copy(xT_lo[:, 4 * q:4 * q + 4, :], turned(6)).then_inc(s_xlo, 1)

                def activate(i, j):
                    o = j % 2
                    for x in range(2):
                        f = 2 * j + x
                        dve.wait_ge(s_gu, i * 8 + (f + 1))
                        dve.tensor_scalar(g_lin[o][:, x * SL:x * SL + SL], bank[f % 4][:, 0:SL], b_cur[:, f:f + 1], 7.0, ALU.add, ALU.min)
                        dve.tensor_scalar(u_lin[o][:, x * SL:x * SL + SL], bank[f % 4][:, SL:2 * SL], b_cur[:, KT + f:KT + f + 1], 8.0,
                                          ALU.add, ALU.min).then_inc(s_clamp, 1)
                    hi = aT_hi[:, 2 * j:2 * j + 2, :].rearrange("p k t -> p (k t)")
                    lo = aT_lo[:, 2 * j:2 * j + 2, :].rearrange("p k t -> p (k t)")
                    dve.wait_ge(s_sig, i * 4 + (j + 1))
                    dve.tensor_tensor(g_act[o], g_lin[o], sig[o], ALU.mult).then_inc(s_act, 1)
                    dve.wait_ge(s_act, i * 12 + (3 * j + 1))
                    dve.scalar_tensor_tensor(out=act32[o], in0=u_lin[o], scalar=-6.0, in1=g_act[o], op0=ALU.max, op1=ALU.mult)
                    dve.scalar_tensor_tensor(out=hi, in0=u_lin[o], scalar=-6.0, in1=g_act[o], op0=ALU.max, op1=ALU.mult).then_inc(s_act, 1)
                    dve.wait_ge(s_act, i * 12 + (3 * j + 2))
                    dve.tensor_tensor(lo, act32[o], hi, ALU.subtract).then_inc(s_act, 1)

                dve.wait_ge(s_init, 6)
                dve.tensor_copy(ident16, ident[:, :]).then_inc(s_id, 1)
                choose(0, 0)
                bias(0)
                rows(0)
                low_part(0, 0)
                low_part(1, 1)
                for q in range(2):
                    x_low(0, q)
                choose(1, 0)
                with dve.Fori(0, n_items) as i:
                    e_next = dve.value_load(table[0:1, ds(i + 1, 1)], min_val=0, max_val=NE - 1)
                    e_after = dve.value_load(table[0:1, ds(i + 2, 1)], min_val=0, max_val=NE - 1)
                    base_after = dve.value_load(table[0:1, ds(i + (TAB + 2), 1)], min_val=0, max_val=(MAXC - 1) * SL)
                    shift(i)
                    rows(i + 1)
                    for j in range(CH):
                        if j == 0:
                            dve.wait_ge(s_bcur, i + 1)
                        if j == GU - 1:
                            activate(i, j)
                        low_part(i * CH + (j + 2), j + 2)
                        if j < GU - 1:
                            activate(i, j)
                        if j == 3:
                            bias(e_next)
                        if j == 3 or j == 4:
                            x_low(i + 1, j - 3)
                        if j == 4:
                            choose(e_after, base_after)
                shift(n_items)

            @block.tensor
            def _(pe):
                pe.nop().then_inc(s_dn, C1)
                pe.wait_ge(s_init, 6)
                n_items = count_items(pe)

                def find(item):
                    pe.wait_ge(s_pick, item + 1)
                    for h in range(2):
                        for n in range(NT):
                            mm = pe.matmul(bank[6][0:HS, h * 6:h * 6 + 6], pick[:, n, h * HS:h * HS + HS], values[:, n, :],
                                           start=(n == 0), stop=(n == NT - 1))
                    mm.then_inc(s_idx, 1)

                def turn_x(item, q):
                    if q == 0:
                        pe.wait_ge(s_xg, item * 32 + 32)
                    for s in range(2):
                        if q == 1:
                            pe.wait_ge((s_xhi, s_xlo)[s], item * 2 + 1)
                        for k in range(4):
                            for h in range(2):
                                at = s * D + (4 * q + k) * P
                                mm = pe.transpose(turned(7 - s)[:, k, h * HS:h * HS + HS], xg[:, h, at:at + P], ident16[0:HS, 0:HS])
                        mm.then_inc(s_xgT, 1)

                def turn_y(i, g):
                    h, q = g // 2, g % 2
                    if g == 0:
                        pe.wait_ge(s_dnc, i * 4 + CDN)
                    for d in range(4):
                        mm = pe.transpose(bank[Y_BANK[g]][0:HS, d * P:d * P + P], yT[:, 4 * q + d, h * HS:h * HS + HS], ident[:, :])
                    mm.then_inc(s_yT, 1)

                def parts_ready(c):
                    pe.wait_ge(s_lod, c + 1)
                    pe.wait_ge(s_lop, c + 1)

                def product(out_ap, r, col, k, hi, lo, clear=True):
                    wh, wl = part_hi[r][:, k, col * P:col * P + P], part_lo[r][:, k, col * P:col * P + P]
                    for s, (a, b) in enumerate(((wh, hi[:, k, :]), (wh, lo[:, k, :]), (wl, hi[:, k, :]))):
                        mm = pe.matmul(out_ap, a, b, start=(clear and k == 0 and s == 0), stop=(k == KT - 1 and s == 2),
                                       skip_group_check=True)
                    return mm

                def gate_up(i, j):
                    parts_ready(i * CH + j)
                    for x in range(2):
                        f = 2 * j + x
                        pe.wait_ge(s_clamp, i * 8 + (f + 1))
                        for g in range(2):
                            for k in range(KT):
                                if f == 0 and g == 0 and k % 4 == 0:
                                    pe.wait_ge(s_xhi, i * 2 + (k // 4 + 1))
                                    pe.wait_ge(s_xlo, i * 2 + (k // 4 + 1))
                                mm = product(bank[f % 4][:, g * SL:g * SL + SL], j % RING, 2 * g + x, k, xT_hi, xT_lo)
                        mm.then_inc(s_gu, 1)
                        if f == 0:
                            find(i + 1)

                def down(i, j):
                    parts_ready(i * CH + j)
                    for k0, k1 in ((0, KT - 2), (KT - 2, KT)) if j == GU else ((0, KT),):
                        for x in range(2):
                            q = 2 * (j - GU) + x
                            if k0 == 0:
                                pe.wait_ge(s_dnc, i * 4 + (q + 1))
                            for y in range(2):
                                for k in range(k0, k1):
                                    if j == GU and x == 0 and y == 0 and k % 2 == 0:
                                        pe.wait_ge(s_act, i * 12 + 3 * (k // 2 + 1))
                                    mm = product(bank[4 + q % 2][:, y * SL:y * SL + SL], j % RING, 2 * x + y, k, aT_hi, aT_lo, y == 0)
                            if k1 == KT:
                                mm.then_inc(s_dn, 1)

                pe.wait_ge(s_id, 1)
                find(0)
                pe.wait_ge(s_pi, 1)
                for q in range(2):
                    turn_x(0, q)
                with pe.Fori(0, n_items) as i:
                    gate_up(i, 0)
                    for g in range(3):
                        turn_y(i, g)
                    gate_up(i, 1)
                    pe.wait_ge(s_pi, i + 2)
                    turn_y(i, 3)
                    gate_up(i, 2)
                    gate_up(i, 3)
                    pe.wait_ge(s_yrow, i * 4 + (4 + C1))
                    turn_x(i + 1, 0)
                    down(i, 4)
                    turn_x(i + 1, 1)
                    down(i, 5)
                pe.wait_ge(s_xhi, n_items * 2 + 2)
                pe.wait_ge(s_xlo, n_items * 2 + 2)
                for g in range(4):
                    turn_y(n_items, g)

NAMES = ["x", "norm1_g", "w_in", "sb_q_norm_g", "sb_k_norm_g", "sb_out_norm_g", "hg_lb_logits", "hg_out_norm_g",
         "w_out", "norm2_g", "w_router", "b_router", "w_gate_up", "b_gate_up", "w_down", "b_down"]


def kernel(**inputs):
    import numpy as np
    import concourse.bacc as bacc
    from concourse.bass_utils import run_bass_kernel_spmd

    nc = bacc.Bacc("TRN2", target_bir_lowering=False, num_devices=1)
    arrays, args = {}, []
    for name in NAMES:
        a = np.ascontiguousarray(inputs[name])
        arrays[name + "_dram"] = a
        args.append(nc.dram_tensor(name + "_dram", a.shape, mybir.dt.from_np(a.dtype), kind="ExternalInput").ap())
    out = nc.dram_tensor("out_dram", inputs["x"].shape, F32, kind="ExternalOutput").ap()
    build_trunk(nc, *args, out)
    r = run_bass_kernel_spmd(nc, [arrays], core_ids=[0])
    return r.results[0]["out_dram"]
```
